# Optimizing a Trainium2 kernel written in Bass

```python
import functools
import jax, jax.numpy as jnp
from jax import lax
import numpy as np

D_MODEL = 1024
BATCH = 1
SEQ = 512
DEPTH = 1
DEC_BATCH = 8
DEC_SEQ = 1
PAST_LEN = 256
PAGE_SIZE = 128

MIX_W = D_MODEL
GROUP_W = MIX_W // 4
POOL_W = GROUP_W
POOL_WINDOWS = (2, 4, 8, 16)
POOL_GROUP = POOL_W // len(POOL_WINDOWS)
POOL_KEEP = max(POOL_WINDOWS) - 1
RG_W = GROUP_W
RG_HEADS = 4
RG_BLOCK = RG_W // RG_HEADS
RG_CONV = 4
RG_C = 8.0
HEAD_DIM = 64
N_HEADS = GROUP_W // HEAD_DIM
N_KV = 2
GQA = N_HEADS // N_KV
CMP_BLOCK = 32
CMP_STRIDE = 16
SEL_BLOCK = 64
SEL_TOPK = 16
WINDOW = 512
Q_BLOCK = 128
SC_W = GROUP_W
SC_CONV = 3
N_GROUPS = 4
EXP_PER_GROUP = 8
N_EXPERTS = N_GROUPS * EXP_PER_GROUP
TOP_E = 2
D_EXPERT = 512
MOE_BLOCK = 128
EPS = 1e-6
SPLIT_SIZES = (POOL_W, RG_W, RG_W, N_HEADS * HEAD_DIM, 6 * N_KV * HEAD_DIM, 3 * N_HEADS, 3 * SC_W)
N_IN = sum(SPLIT_SIZES)

kernel_name = 'hymba_pool_rglru_nsa_shortconv_hmoe_step'

def rmsnorm(x, g):
    xf = x.astype(jnp.float32)
    y = xf * lax.rsqrt(jnp.mean(xf * xf, axis=-1, keepdims=True) + EPS)
    return (y * g.astype(jnp.float32)).astype(x.dtype)

def split_cols(a, sizes):
    outs, o = [], 0
    for s in sizes:
        outs.append(a[..., o:o + s])
        o += s
    return outs

def causal_dwconv(u, prev, w, b):
    L = u.shape[1]
    ext = jnp.concatenate([prev.astype(u.dtype), u], axis=1)
    y = lax.conv_general_dilated(ext, w[:, None, :].astype(u.dtype), window_strides=(1,), padding='VALID',
                                 dimension_numbers=('NWC', 'WIO', 'NWC'), feature_group_count=u.shape[-1])
    return y + b.astype(u.dtype), ext[:, L:]

def pool_mixer(u, prev, pos0, w, scale):
    B_, L, C = u.shape
    ext = jnp.concatenate([prev.astype(u.dtype), u], axis=1)
    ef = ext.astype(jnp.float32)
    cs = jnp.concatenate([jnp.zeros((B_, 1, C), jnp.float32), jnp.cumsum(ef, axis=1)], axis=1)
    pos = pos0 + jnp.arange(L)
    means = []
    for g, win in enumerate(POOL_WINDOWS):
        sl = slice(g * POOL_GROUP, (g + 1) * POOL_GROUP)
        tot = cs[:, POOL_KEEP + 1:POOL_KEEP + 1 + L, sl] - cs[:, POOL_KEEP + 1 - win:POOL_KEEP + 1 - win + L, sl]
        cnt = jnp.minimum(win, pos + 1).astype(jnp.float32)
        means.append(tot / cnt[None, :, None])
    d = (jnp.concatenate(means, axis=-1) - ef[:, POOL_KEEP:]).astype(u.dtype)
    y = jnp.einsum('blgc,gcd->blgd', d.reshape(B_, L, len(POOL_WINDOWS), POOL_GROUP), w).reshape(B_, L, C)
    return y * scale, ext[:, L:]

def rglru_mixer(xb, gb, conv_prev, h0, conv_w, conv_b, w_a, b_a, w_x, b_x, lam):
    B_, L, C = xb.shape
    xc, conv_new = causal_dwconv(xb, conv_prev, conv_w, conv_b)
    xh = xc.reshape(B_, L, RG_HEADS, RG_BLOCK)
    r = jax.nn.sigmoid(jnp.einsum('blhi,hij->blhj', xh, w_a).reshape(B_, L, C) + b_a)
    ig = jax.nn.sigmoid(jnp.einsum('blhi,hij->blhj', xh, w_x).reshape(B_, L, C) + b_x)
    log_a = -RG_C * r.astype(jnp.float32) * jax.nn.softplus(-lam.astype(jnp.float32))
    a = jnp.exp(log_a)
    bt = jnp.sqrt(-jnp.expm1(2.0 * log_a)) * (ig * xc).astype(jnp.float32)
    bt = bt.at[:, 0].add(a[:, 0] * h0.astype(jnp.float32))
    _, h = lax.associative_scan(lambda e1, e2: (e1[0] * e2[0], e2[0] * e1[1] + e2[1]), (a, bt), axis=1)
    y = h.astype(xb.dtype) * jax.nn.gelu(gb)
    return y, conv_new, h[:, -1].astype(xb.dtype)

def masked_softmax(s, mask):
    s = jnp.where(mask, s.astype(jnp.float32), -jnp.inf)
    m = jnp.max(s, axis=-1, keepdims=True)
    e = jnp.exp(s - jnp.where(jnp.isfinite(m), m, 0.0))
    d = jnp.sum(e, axis=-1, keepdims=True)
    return e / jnp.where(d > 0, d, 1.0)

def nsa_compress(k_raw, v_raw, phi, phi_b, g_kc):
    B_, T = k_raw.shape[:2]
    R = CMP_BLOCK // CMP_STRIDE
    nch = T // CMP_STRIDE
    ncmp = nch - (R - 1)

    def comp(a, w, bias):
        ch = a[:, :nch * CMP_STRIDE].reshape(B_, nch, CMP_STRIDE, N_KV, HEAD_DIM)
        ch = ch.transpose(0, 1, 3, 2, 4).reshape(B_, nch, N_KV, CMP_STRIDE * HEAD_DIM)
        wr = w.reshape(R, CMP_STRIDE * HEAD_DIM, HEAD_DIM)
        out = jnp.einsum('bckf,fd->bckd', ch[:, 0:ncmp], wr[0])
        for r in range(1, R):
            out = out + jnp.einsum('bckf,fd->bckd', ch[:, r:r + ncmp], wr[r])
        return out + bias

    kc = rmsnorm(comp(k_raw, phi[0], phi_b[0]), g_kc)
    vc = comp(v_raw, phi[1], phi_b[1])
    cmp_end = jnp.arange(ncmp) * CMP_STRIDE + (CMP_BLOCK - 1)
    return kc, vc, cmp_end

def sel_blocks(a):
    B_, T = a.shape[:2]
    n_sel = -(-T // SEL_BLOCK)
    a = jnp.pad(a, ((0, 0), (0, n_sel * SEL_BLOCK - T), (0, 0), (0, 0)))
    return a.reshape(B_, n_sel, SEL_BLOCK, N_KV, HEAD_DIM).transpose(0, 3, 1, 2, 4)

def nsa_attend(q, q_pos, gates, kc, vc, cmp_end, ks_blk, vs_blk, kw, vw, w_pos):
    dt = q.dtype
    B_, Q = q.shape[:2]
    t = q_pos[:, None]
    s = jnp.einsum('bqkgd,bckd->bqkgc', q, kc)
    p_cmp = masked_softmax(s, (cmp_end[None, :] <= t)[None, :, None, None, :])
    o_cmp = jnp.einsum('bqkgc,bckd->bqkgd', p_cmp.astype(dt), vc)
    n_sel = ks_blk.shape[2]
    ci = jnp.arange(kc.shape[1])[:, None] * CMP_STRIDE
    sj = jnp.arange(n_sel)[None, :] * SEL_BLOCK
    overlap = ((ci < sj + SEL_BLOCK) & (ci + CMP_BLOCK > sj)).astype(jnp.float32)
    imp = jnp.einsum('bqkgc,cs->bqks', p_cmp, overlap)
    blk = jnp.arange(n_sel)[None, :]
    cur = t // SEL_BLOCK
    valid = blk <= cur
    forced = (blk == 0) | (blk == cur) | (blk == cur - 1)
    score = jnp.where(valid[None, :, None, :], imp, -jnp.inf)
    score = jnp.where((forced & valid)[None, :, None, :], jnp.inf, score)
    top_v, top_i = lax.top_k(score, min(SEL_TOPK, n_sel))
    kk = top_i.shape[-1]
    bi = jnp.arange(B_)[:, None, None, None]
    hi = jnp.arange(N_KV)[None, None, :, None]
    ks = ks_blk[bi, hi, top_i].reshape(B_, Q, N_KV, kk * SEL_BLOCK, HEAD_DIM)
    vs = vs_blk[bi, hi, top_i].reshape(B_, Q, N_KV, kk * SEL_BLOCK, HEAD_DIM)
    spos = (top_i[..., None] * SEL_BLOCK + jnp.arange(SEL_BLOCK)).reshape(B_, Q, N_KV, kk * SEL_BLOCK)
    smask = (spos <= q_pos[None, :, None, None]) & jnp.repeat(top_v > -jnp.inf, SEL_BLOCK, axis=-1)
    s = jnp.einsum('bqkgd,bqknd->bqkgn', q, ks)
    o_sel = jnp.einsum('bqkgn,bqknd->bqkgd', masked_softmax(s, smask[:, :, :, None, :]).astype(dt), vs)
    wd = t - w_pos[None, :]
    wmask = (w_pos[None, :] >= 0) & (wd >= 0) & (wd <= WINDOW)
    s = jnp.einsum('bqkgd,bnkd->bqkgn', q, kw)
    o_win = jnp.einsum('bqkgn,bnkd->bqkgd', masked_softmax(s, wmask[None, :, None, None, :]).astype(dt), vw)
    return gates[..., 0:1] * o_cmp + gates[..., 1:2] * o_sel + gates[..., 2:3] * o_win

def nsa_prompt(q, gates, kc_raw, vc_raw, ksel, vsel, kwin, vwin, phi, phi_b, g_kc):
    B_, S = q.shape[:2]
    kc, vc, cmp_end = nsa_compress(kc_raw, vc_raw, phi, phi_b, g_kc)
    ks_blk, vs_blk = sel_blocks(ksel), sel_blocks(vsel)
    zpad = jnp.zeros((B_, WINDOW, N_KV, HEAD_DIM), kwin.dtype)
    kw_pad = jnp.concatenate([zpad, kwin], axis=1)
    vw_pad = jnp.concatenate([zpad, vwin], axis=1)
    nq = S // Q_BLOCK

    def body(args):
        qc, gc, i = args
        start = i * Q_BLOCK
        kw = lax.dynamic_slice_in_dim(kw_pad, start, WINDOW + Q_BLOCK, axis=1)
        vw = lax.dynamic_slice_in_dim(vw_pad, start, WINDOW + Q_BLOCK, axis=1)
        return nsa_attend(qc, start + jnp.arange(Q_BLOCK), gc, kc, vc, cmp_end, ks_blk, vs_blk,
                          kw, vw, start - WINDOW + jnp.arange(WINDOW + Q_BLOCK))

    qb = q.reshape(B_, nq, Q_BLOCK, N_KV, GQA, HEAD_DIM).swapaxes(0, 1)
    gb = gates.reshape(B_, nq, Q_BLOCK, N_KV, GQA, 3).swapaxes(0, 1)
    o = lax.map(body, (qb, gb, jnp.arange(nq)))
    o = o.swapaxes(0, 1).reshape(B_, S, N_HEADS * HEAD_DIM)
    rows = jnp.stack([kc_raw, vc_raw, ksel, vsel], axis=2)
    win_new = jnp.stack([kwin, vwin], axis=2)[:, S - min(WINDOW, S):]
    return o, rows, win_new

def nsa_sample(pool, page_table, win_buf, q, gates, kc_raw, vc_raw, ksel, vsel, kwin, vwin, phi, phi_b, g_kc):
    B_, L = q.shape[:2]
    past = pool[page_table]
    past = past.reshape(B_, past.shape[1] * past.shape[2], 4, N_KV, HEAD_DIM)
    P = past.shape[1]
    rows = jnp.stack([kc_raw, vc_raw, ksel, vsel], axis=2)
    full = jnp.concatenate([past.astype(rows.dtype), rows], axis=1)
    kc, vc, cmp_end = nsa_compress(full[:, :, 0], full[:, :, 1], phi, phi_b, g_kc)
    ks_blk, vs_blk = sel_blocks(full[:, :, 2]), sel_blocks(full[:, :, 3])
    Lw = win_buf.shape[1]
    new_w = jnp.stack([kwin, vwin], axis=2)
    wfull = jnp.concatenate([win_buf.astype(new_w.dtype), new_w], axis=1)
    o = nsa_attend(q, P + jnp.arange(L), gates, kc, vc, cmp_end, ks_blk, vs_blk,
                   wfull[:, :, 0], wfull[:, :, 1], P - Lw + jnp.arange(Lw + L))
    return o.reshape(B_, L, N_HEADS * HEAD_DIM), rows, wfull[:, L:]

def expert_dispatch(xt, eidx, gate, w_gu, w_down):
    T, D = xt.shape
    M = T * TOP_E
    fe = eidx.reshape(M)
    ftok = jnp.arange(M, dtype=jnp.int32) // TOP_E
    fgate = gate.reshape(M)
    order = jnp.argsort(fe)
    se, stok, sgate = fe[order], ftok[order], fgate[order]
    counts = jnp.bincount(fe, length=N_EXPERTS)
    padded = (counts + MOE_BLOCK - 1) // MOE_BLOCK * MOE_BLOCK
    pad_end = jnp.cumsum(padded)
    pad_start = pad_end - padded
    start = jnp.cumsum(counts) - counts
    dest = pad_start[se] + jnp.arange(M) - start[se]
    n_blk = -(-M // MOE_BLOCK) + N_EXPERTS
    P = n_blk * MOE_BLOCK
    buf_tok = jnp.zeros((P,), jnp.int32).at[dest].set(stok)
    buf_gate = jnp.zeros((P,), fgate.dtype).at[dest].set(sgate)
    blk_exp = jnp.minimum(jnp.searchsorted(pad_end, jnp.arange(n_blk) * MOE_BLOCK, side='right'), N_EXPERTS - 1)
    xb = xt[buf_tok].reshape(n_blk, MOE_BLOCK, D)

    def run(args):
        xi, e = args
        a, b = jnp.split(xi @ w_gu[e], 2, axis=-1)
        return (jax.nn.silu(a) * b) @ w_down[e]

    yb = lax.map(run, (xb, blk_exp)).reshape(P, D)
    return jax.ops.segment_sum(yb * buf_gate[:, None].astype(yb.dtype), buf_tok, num_segments=T)

def moe_ffn(x, wg_r, bg_r, we_r, be_r, w_gu, w_down):
    B_, L, D = x.shape
    xt = x.reshape(B_ * L, D)
    T = xt.shape[0]
    lg = (xt @ wg_r + bg_r).astype(jnp.float32)
    pg = jax.nn.softmax(lg, axis=-1)
    gsel = jnp.argmax(lg, axis=-1)
    p_group = jnp.take_along_axis(pg, gsel[:, None], axis=-1)
    le = (xt @ we_r + be_r).astype(jnp.float32).reshape(T, N_GROUPS, EXP_PER_GROUP)
    le_g = jnp.take_along_axis(le, gsel[:, None, None], axis=1)[:, 0]
    tv, ti = lax.top_k(le_g, TOP_E)
    gate = p_group * jax.nn.softmax(tv, axis=-1)
    eidx = gsel[:, None] * EXP_PER_GROUP + ti
    return expert_dispatch(xt, eidx, gate, w_gu, w_down).reshape(B_, L, D)

def layer_forward(x, pos0, lw, pool_prev, rgc_prev, rgh0, sc_prev, nsa_fn):
    B_, L, _ = x.shape
    h = rmsnorm(x, lw['norm_mix_g'])
    proj = jnp.einsum('bld,dn->bln', h, lw['w_in'])
    pu, rx, rgate, q, kv, ng, sc = split_cols(proj, SPLIT_SIZES)
    y_pool, pool_new = pool_mixer(pu, pool_prev, pos0, lw['pool_w'], lw['pool_scale'])
    y_rg, rgc_new, rgh_new = rglru_mixer(rx, rgate, rgc_prev, rgh0, lw['rg_conv_w'], lw['rg_conv_b'],
                                         lw['rg_w_a'], lw['rg_b_a'], lw['rg_w_x'], lw['rg_b_x'], lw['rg_lambda'])
    qk_g = lw['nsa_qk_g']
    q = rmsnorm(q.reshape(B_, L, N_KV, GQA, HEAD_DIM), qk_g[0]) * (HEAD_DIM ** -0.5)
    kv = kv.reshape(B_, L, 6, N_KV, HEAD_DIM)
    gates = jax.nn.sigmoid(ng.reshape(B_, L, N_KV, GQA, 3))
    y_nsa, nsa_rows, win_new = nsa_fn(q, gates, kv[:, :, 0], kv[:, :, 1], rmsnorm(kv[:, :, 2], qk_g[2]), kv[:, :, 3],
                                      rmsnorm(kv[:, :, 4], qk_g[3]), kv[:, :, 5], lw['nsa_phi'], lw['nsa_phi_b'], qk_g[1])
    z, bg, cg = split_cols(sc, (SC_W, SC_W, SC_W))
    v, sc_new = causal_dwconv(cg * z, sc_prev, lw['sc_conv_w'], lw['sc_conv_b'])
    y_sc = bg * v
    og = lw['mix_out_g'].reshape(4, GROUP_W)
    y = jnp.concatenate([rmsnorm(yi, og[i]) for i, yi in enumerate((y_pool, y_rg, y_nsa, y_sc))], axis=-1)
    x = x + jnp.einsum('blm,md->bld', y, lw['w_out'])
    x = x + moe_ffn(rmsnorm(x, lw['norm_ffn_g']), lw['router_group_w'], lw['router_group_b'],
                    lw['router_expert_w'], lw['router_expert_b'], lw['exp_w_gu'], lw['exp_w_down'])
    return x, (nsa_rows, win_new, pool_new, rgc_new, rgh_new, sc_new)

def setup_inputs(seed: int = 0) -> dict:
    key = jax.random.key(seed)
    keys = jax.random.split(key, 48)
    ctr = iter(range(48))

    def nrm(shape, scale):
        return jax.random.normal(keys[next(ctr)], shape, jnp.float32) * scale

    n_pages = PAST_LEN // PAGE_SIZE
    n_phys = (DEC_BATCH * n_pages * 5 + 3) // 4
    win_keep = min(WINDOW, PAST_LEN)
    u = jax.random.uniform(keys[next(ctr)], (DEPTH, RG_W), jnp.float32, 0.9, 0.999)
    a0 = u ** (1.0 / RG_C)
    page_table = jax.random.permutation(keys[next(ctr)], n_phys)[:DEC_BATCH * n_pages].reshape(DEC_BATCH, n_pages).astype(jnp.int32)
    return {
        'x_prompt': nrm((BATCH, SEQ, D_MODEL), 1.0),
        'x_sample': nrm((DEC_BATCH, DEC_SEQ, D_MODEL), 1.0),
        'cache_nsa': nrm((DEPTH, n_phys, PAGE_SIZE, 4, N_KV, HEAD_DIM), 1.0),
        'state_win_kv': nrm((DEPTH, DEC_BATCH, win_keep, 2, N_KV, HEAD_DIM), 1.0),
        'state_pool': nrm((DEPTH, DEC_BATCH, POOL_KEEP, POOL_W), 1.0),
        'state_rg_conv': nrm((DEPTH, DEC_BATCH, RG_CONV - 1, RG_W), 1.0),
        'state_rg_h': nrm((DEPTH, DEC_BATCH, RG_W), 0.5),
        'state_sc_conv': nrm((DEPTH, DEC_BATCH, SC_CONV - 1, SC_W), 1.0),
        'page_table': page_table,
        'norm_mix_g': 1.0 + nrm((DEPTH, D_MODEL), 0.02),
        'w_in': nrm((DEPTH, D_MODEL, N_IN), D_MODEL ** -0.5),
        'pool_w': nrm((DEPTH, len(POOL_WINDOWS), POOL_GROUP, POOL_GROUP), POOL_GROUP ** -0.5),
        'pool_scale': 1.0 + nrm((DEPTH, POOL_W), 0.02),
        'rg_conv_w': nrm((DEPTH, RG_CONV, RG_W), RG_CONV ** -0.5),
        'rg_conv_b': nrm((DEPTH, RG_W), 0.02),
        'rg_w_a': nrm((DEPTH, RG_HEADS, RG_BLOCK, RG_BLOCK), RG_BLOCK ** -0.5),
        'rg_b_a': nrm((DEPTH, RG_W), 0.02),
        'rg_w_x': nrm((DEPTH, RG_HEADS, RG_BLOCK, RG_BLOCK), RG_BLOCK ** -0.5),
        'rg_b_x': nrm((DEPTH, RG_W), 0.02),
        'rg_lambda': jnp.log(a0) - jnp.log1p(-a0),
        'nsa_phi': nrm((DEPTH, 2, CMP_BLOCK * HEAD_DIM, HEAD_DIM), (CMP_BLOCK * HEAD_DIM) ** -0.5),
        'nsa_phi_b': nrm((DEPTH, 2, HEAD_DIM), 0.02),
        'nsa_qk_g': 1.0 + nrm((DEPTH, 4, HEAD_DIM), 0.02),
        'sc_conv_w': nrm((DEPTH, SC_CONV, SC_W), SC_CONV ** -0.5),
        'sc_conv_b': nrm((DEPTH, SC_W), 0.02),
        'mix_out_g': 1.0 + nrm((DEPTH, MIX_W), 0.02),
        'w_out': nrm((DEPTH, MIX_W, D_MODEL), MIX_W ** -0.5),
        'norm_ffn_g': 1.0 + nrm((DEPTH, D_MODEL), 0.02),
        'router_group_w': nrm((DEPTH, D_MODEL, N_GROUPS), D_MODEL ** -0.5),
        'router_group_b': nrm((DEPTH, N_GROUPS), 0.01),
        'router_expert_w': nrm((DEPTH, D_MODEL, N_EXPERTS), D_MODEL ** -0.5),
        'router_expert_b': nrm((DEPTH, N_EXPERTS), 0.01),
        'exp_w_gu': nrm((DEPTH, N_EXPERTS, D_MODEL, 2 * D_EXPERT), D_MODEL ** -0.5),
        'exp_w_down': nrm((DEPTH, N_EXPERTS, D_EXPERT, D_MODEL), D_EXPERT ** -0.5),
    }

def reference(x_prompt, x_sample, cache_nsa, state_win_kv, state_pool, state_rg_conv, state_rg_h, state_sc_conv,
              page_table, norm_mix_g, w_in, pool_w, pool_scale, rg_conv_w, rg_conv_b, rg_w_a, rg_b_a, rg_w_x, rg_b_x,
              rg_lambda, nsa_phi, nsa_phi_b, nsa_qk_g, sc_conv_w, sc_conv_b, mix_out_g, w_out, norm_ffn_g,
              router_group_w, router_group_b, router_expert_w, router_expert_b, exp_w_gu, exp_w_down):
    past_len = page_table.shape[1] * cache_nsa.shape[2]
    xp, xs = x_prompt, x_sample
    Bp = xp.shape[0]
    st_p, st_s = [], []
    for l in range(DEPTH):
        lw = dict(norm_mix_g=norm_mix_g[l], w_in=w_in[l], pool_w=pool_w[l], pool_scale=pool_scale[l],
                  rg_conv_w=rg_conv_w[l], rg_conv_b=rg_conv_b[l], rg_w_a=rg_w_a[l], rg_b_a=rg_b_a[l],
                  rg_w_x=rg_w_x[l], rg_b_x=rg_b_x[l], rg_lambda=rg_lambda[l], nsa_phi=nsa_phi[l],
                  nsa_phi_b=nsa_phi_b[l], nsa_qk_g=nsa_qk_g[l], sc_conv_w=sc_conv_w[l], sc_conv_b=sc_conv_b[l],
                  mix_out_g=mix_out_g[l], w_out=w_out[l], norm_ffn_g=norm_ffn_g[l],
                  router_group_w=router_group_w[l], router_group_b=router_group_b[l],
                  router_expert_w=router_expert_w[l], router_expert_b=router_expert_b[l],
                  exp_w_gu=exp_w_gu[l], exp_w_down=exp_w_down[l])
        xp, sp = layer_forward(xp, 0, lw,
                               jnp.zeros((Bp, POOL_KEEP, POOL_W), xp.dtype),
                               jnp.zeros((Bp, RG_CONV - 1, RG_W), xp.dtype),
                               jnp.zeros((Bp, RG_W), xp.dtype),
                               jnp.zeros((Bp, SC_CONV - 1, SC_W), xp.dtype),
                               nsa_prompt)
        xs, ss = layer_forward(xs, past_len, lw, state_pool[l], state_rg_conv[l], state_rg_h[l], state_sc_conv[l],
                               functools.partial(nsa_sample, cache_nsa[l], page_table, state_win_kv[l]))
        st_p.append(sp)
        st_s.append(ss)

    def stk(lst, i):
        return jnp.stack([s[i] for s in lst])

    return (xp, xs, stk(st_p, 0), stk(st_s, 0), stk(st_p, 1), stk(st_s, 1), stk(st_p, 2), stk(st_s, 2),
            stk(st_p, 3), stk(st_s, 3), stk(st_p, 4), stk(st_s, 4), stk(st_p, 5), stk(st_s, 5))


_drawn_inputs = setup_inputs


def setup_inputs(seed=0):
    import zlib

    import numpy as np

    out = dict(_drawn_inputs(seed))
    spreads = {}
    factors = {'pool_scale': 4.674,
     'rg_b_a': 8.0,
     'rg_b_x': 8.0,
     'nsa_qk_g': 3.454,
     'sc_conv_b': 4.299,
     'norm_ffn_g': 2.679,
     'router_group_b': 6.612,
     'router_expert_b': 5.971}
    for name, (base, spread) in spreads.items():
        noise = np.random.default_rng([zlib.crc32(name.encode()), seed]).standard_normal(out[name].shape)
        drawn = base * np.exp(spread * noise) if base else spread * noise
        out[name] = __import__('jax').numpy.asarray(drawn.astype(out[name].dtype))
    for name, factor in factors.items():
        out[name] = (out[name] * factor).astype(out[name].dtype)
    return out
```

```python
import concourse.bass as bass
from concourse import mybir
from contextlib import ExitStack

F32 = mybir.dt.float32
BF16 = mybir.dt.bfloat16
I32 = mybir.dt.int32
U32 = mybir.dt.uint32
ALU = mybir.AluOpType
ACT = mybir.ActivationFunctionType
X_AXIS = mybir.AxisListType.X

D = 1024
SEQ = 512
NS = 8
T = SEQ + NS
PAST = 256
PAGE = 128
GW = 256
HD = 64
NTILE = 5
KC = D // 128
POOL_KEEP = 15
RG_KEEP = 3
SC_KEEP = 2
N_CMP_P = SEQ // 16
N_CMP_S = PAST // 16
N_CHUNK = N_CMP_P + NS * N_CMP_S
N_GROUPS = 4
N_EXP = 32
DE = 512
CAP = 64
ROUNDS = -(-T // CAP)
EPS = 1e-6
NEG = -1e30
OFF_U, OFF_X, OFF_R, OFF_Q = 0, 256, 512, 768
OFF_GATE, OFF_Z, OFF_BG, OFF_CG = 1792, 1804, 2060, 2316
W_CHUNKS = [OFF_Q, OFF_Q + 256, OFF_Q + 512, OFF_Q + 768, OFF_U, OFF_X, OFF_R, OFF_Z, OFF_CG, OFF_BG]
W_SLOTS = 4
TILES = [4, 0, 1, 2, 3]
ROWS = [128] * 4 + [NS]
COL = [0, 128, 256, 384, SEQ]

P_POOL_SCALE, P_CONV_W, P_CONV_B, P_BA, P_BX, P_LAM = 0, 2, 10, 12, 14, 16
P_SC_W, P_SC_B, P_OUT_G, P_PHI_B, P_QG, P_KCG, P_ROWS = 18, 24, 26, 34, 36, 37, 38


def psum_jobs():
    jobs, turn = [], [0]

    def take(name, bank=None):
        if bank is None:
            bank = turn[0] % 6
            turn[0] += 1
        jobs.append((name, bank))

    take("params")
    take("xT4")
    for i in range(4):
        take(f"xTa{i}")
        take(f"xTb{i}")
    take("states")
    last = None
    for i in TILES:
        take(f"A{i}")
        take(f"B{i}")
        if last is not None:
            take(f"K{last}")
            if last < 4:
                take(f"R{last}")
        last = i
    take("K3")
    take("R3")
    take("G")
    take("SS", 6)
    take("SW", 7)
    for b in range(NS):
        take(f"sR{b}")
        take(f"sK{b}")
    for n in ("CK0", "CK1", "CV0", "CV1"):
        take(n)
    take("CN")
    take("VT")
    take("cs")
    take("cp0")
    take("cp1")
    take("g32")
    for g in "UX":
        take(f"F{g}s")
        take(f"F{g}0")
        take(f"F{g}1")
    take("PT")
    take("pn")
    take("SO")
    for g in "R":
        take(f"F{g}s")
        take(f"F{g}0")
        take(f"F{g}1")
    take("PBs")
    take("PB0")
    take("PB1")
    for g in "Z":
        take(f"F{g}s")
        take(f"F{g}0")
        take(f"F{g}1")
    take("RGs")
    for n in ("RA0", "RX0", "RA1", "RX1"):
        take(n)
    for g in "CB":
        take(f"F{g}s")
        take(f"F{g}0")
        take(f"F{g}1")
    for i in range(4):
        take(f"O{i}", 6 + i % 2)
        for pair in range(5):
            if pair < 4:
                take(f"S{i}.{2 * pair}")
                take(f"S{i}.{2 * pair + 1}")
            if pair > 0:
                take(f"T{i}.{2 * pair - 2}")
                take(f"T{i}.{2 * pair - 1}")
    take("cT")
    for i in range(4):
        take(f"Oc{i}")
    for g in range(3):
        take(f"N{g}")
    take("Ns")
    take("TLa")
    take("TLb")
    for i in TILES:
        take(f"NT{i}")
    last = None
    take("L", 7)
    for i in TILES:
        take(f"Y{i}.0")
        take(f"Y{i}.1")
        if last is not None:
            take(f"hTa{last}")
            take(f"hTb{last}")
        last = i
    take("hTa3")
    take("hTb3")
    take("pos")
    take("cnt")
    return jobs


def layer_kernel(nc, a, o):
    jobs = psum_jobs()
    bank_of, turn_of, uses = {}, {}, [0] * 8
    for name, bank in jobs:
        bank_of[name], turn_of[name] = bank, uses[bank]
        uses[bank] += 1

    ctx = ExitStack()
    with ctx:
        def sb(name, shape, dt=F32):
            return ctx.enter_context(nc.sbuf_tensor(name, shape, dt))

        def sem(name):
            return ctx.enter_context(nc.semaphore(name))

        class Region:

            def __init__(self, name, floats):
                self.t, self.n, self.at = sb(name, [128, floats]), floats, 0

            def cut(self, floats, pattern=None, **dims):
                assert self.at + floats <= self.n, (self.at, floats, self.n)
                v = self.t[:, self.at:self.at + floats]
                self.at += floats
                return v.rearrange(pattern, **dims) if pattern else v

            def rewind(self, at=0):
                self.at = at

        reg_a = Region("reg_a", 12288)
        reg_b = Region("reg_b", 12288)
        reg_x = Region("reg_x", 5120)
        reg_h = Region("reg_h", 5120)
        reg_y = Region("reg_y", 4352)
        reg_w = Region("reg_w", 8288)
        reg_q = Region("reg_q", 2080)
        small = Region("small", 2240)

        gu_w = [r.t[:, 0:8192].rearrange("p (c n) -> p c n", c=8) for r in (reg_a, reg_b)]
        down_w = [r.t[:, 8192:12288].rearrange("p (s c n) -> p s c n", s=2, c=2) for r in (reg_a, reg_b)]

        x_in = reg_x.cut(5120, "p (t d) -> p t d", t=5)
        xn = reg_h.cut(5120, "p (t d) -> p t d", t=5)
        xnT = reg_b.cut(8 * T, "p (c t) -> p c t", c=8)
        w_slot = [reg_w.cut(2048, "p (c n) -> p c n", c=8) for _ in range(W_SLOTS)]
        w_gate = reg_w.cut(96, "p (c n) -> p c n", c=8)
        reg_h.rewind()
        rows = reg_h.cut(2560, "p (t f) -> p t f", t=5)
        win = reg_h.cut(1280, "p (t f) -> p t f", t=5)
        ynsa = reg_h.cut(1280, "p (t f) -> p t f", t=5)
        qT = reg_q.cut(2 * T, "p (g t) -> p g t", g=2)
        kT = reg_q.cut(2 * T, "p (r t) -> p r t", r=2)
        raw = reg_x.t[:, :].rearrange("p (c t) -> p c t", c=2)
        gain_mix = reg_y.cut(D)
        par_rows = reg_y.cut(128)[0:P_ROWS]
        st_rows = reg_y.cut(GW)[0:48]
        st_pool = reg_y.cut(GW)[0:120]
        qn_buf = [reg_b.t[:, 4160 + 512 * k:4672 + 512 * k] for k in range(2)]
        sq_buf = [reg_b.t[:, 5184 + 512 * k:5696 + 512 * k] for k in range(2)]
        phi = reg_a.cut(4096, "p (c j n) -> p c j n", c=2, j=32)
        page_k = [reg_a.cut(768, "p (g f) -> p g f", g=2) for _ in range(2)]
        win_k = [reg_a.cut(256, "p (g f) -> p g f", g=2) for _ in range(2)]
        vs_cache = reg_a.cut(2048, "p (b g f) -> p b g f", b=NS, g=2)
        vw_cache = reg_a.cut(2048, "p (b g f) -> p b g f", b=NS, g=2)
        smp_kT = [reg_a.cut(514, "p (r t) -> p r t", r=2) for _ in range(2)]
        reg_b.at = 6208
        q_masked = reg_b.cut(NS * 32)
        p_masked = reg_b.cut(4 * NS * 32)
        smp_p = reg_b.cut(2 * 257, "p (r t) -> p r t", r=2)
        smp_pc = reg_b.cut(16)
        smp_pc3 = reg_b.cut(128, "p (b c) -> p b c", b=NS)
        smp_pcT = reg_b.cut(32)
        smp_diag = reg_b.cut(64, "p (r t) -> p r t", r=2)
        smp_new = reg_b.cut(64, "p (r t) -> p r t", r=2)
        smp_o = reg_b.cut(64)
        smp_o2 = reg_b.cut(64)
        kc_a = reg_b.cut(N_CHUNK)
        kcT = reg_b.cut(N_CHUNK)
        kc_sq = reg_b.cut(N_CHUNK)
        vcT = reg_b.cut(N_CHUNK)
        vc_smp = reg_b.cut(128)
        vc_blk = reg_b.cut(256)
        cmp_s = reg_b.cut(512, "p (u c) -> p u c", u=16)
        reg_x.rewind()
        u_ext = reg_x.cut(2 * (POOL_KEEP + SEQ), "p (j t) -> p j t", j=2)
        r_ext = reg_x.cut(2 * (RG_KEEP + SEQ), "p (j t) -> p j t", j=2)
        c_ext = reg_x.cut(2 * (SC_KEEP + SEQ), "p (j t) -> p j t", j=2)
        u_smp = reg_x.cut(16, "p (j t) -> p j t", j=2)
        r_smp = reg_x.cut(16, "p (j t) -> p j t", j=2)
        c_smp = reg_x.cut(16, "p (j t) -> p j t", j=2)
        z_buf = reg_x.cut(2 * T, "p (j t) -> p j t", j=2)
        pool_w = reg_a.t[:, 11904:12160].rearrange("p (j n) -> p j n", j=2)
        m = [reg_a.t[:, 1040 * k:1040 * (k + 1)].rearrange("p (j t) -> p j t", j=2) for k in range(8)]
        g_buf = m[7]
        reg_y.rewind()
        yT = reg_y.cut(8 * T, "p (c t) -> p c t", c=8)
        tails = reg_y.cut(8 * 24, "p (c t) -> p c t", c=8)
        p_buf = [reg_b.t[:, 4160 + 512 * k:4672 + 512 * k] for k in range(4)]
        pT_buf = [reg_a.t[:, 8320 + 512 * k:8832 + 512 * k] for k in range(4)]
        o_tmp = reg_a.t[:, 10368:10880]
        tail_rows = reg_a.t[:, 10880:11904]
        w_out = reg_w.t[:, 0:8192].rearrange("p (c n) -> p c n", c=8)
        x1 = x_in
        h2 = xn
        h2T = reg_q.t[:, 0:1024].rearrange("p (c t) -> p c t", c=8)
        gain_ffn = reg_q.t[:, 1024:2048]
        reg_y.rewind()
        xe = [reg_y.cut(512, "p (c s) -> p c s", c=8) for _ in range(2)]
        hT = [reg_y.cut(256, "p (c s) -> p c s", c=2) for _ in range(2)]
        onehot = [reg_y.cut(320, "p (t s) -> p t s", t=5) for _ in range(2)]
        silu = [reg_y.cut(256) for _ in range(2)]
        hid = [reg_y.cut(256) for _ in range(2)]
        y_out = [reg_w.t[:, 512 * k:512 * (k + 1)] for k in range(2)]
        n_cols = ROUNDS * N_EXP + 2
        posm = reg_w.t[:, 1024:1024 + 5 * n_cols].rearrange("p (t n) -> p t n", t=5)
        rt_at = [1024 + 5 * n_cols]

        def rt(floats, pattern=None, **dims):
            v = reg_w.t[:, rt_at[0]:rt_at[0] + floats]
            rt_at[0] += floats
            assert rt_at[0] <= 8192
            return v.rearrange(pattern, **dims) if pattern else v

        logits = rt(5 * 36, "p (t e) -> p t e", t=5)
        lg8 = rt(40, "p (t e) -> p t e", t=5)
        mx8 = rt(40, "p (t e) -> p t e", t=5)
        tv8 = rt(40, "p (t e) -> p t e", t=5)
        mi8 = rt(40, "p (t e) -> p t e", t=5)
        ti8 = rt(40, "p (t e) -> p t e", t=5)
        gsel = rt(5)
        lex = rt(20, "p (t e) -> p t e", t=5)
        psel = rt(5)
        eqg = rt(160, "p (t e) -> p t e", t=5)
        eqt = rt(160, "p (t e) -> p t e", t=5)
        tif = rt(10, "p (k t) -> p k t", k=2)
        tdx = rt(5)
        gate = rt(10, "p (k t) -> p k t", k=2)
        oh = rt(320, "p (k t e) -> p k t e", k=2, t=5)
        mask = rt(160, "p (t e) -> p t e", t=5)
        pos = rt(160, "p (t e) -> p t e", t=5)
        ohp = rt(320, "p (k t e) -> p k t e", k=2, t=5)
        pk = rt(10, "p (k t) -> p k t", k=2)
        flr = rt(80, "p (k e) -> p k e", k=10)
        flk = rt(10)
        gate_r = rt(10, "p (k t) -> p k t", k=2)
        pass_no = rt(1)
        pass_next = rt(1)
        slot_f = rt(10, "p (k t) -> p k t", k=2)
        cnt = rt(8)
        mask_bf = sb("mask_bf", [128, 5, N_EXP], BF16)

        ident = small.cut(128)
        ones = small.cut(128)
        block_ones = small.cut(128)
        cmp_mask = small.cut(128, "p (t c) -> p t c", t=4)
        cap_iota = small.cut(CAP)
        exp_iota = small.cut(N_EXP)
        grp_iota = small.cut(N_EXP)
        thr = small.cut(8)
        valid = small.cut(5)
        minus_half = small.cut(160)
        params = small.cut(P_ROWS)
        half_b = small.cut(4)
        qg_scaled = small.cut(1)
        sp = small.cut(12, "p (k j) -> p k j", j=2)
        row_of_sample = small.cut(NS)
        sample_of_row = small.cut(32)
        head_of_row = small.cut(4)
        hr3 = small.cut(32, "p (b h) -> p b h", b=NS)
        kv_of_row = small.cut(2)
        inv_cnt = small.cut(32, "p (j t) -> p j t", j=2)
        inv_win = small.cut(2)
        eps_col = small.cut(1)
        rt_w = small.cut(KC * 36, "p (c e) -> p c e", c=KC)
        rt_b = small.cut(36)
        kg = small.cut(128, "p (r d) -> p r d", r=2)
        sumsq = small.cut(8)
        rstd = small.cut(8)
        hss = small.cut(40, "p (t h) -> p t h", t=5)
        hrs = small.cut(40, "p (t h) -> p t h", t=5)
        gates = small.cut(60, "p (t h) -> p t h", t=5)
        g32 = small.cut(12)
        g32m = small.cut(12)
        g3 = small.cut(3)
        smx = small.cut(3)
        ssum = small.cut(3)
        att_mx = small.cut(32)
        att_sum = small.cut(32)
        att_w = small.cut(32)
        cmp_mx = small.cut(16)
        cmp_sum = small.cut(16)
        cmp_w = small.cut(16)
        yss = small.cut(8)
        yrs = small.cut(8)
        n_rounds = sb("n_rounds", [128, 1], I32)
        slot_u = sb("slot_u", [128, 10], U32)
        pages = sb("pages", [1, 2 * NS], I32)
        ident_bf = sb("ident_bf", [128, 128], BF16)
        causal_bf = sb("causal_bf", [128, 128], BF16)
        before_bf = sb("before_bf", [128, 128], BF16)
        ones_bf = sb("ones_bf", [128, 128], BF16)
        rg_w = sb("rg_w", [128, 4, 128])
        states = sb("states", [128, 336])
        st_misc = [states[:, 48 * j:48 * j + 48] for j in range(2)]
        st_poolT = [states[:, 96 + 120 * j:216 + 120 * j].rearrange("p (b k) -> p b k", k=POOL_KEEP) for j in range(2)]
        bank = [ctx.enter_context(nc.psum_tensor(f"bank{i}", [128, 512], F32)) for i in range(8)]
        y_dram = nc.dram_tensor("expert_rows", [N_EXP * CAP, D], F32, kind="Internal").ap()

        bank_full = [sem(f"bank_full{i}") for i in range(8)]
        bank_read = [sem(f"bank_read{i}") for i in range(8)]
        names = """par_loaded gain_loaded gainf_loaded states_loaded blocks_loaded phi_loaded pages_loaded
            kg_loaded wout_loaded rtw_loaded win_loaded
            vcache_loaded consts_made vector_chain scalar_chain pool_chain
            xsq_done rstd_asked rstd_made xn_made xn_read qk_raw hss_made hrs_made qk_normed gates_raw
            rows_stored states_stored params_made sp_exp_asked sp_exp sample_scores q_masked_made
            kc_copied kc_sum kc_ms kc_rstd kc_made smax_made sexp_made sp_scaled pn_diag pc3_made smp_o_made smp_o_moved
            u_copied pool_pad pool_d f_copied conv_made rg_tanh rg_t2 rg_sqrt_asked rg_sqrt h_made sc_z sc_b sc_bread
            att_max att_exp att_pv cmp_max cmp_exp cmp_sums cmp_scaled yn_made yn_ss yn_rs yn_scaled sq_made nrm_sqrt tails_made
            tails_stored x1_ss x1_asked x1_rs h2_made x_reloaded yT_ready routed h2_zeroed kc_squared yn_sq
            rt_d rt_exp rt_exp2_asked rt_exp2 mask_made rounds_made slots_made
            gathered xe_made gu_done silu_done hid_made xt_turned hT_made down_done y_copied
            onehot_made moe_stored round_combined pass_counted half_added y_tile_done y_stored_out gather_begun reload_begun""".split()
        S = {n: sem(n) for n in names}
        x_loaded = [sem(f"x_loaded{i}") for i in range(NTILE)]
        w_loaded = [sem(f"w_loaded{i}") for i in range(W_SLOTS)]
        smp_loaded = [sem(f"smp_loaded{i}") for i in range(2)]
        gu_loaded = [sem(f"gu_loaded{i}") for i in range(2)]
        down_loaded = [sem(f"down_loaded{i}") for i in range(2)]
        y_stored = [sem(f"y_stored{i}") for i in range(2)]
        rows_gathered = [sem(f"rows_gathered{i}") for i in range(NTILE)]

        def claim(eng, job):
            if turn_of[job]:
                eng.wait_ge(bank_read[bank_of[job]], turn_of[job])
            return bank[bank_of[job]]

        def filled(ins, job):
            ins.then_inc(bank_full[bank_of[job]], 1)

        def taken(eng, job):
            eng.wait_ge(bank_full[bank_of[job]], turn_of[job] + 1)
            return bank[bank_of[job]]

        def copied(ins, job):
            ins.then_inc(bank_read[bank_of[job]], 1)

        def drained(eng, job):
            eng.wait_ge(bank_read[bank_of[job]], turn_of[job] + 1)

        def pv_done(eng, n):
            if n % 8 == 7:
                eng.wait_ge(bank_full[bank_of[f"O{n // 8}"]], turn_of[f"O{n // 8}"] + 1)
            else:
                eng.wait_ge(S["att_pv"], 7 * (n // 8) + n % 8 + 1)

        def chain_of(eng, s):
            count = [0]

            def link(ins):
                count[0] += 1
                ins.then_inc(S[s], 1)
                eng.wait_ge(S[s], count[0])
            return link

        cache = a["cache_nsa"].rearrange("l n p c k d -> (l n p) (c k d)")
        win_state = a["state_win_kv"].rearrange("l b t c k d -> (l b) t (c k d)")
        w_in = a["w_in"].rearrange("l (c p) n -> p (l c) n", p=128)
        gu_dram = a["exp_w_gu"].rearrange("l e (p c) n -> (l e p) c n", c=8)
        down_dram = a["exp_w_down"].rearrange("l e (s p c) n -> (l e) p s c n", s=2, c=2)
        x_dram = a["x_prompt"].rearrange("b (t p) d -> p (b t) d", p=128)
        xs_dram = a["x_sample"].rearrange("b t d -> (b t) d")
        PAR_DMAS = 13

        block = ctx.enter_context(nc.Block())

        @block.sync
        def _(sp_eng):
            eng = sp_eng
            eng.dma_start(x_in[0:NS, 4, :], xs_dram).then_inc(x_loaded[4], 16)
            eng.dma_start(gain_mix, a["norm_mix_g"].rearrange("l d -> (l d)").partition_broadcast(128)).then_inc(S["gain_loaded"], 16)
            for i in range(4):
                eng.dma_start(x_in[:, i, :], x_dram[:, i, :]).then_inc(x_loaded[i], 16)
            for n, off in enumerate(W_CHUNKS[:W_SLOTS]):
                eng.dma_start(w_slot[n], w_in[:, :, off:off + 256]).then_inc(w_loaded[n], 16)
            eng.dma_start(w_gate, w_in[:, :, OFF_GATE:OFF_GATE + 12]).then_inc(w_loaded[3], 16)
            eng.dma_start(kg[:, :, :], a["nsa_qk_g"].rearrange("l r d -> (l r) d")[2:4].partition_broadcast(128)).then_inc(S["kg_loaded"], 16)
            eng.dma_start(pages[:, :], a["page_table"].rearrange("b n -> (b n)").unsqueeze(0)).then_inc(S["pages_loaded"], 16)
            for c in range(2):
                for kv in range(2):
                    eng.dma_start(phi[64 * kv:64 * kv + 64, c], a["nsa_phi"].rearrange("l c (j d) n -> d (l c) j n", d=HD)[:, c]).then_inc(S["phi_loaded"], 16)
            eng.wait_ge(S["pages_loaded"], 16)
            for b in range(NS):
                if b >= 2:
                    eng.wait_ge(bank_full[bank_of[f"sK{b - 2}"]], turn_of[f"sK{b - 2}"] + 1)
                for g in range(2):
                    page = eng.value_load(pages[0:1, 2 * b + g:2 * b + g + 1], min_val=0, max_val=cache.shape[0] // PAGE - 1)
                    rows_of_page = cache[bass.ds(page * PAGE, PAGE)]
                    eng.dma_start(page_k[b % 2][:, g, :], rows_of_page[:, 0:384]).then_inc(smp_loaded[b % 2], 16)
                    eng.dma_start(vs_cache[:, b, g, :], rows_of_page[:, 384:512]).then_inc(S["vcache_loaded"], 16)
                eng.dma_start(win_k[b % 2][:, :, :], win_state[b].rearrange("(g p) f -> p g f", p=128)[:, :, 0:128]).then_inc(smp_loaded[b % 2], 16)
            eng.dma_start(vw_cache[:, :, 0, :], win_state[:, 0:128, 128:256].rearrange("b p f -> p b f")).then_inc(S["vcache_loaded"], 16)
            eng.dma_start(vw_cache[:, :, 1, :], win_state[:, 128:256, 128:256].rearrange("b p f -> p b f")).then_inc(S["vcache_loaded"], 16)
            readers = ["A3", "A3", "B3", "B3", "FU1", "FX1"]
            for n in range(W_SLOTS, len(W_CHUNKS)):
                reader = readers[n - W_SLOTS]
                eng.wait_ge(bank_full[bank_of[reader]], turn_of[reader] + 1)
                off = W_CHUNKS[n]
                eng.dma_start(w_slot[n % W_SLOTS], w_in[:, :, off:off + 256]).then_inc(w_loaded[n % W_SLOTS], 16)
            eng.dma_start(rt_w[:, :, 0:4], a["router_group_w"].rearrange("l (c p) n -> p (l c) n", p=128)).then_inc(S["rtw_loaded"], 16)
            eng.dma_start(rt_w[:, :, 4:36], a["router_expert_w"].rearrange("l (c p) n -> p (l c) n", p=128)).then_inc(S["rtw_loaded"], 16)
            eng.dma_start(rt_b[:, 0:4], a["router_group_b"].rearrange("l d -> (l d)").partition_broadcast(128)).then_inc(S["rtw_loaded"], 16)
            eng.dma_start(rt_b[:, 4:36], a["router_expert_b"].rearrange("l d -> (l d)").partition_broadcast(128)).then_inc(S["rtw_loaded"], 16)
            eng.wait_ge(S["smp_o_made"], 1)
            eng.dma_start(ynsa[0:NS, 4, :], smp_o2[0:32, :]).then_inc(S["smp_o_moved"], 16)
            eng.wait_ge(S["qk_normed"], NTILE)
            eng.dma_start(o["rows_p"].rearrange("l b (t p) c k d -> p (l b t) (c k d)", p=128), rows[:, 0:4, :]).then_inc(S["rows_stored"], 16)
            eng.dma_start(o["rows_s"].rearrange("l b t c k d -> (l b t) (c k d)"), rows[0:NS, 4, :]).then_inc(S["rows_stored"], 16)
            eng.dma_start(o["win_p"].rearrange("l b (t p) c k d -> p (l b t) (c k d)", p=128), win[:, 0:4, :]).then_inc(S["rows_stored"], 16)
            eng.dma_start(o["win_s"].rearrange("l b t c k d -> (l b) t (c k d)")[:, PAST - 1, :], win[0:NS, 4, :]).then_inc(S["rows_stored"], 16)
            eng.wait_ge(bank_full[bank_of["FB1"]], turn_of["FB1"] + 1)
            eng.dma_start(w_out, a["w_out"].rearrange("l (c p) n -> p (l c) n", p=128)).then_inc(S["wout_loaded"], 16)
            eng.wait_ge(S["sc_b"], 1)
            eng.wait_ge(S["tails_made"], 1)
            eng.dma_start(x1[0:NS, 4, :], xs_dram).then_inc(S["x_reloaded"], 16)
            eng.dma_start(x1[:, 0:4, :], x_dram).then_inc(S["x_reloaded"], 16)

            def load_expert(e, b, free=None):
                if free is not None:
                    eng.wait_ge(S["gu_done"], free)
                eng.dma_start(gu_w[b], gu_dram[bass.ds(e * 128, 128)]).then_inc(gu_loaded[b], 16)
                if free is not None:
                    eng.wait_ge(S["down_done"], free)
                eng.dma_start(down_w[b], down_dram[bass.ds(e, 1)].rearrange("e p s c n -> (e p) s c n")).then_inc(down_loaded[b], 16)

            drained(eng, "Oc3")
            eng.wait_ge(S["tails_stored"], 16 * 8)
            eng.wait_ge(S["yT_ready"], 1)
            eng.dma_start(gain_ffn, a["norm_ffn_g"].rearrange("l d -> (l d)").partition_broadcast(128)).then_inc(S["gainf_loaded"], 16)
            load_expert(0, 0)
            load_expert(1, 1)
            with eng.Fori(1, N_EXP // 2) as i:
                for b in range(2):
                    load_expert(2 * i + b, b, 2 * i - 1 + b)
            eng.wait_ge(S["rounds_made"], 1)
            rounds = eng.value_load(n_rounds[0:1, 0:1], min_val=1, max_val=ROUNDS)
            with eng.If(rounds > 1):
                with eng.Fori(1, rounds) as r:
                    eng.wait_ge(S["round_combined"], r + 1)
                    eng.sem_inc(S["reload_begun"], 1)
                    with eng.Fori(0, N_EXP // 2) as i:
                        for b in range(2):
                            load_expert(2 * i + b, b, N_EXP * r + 2 * i - 1 + b)
            for n in range(NTILE):
                i = TILES[n]
                eng.wait_ge(S["y_tile_done"], rounds * NTILE + n + 1)
                if i == 4:
                    eng.dma_start(o["y_s"].rearrange("b t d -> (b t) d"), x1[0:NS, 4, :]).then_inc(S["y_stored_out"], 16)
                else:
                    eng.dma_start(o["y_p"].rearrange("b (t p) d -> p (b t) d", p=128)[:, i, :], x1[:, i, :]).then_inc(S["y_stored_out"], 16)
            eng.wait_ge(S["y_stored_out"], 16 * NTILE)
            eng.wait_ge(S["rows_stored"], 16 * 4)
            eng.wait_ge(S["states_stored"], 16 * 4)
            eng.wait_ge(S["tails_stored"], 16 * 8)

        @block.gpsimd
        def _(eng):
            link = chain_of(eng, "pool_chain")
            eng.memset(ident, 0.0)
            eng.memset(ones, 1.0)
            eng.memset(ones_bf[:, :], 1.0)
            eng.memset(ident_bf[:, :], 0.0)
            eng.memset(causal_bf[:, :], 0.0)
            eng.memset(before_bf[:, :], 1.0)
            eng.memset(minus_half, -0.5)
            eng.memset(eps_col, EPS)
            link(eng.memset(pool_w[:, :, :], 0.0))
            for t in (ident, ident_bf[:, :]):
                eng.affine_select(out=t, in_=t, compare_op=ALU.not_equal, fill=1.0, base=0, pattern=[[-1, 128]], channel_multiplier=1)
            link(eng.memset(rg_w[:, :, :], 0.0))
            for k in range(4):
                lo, j = 64 * (k % 2), k // 2
                eng.dma_start(pool_w[lo:lo + 64, j, lo:lo + 64], a["pool_w"][0, k]).then_inc(S["blocks_loaded"], 16)
                eng.dma_start(rg_w[lo:lo + 64, j, lo:lo + 64], a["rg_w_a"][0, k]).then_inc(S["blocks_loaded"], 16)
                eng.dma_start(rg_w[lo:lo + 64, 2 + j, lo:lo + 64], a["rg_w_x"][0, k]).then_inc(S["blocks_loaded"], 16)
            eng.affine_select(out=causal_bf[:, :], in_=causal_bf[:, :], compare_op=ALU.is_ge, fill=NEG, base=0, pattern=[[-1, 128]], channel_multiplier=1)
            eng.affine_select(out=before_bf[:, :], in_=before_bf[:, :], compare_op=ALU.is_gt, fill=0.0, base=0, pattern=[[1, 128]], channel_multiplier=-1)
            link(eng.memset(block_ones, 1.0))
            eng.affine_select(out=block_ones[:, 0:64], in_=block_ones[:, 0:64], compare_op=ALU.is_ge, fill=0.0, base=63, pattern=[[0, 64]], channel_multiplier=-1)
            eng.affine_select(out=block_ones[:, 64:128], in_=block_ones[:, 64:128], compare_op=ALU.is_ge, fill=0.0, base=-64, pattern=[[0, 64]], channel_multiplier=1)
            eng.memset(cmp_mask, 0.0)
            eng.memset(valid, 1.0)
            eng.memset(row_of_sample[0:32, :], 1.0)
            eng.memset(sample_of_row[0:8, :], 1.0)
            eng.memset(q_masked, 0.0)
            eng.memset(p_masked, 0.0)
            eng.memset(vc_blk, 0.0)
            eng.memset(hr3[0:32], 0.0)
            eng.iota(cap_iota, pattern=[[1, CAP]], base=0, channel_multiplier=0, allow_small_or_imprecise_dtypes=True)
            eng.iota(exp_iota, pattern=[[1, N_EXP]], base=0, channel_multiplier=0, allow_small_or_imprecise_dtypes=True)
            eng.iota(grp_iota, pattern=[[1, N_GROUPS], [0, N_EXP // N_GROUPS]], base=0, channel_multiplier=0, allow_small_or_imprecise_dtypes=True)
            eng.iota(thr, pattern=[[CAP, 8]], base=CAP, channel_multiplier=0, allow_small_or_imprecise_dtypes=True)
            link(eng.iota(inv_cnt, pattern=[[0, 2], [1, 16]], base=1, channel_multiplier=0, allow_small_or_imprecise_dtypes=True))
            eng.affine_select(out=cmp_mask, in_=cmp_mask, compare_op=ALU.is_ge, fill=NEG, base=-31, pattern=[[128, 4], [-16, 32]], channel_multiplier=1)
            eng.affine_select(out=valid, in_=valid, compare_op=ALU.is_ge, fill=0.0, base=SEQ + NS - 1, pattern=[[-128, 5]], channel_multiplier=-1)
            link(eng.affine_select(out=hr3[0:32], in_=hr3[0:32], compare_op=ALU.not_equal, fill=1.0, base=0, pattern=[[-4, NS], [-1, 4]], channel_multiplier=1))
            link(eng.affine_select(out=row_of_sample[0:32, :], in_=row_of_sample[0:32, :], compare_op=ALU.is_ge, fill=0.0, base=0, pattern=[[-4, NS]], channel_multiplier=1))
            link(eng.affine_select(out=row_of_sample[0:32, :], in_=row_of_sample[0:32, :], compare_op=ALU.is_ge, fill=0.0, base=3, pattern=[[4, NS]], channel_multiplier=-1))
            link(eng.affine_select(out=sample_of_row[0:8, :], in_=sample_of_row[0:8, :], compare_op=ALU.is_ge, fill=0.0, base=0, pattern=[[1, 32]], channel_multiplier=-4))
            link(eng.affine_select(out=sample_of_row[0:8, :], in_=sample_of_row[0:8, :], compare_op=ALU.is_ge, fill=0.0, base=3, pattern=[[-1, 32]], channel_multiplier=4))
            eng.sem_inc(S["consts_made"], 1)

            def power(out, in_, s_ask, asked, s_done):
                eng.wait_ge(S[s_ask], asked)
                eng.tensor_tensor(out, in_, minus_half[0:out.shape[0], 0:out.shape[-1]], ALU.pow).then_inc(S[s_done], 1)

            for n, i in enumerate(TILES):
                power(rstd[0:ROWS[i], i:i + 1], sumsq[0:ROWS[i], i:i + 1], "rstd_asked", n + 1, "rstd_made")
            for n, i in enumerate(TILES):
                power(hrs[0:ROWS[i], i, :], hss[0:ROWS[i], i, :], "hss_made", n + 1, "hrs_made")
            power(kc_sq, kc_a, "kc_ms", 1, "kc_rstd")
            eng.wait_ge(S["u_copied"], 2)
            eng.wait_ge(S["smp_o_made"], 1)
            E = POOL_KEEP + SEQ
            s2, s4, s8, d = m[0], m[1], m[2], m[3]
            link(eng.tensor_tensor(s2[:, 0, 0:SEQ], u_ext[:, 0, 15:E], u_ext[:, 0, 14:E - 1], ALU.add))
            link(eng.tensor_copy(s4[64:128, 0, 0:SEQ], s2[64:128, 0, 0:SEQ]))
            link(eng.tensor_tensor(s4[64:128, 0, 2:SEQ], s2[64:128, 0, 2:SEQ], s2[64:128, 0, 0:SEQ - 2], ALU.add))
            link(eng.tensor_tensor(s2[:, 1, 0:SEQ], u_ext[:, 1, 15:E], u_ext[:, 1, 14:E - 1], ALU.add))
            link(eng.tensor_copy(s4[:, 1, 0:2], s2[:, 1, 0:2]))
            link(eng.tensor_tensor(s4[:, 1, 2:SEQ], s2[:, 1, 2:SEQ], s2[:, 1, 0:SEQ - 2], ALU.add))
            link(eng.tensor_copy(s8[:, 1, 0:4], s4[:, 1, 0:4]))
            link(eng.tensor_tensor(s8[:, 1, 4:SEQ], s4[:, 1, 4:SEQ], s4[:, 1, 0:SEQ - 4], ALU.add))
            link(eng.tensor_copy(d[64:128, 1, 0:8], s8[64:128, 1, 0:8]))
            link(eng.tensor_tensor(d[64:128, 1, 8:SEQ], s8[64:128, 1, 8:SEQ], s8[64:128, 1, 0:SEQ - 8], ALU.add))
            sums = [(0, 0, s2), (64, 0, s4), (0, 1, s8), (64, 1, d)]
            for lo, j, s in sums:
                hi = lo + 64
                link(eng.tensor_tensor(m[2][lo:hi, 0, 16 * j:16 * j + 16], s[lo:hi, j, 0:16], inv_cnt[lo:hi, j, :], ALU.mult))
                link(eng.tensor_scalar(d[lo:hi, j, 16:SEQ], s[lo:hi, j, 16:SEQ], inv_win[lo:hi, j:j + 1], None, ALU.mult))
                link(eng.tensor_copy(d[lo:hi, j, 0:16], m[2][lo:hi, 0, 16 * j:16 * j + 16]))
            eng.wait_ge(S["pool_pad"], 1)
            link(eng.tensor_tensor(d[:, :, 0:SEQ], d[:, :, 0:SEQ], u_ext[:, :, 15:E], ALU.subtract))
            eng.tensor_tensor(d[:, :, SEQ:T], d[:, :, SEQ:T], u_smp[:, :, :], ALU.subtract).then_inc(S["pool_d"], 1)
            eng.tensor_copy(tails[:, 0:2, 0:16], u_ext[:, :, E - 16:E])
            eng.tensor_copy(tails[:, 0:2, 16:24], u_smp[:, :, :])
            eng.wait_ge(S["f_copied"], 1)
            eng.tensor_copy(tails[:, 2:4, 0:16], r_ext[:, :, RG_KEEP + SEQ - 16:RG_KEEP + SEQ])
            eng.tensor_copy(tails[:, 2:4, 16:24], r_smp[:, :, :])
            eng.wait_ge(S["sc_z"], 1)
            eng.tensor_copy(tails[:, 4:6, 0:16], c_ext[:, :, SC_KEEP + SEQ - 16:SC_KEEP + SEQ])
            eng.tensor_copy(tails[:, 4:6, 16:24], c_smp[:, :, :])
            eng.wait_ge(S["h_made"], 1)
            eng.tensor_copy(tails[:, 6:8, :], m[3][:, :, T - 24:T]).then_inc(S["tails_made"], 1)
            power(yrs[:, 0:4], yss[:, 0:4], "yn_ss", 1, "yn_rs")
            power(yrs[0:NS, 4:5], yss[0:NS, 4:5], "yn_ss", 1, "yn_rs")
            for n, i in enumerate(TILES):
                power(rstd[0:ROWS[i], i:i + 1], sumsq[0:ROWS[i], i:i + 1], "x1_asked", n + 1, "x1_rs")
            eng.wait_ge(S["slots_made"], 1)
            rounds = eng.value_load(n_rounds[0:1, 0:1], min_val=1, max_val=ROUNDS)
            with eng.Fori(0, rounds) as r:
                eng.wait_ge(S["moe_stored"], r + 1)
                eng.sem_inc(S["gather_begun"], 1)
                for i in TILES:
                    for k in range(2):
                        dst = reg_a.t[0:ROWS[i], (2 * i + k) * D:(2 * i + k + 1) * D]
                        eng.indirect_dma_start(dst, None, y_dram[:, :], bass.IndirectOffsetOnAxis(ap=slot_u[0:ROWS[i], 5 * k + i:5 * k + i + 1], axis=0)).then_inc(rows_gathered[i], 16)

        @block.scalar
        def _(eng):
            link = chain_of(eng, "scalar_chain")

            def copy(out, in_):
                return eng.activation(out, in_, ACT.Copy)

            eng.dma_start(par_rows[P_POOL_SCALE:P_POOL_SCALE + 2, :], a["pool_scale"].rearrange("l (j p) -> (l j) p", p=128)).then_inc(S["par_loaded"], 16)
            eng.dma_start(par_rows[P_CONV_W:P_CONV_W + 8, :], a["rg_conv_w"].rearrange("l k (j p) -> (l k j) p", p=128)).then_inc(S["par_loaded"], 16)
            for name, at in (("rg_conv_b", P_CONV_B), ("rg_b_a", P_BA), ("rg_b_x", P_BX), ("rg_lambda", P_LAM), ("sc_conv_b", P_SC_B)):
                eng.dma_start(par_rows[at:at + 2, :], a[name].rearrange("l (j p) -> (l j) p", p=128)).then_inc(S["par_loaded"], 16)
            eng.dma_start(par_rows[P_SC_W:P_SC_W + 6, :], a["sc_conv_w"].rearrange("l k (j p) -> (l k j) p", p=128)).then_inc(S["par_loaded"], 16)
            eng.dma_start(par_rows[P_OUT_G:P_OUT_G + 8, :], a["mix_out_g"].rearrange("l (j p) -> (l j) p", p=128)).then_inc(S["par_loaded"], 16)
            for half in range(2):
                lo = 64 * half
                eng.dma_start(par_rows[P_PHI_B:P_PHI_B + 2, lo:lo + 64], a["nsa_phi_b"].rearrange("l c d -> (l c) d")).then_inc(S["par_loaded"], 16)
                eng.dma_start(par_rows[P_QG:P_QG + 2, lo:lo + 64], a["nsa_qk_g"].rearrange("l c d -> (l c) d")[0:2]).then_inc(S["par_loaded"], 16)
            eng.dma_start(st_rows[0:24, :], a["state_rg_conv"].rearrange("l b k c -> (l b k) c")).then_inc(S["states_loaded"], 16)
            eng.dma_start(st_rows[24:40, :], a["state_sc_conv"].rearrange("l b k c -> (l b k) c")).then_inc(S["states_loaded"], 16)
            eng.dma_start(st_rows[40:48, :], a["state_rg_h"].rearrange("l b c -> (l b) c")).then_inc(S["states_loaded"], 16)
            eng.dma_start(st_pool[:, :], a["state_pool"].rearrange("l b k c -> (l b k) c")).then_inc(S["states_loaded"], 16)
            eng.dma_start(o["pool_s"].rearrange("l b k c -> (l b) k c")[:, 0:POOL_KEEP - 1, :], a["state_pool"].rearrange("l b k c -> (l b) k c")[:, 1:POOL_KEEP, :]).then_inc(S["states_stored"], 16)
            eng.dma_start(o["rgc_s"].rearrange("l b k c -> (l b) k c")[:, 0:RG_KEEP - 1, :], a["state_rg_conv"].rearrange("l b k c -> (l b) k c")[:, 1:RG_KEEP, :]).then_inc(S["states_stored"], 16)
            eng.dma_start(o["scc_s"].rearrange("l b k c -> (l b) k c")[:, 0:SC_KEEP - 1, :], a["state_sc_conv"].rearrange("l b k c -> (l b) k c")[:, 1:SC_KEEP, :]).then_inc(S["states_stored"], 16)
            eng.dma_start(o["win_s"].rearrange("l b t c k d -> (l b) t (c k d)")[:, 0:PAST - 1, :], win_state[:, 1:PAST, :]).then_inc(S["states_stored"], 16)

            for i in TILES:
                eng.wait_ge(x_loaded[i], 16)
                eng.activation(xn[0:ROWS[i], i, :], x_in[0:ROWS[i], i, :], ACT.Square, accum_out=sumsq[0:ROWS[i], i:i + 1]).then_inc(S["xsq_done"], 1)
            eng.wait_ge(S["sp_exp_asked"], 1)
            eng.activation(sp[:, 1, :], sp[:, 0, :], ACT.Exp, scale=-1.0).then_inc(S["sp_exp"], 1)
            ps = taken(eng, "xT4")
            copied(copy(xnT[:, :, SEQ:T], ps[:, 0:64].rearrange("p (c t) -> p c t", c=8)), "xT4")
            for i in range(4):
                ps = taken(eng, f"xTa{i}")
                copied(copy(xnT[:, 0:4, COL[i]:COL[i] + 128], ps[:, :].rearrange("p (c t) -> p c t", c=4)), f"xTa{i}")
            ps = taken(eng, "states")
            copied(copy(states[:, :], ps[:, 0:336]), "states")

            def kv_rows(n, i):
                r = ROWS[i]
                if n == 0:
                    eng.wait_ge(bank_full[bank_of["xTb3"]], turn_of["xTb3"] + 1)
                if n >= 2:
                    eng.wait_ge(bank_full[bank_of[f"K{TILES[n - 2]}"]], turn_of[f"K{TILES[n - 2]}"] + 1)
                ps = taken(eng, f"A{i}")
                copy(qn_buf[n % 2][0:r, 0:256], ps[0:r, 0:256])
                copied(copy(rows[0:r, i, 0:256], ps[0:r, 256:512]), f"A{i}")
                ps = taken(eng, f"B{i}")
                copy(rows[0:r, i, 256:512], ps[0:r, 0:256])
                copied(copy(win[0:r, i, :], ps[0:r, 256:512]), f"B{i}")

            def feature_qk(i):
                r, c = ROWS[i], COL[i]
                ps = taken(eng, f"K{i}")
                if i == 4:
                    eng.wait_ge(S["params_made"], 1)
                v = ps[:, 0:4 * r].rearrange("p (g t) -> p g t", g=4)
                eng.activation(qT[:, :, c:c + r], v[:, 0:2, :], ACT.Copy, scale=qg_scaled)
                copied(copy(kT[:, :, c:c + r], v[:, 2:4, :]), f"K{i}")
                if i < 4:
                    ps = taken(eng, f"R{i}")
                    copied(copy(raw[:, :, c:c + r], ps[:, 0:256].rearrange("p (g t) -> p g t", g=2)), f"R{i}")

            for n, i in enumerate(TILES):
                kv_rows(n, i)
                if n:
                    feature_qk(TILES[n - 1])
            feature_qk(3)
            ps = taken(eng, "G")
            eng.activation(gates[:, 0:4, :], ps[:, 0:48].rearrange("p (t h) -> p t h", t=4), ACT.Tanh, scale=0.5)
            copied(eng.activation(gates[0:NS, 4, :], ps[0:NS, 48:60], ACT.Tanh, scale=0.5), "G")

            for b in range(NS):
                ps = taken(eng, f"sR{b}")
                copied(copy(raw[:, :, SEQ + PAST * b:SEQ + PAST * (b + 1)], ps[:, :].rearrange("p (c t) -> p c t", c=2)), f"sR{b}")
                if b >= 2:
                    eng.wait_ge(S["sample_scores"], b - 1)
                copy(smp_kT[b % 2][:, :, 256:257], kT[:, :, SEQ + b:SEQ + b + 1])
                ps = taken(eng, f"sK{b}")
                copied(copy(smp_kT[b % 2][:, :, 0:256], ps[:, :].rearrange("p (r t) -> p r t", r=2)), f"sK{b}")
            for comp, (name, out) in enumerate((("CK", kc_a), ("CV", vcT))):
                for kv in range(2):
                    lo = 64 * kv
                    ps = taken(eng, f"{name}{kv}")
                    eng.activation(out[lo:lo + 64], ps[lo:lo + 64, 0:N_CHUNK], ACT.Identity, bias=params[lo:lo + 64, P_PHI_B + comp:P_PHI_B + comp + 1]).then_inc(S["kc_copied"], 1)
            eng.wait_ge(S["kc_sum"], 1)
            eng.activation(kc_sq, kcT, ACT.Square).then_inc(S["kc_squared"], 1)
            for r in range(3):
                eng.wait_ge(S["smax_made"], r + 1)
                if r < 2:
                    ps = taken(eng, "SSSW"[2 * r:2 * r + 2])
                    copied(eng.activation(smp_p[0:32, r, :], ps[0:32, 0:257], ACT.Exp, bias=smx[0:32, r:r + 1], accum_out=ssum[0:32, r:r + 1]), "SSSW"[2 * r:2 * r + 2])
                else:
                    ps = taken(eng, "cs")
                    copied(eng.activation(smp_pc[0:32, 0:15], ps[0:32, 0:15], ACT.Exp, bias=smx[0:32, 2:3], accum_out=ssum[0:32, 2:3]), "cs")
            eng.wait_ge(S["cmp_max"], 1)
            eng.activation(cmp_s, cmp_s, ACT.Exp).then_inc(S["cmp_exp"], 1)

            def features(g, out_p, out_s, pad, func=ACT.Copy):
                ps = taken(eng, f"F{g}0")
                copied(eng.activation(out_p[:, 0, pad:pad + SEQ], ps[:, :], func), f"F{g}0")
                ps = taken(eng, f"F{g}1")
                copied(eng.activation(out_p[:, 1, pad:pad + SEQ], ps[:, :], func), f"F{g}1")
                ps = taken(eng, f"F{g}s")
                copied(eng.activation(out_s, ps[:, 0:16].rearrange("p (j t) -> p j t", j=2), func), f"F{g}s")

            features("U", u_ext, u_smp[:, :, :], POOL_KEEP)
            drained(eng, "FUs")
            eng.sem_inc(S["u_copied"], 1)
            features("X", r_ext, r_smp[:, :, :], RG_KEEP)
            drained(eng, "FXs")
            eng.sem_inc(S["f_copied"], 1)
            ps = taken(eng, "pn")
            copied(copy(smp_new[0:NS, :, :], ps[0:NS, 0:64].rearrange("p (r t) -> p r t", r=2)), "pn")
            drained(eng, "SO")
            features("R", g_buf, g_buf[:, :, SEQ:T], 0, ACT.Gelu_apprx_tanh)
            for j in range(2):
                ps = taken(eng, f"PB{j}")
                copied(eng.activation(yT[:, j, 0:SEQ], ps[:, :], ACT.Copy, scale=params[:, P_POOL_SCALE + j:P_POOL_SCALE + j + 1]), f"PB{j}")
            ps = taken(eng, "PBs")
            for j in range(2):
                ins = eng.activation(yT[:, j, SEQ:T], ps[:, 8 * j:8 * j + 8], ACT.Copy, scale=params[:, P_POOL_SCALE + j:P_POOL_SCALE + j + 1])
            copied(ins, "PBs")
            features("Z", z_buf, z_buf[:, :, SEQ:T], 0)
            drained(eng, "FZs")
            eng.sem_inc(S["f_copied"], 1)
            tr, ti, t2, sq = m[4], m[5], m[6], m[0]
            for j in range(2):
                ps = taken(eng, f"RA{j}")
                copied(eng.activation(tr[:, j, 0:SEQ], ps[:, :], ACT.Tanh, scale=0.5, bias=half_b[:, j:j + 1]), f"RA{j}")
                ps = taken(eng, f"RX{j}")
                copied(eng.activation(ti[:, j, 0:SEQ], ps[:, :], ACT.Tanh, scale=0.5, bias=half_b[:, 2 + j:3 + j]), f"RX{j}")
            ps = taken(eng, "RGs")
            for j in range(2):
                eng.activation(tr[:, j, SEQ:T], ps[:, 8 * j:8 * j + 8], ACT.Tanh, scale=0.5, bias=half_b[:, j:j + 1])
                ins = eng.activation(ti[:, j, SEQ:T], ps[:, 16 + 8 * j:24 + 8 * j], ACT.Tanh, scale=0.5, bias=half_b[:, 2 + j:3 + j])
            copied(ins, "RGs")
            drained(eng, "RGs")
            for j in range(2):
                ins = eng.activation(t2[:, j, :], tr[:, j, :], ACT.Tanh, scale=sp[:, 4, j:j + 1], bias=sp[:, 4, j:j + 1])
            ins.then_inc(S["rg_t2"], 1)
            eng.wait_ge(S["rg_t2"], 1)
            drained(eng, "PB1")
            eng.activation(sq, t2, ACT.Sqrt).then_inc(S["rg_sqrt"], 1)

            def exps(i, u):
                n = 8 * i + u
                eng.wait_ge(S["att_max"], n + 1)
                if n >= 4:
                    job = f"T{(n - 4) // 8}.{(n - 4) % 8}"
                    eng.wait_ge(bank_full[bank_of[job]], turn_of[job] + 1)
                ps = taken(eng, f"S{i}.{u}")
                col = 8 * i + 4 * (u // 4) + 2 * (u % 2) + (u // 2) % 2
                width = 128 * (i + 1)
                copied(eng.activation(p_buf[n % 4][:, 0:width], ps[:, 0:width], ACT.Exp, bias=att_mx[:, col:col + 1], accum_out=att_sum[:, col:col + 1]), f"S{i}.{u}")

            def turned(i, u):
                n = 8 * i + u
                if n >= 4:
                    pv_done(eng, n - 4)
                ps = taken(eng, f"T{i}.{u}")
                width = 128 * (i + 1)
                copied(copy(pT_buf[n % 4][:, 0:width], ps[:, 0:width]), f"T{i}.{u}")

            for i in range(4):
                for pair in range(5):
                    if pair < 4:
                        exps(i, 2 * pair)
                        exps(i, 2 * pair + 1)
                    if pair > 0:
                        turned(i, 2 * pair - 2)
            pv_done(eng, 28)
            ps = taken(eng, "cT")
            copied(copy(pT_buf[0], ps[:, :]), "cT")
            eng.wait_ge(S["yn_made"], 1)
            for i in TILES:
                r = ROWS[i]
                eng.activation(reg_a.t[0:r, 5200 + GW * i:5200 + GW * (i + 1)], ynsa[0:r, i, :], ACT.Square, accum_out=yss[0:r, i:i + 1]).then_inc(S["yn_sq"], 1)
            for g, first in ((0, 0), (1, 2), (2, 6)):
                if g == 0:
                    drained(eng, "PBs")
                    eng.wait_ge(S["h_made"], 2)
                if g == 2:
                    eng.wait_ge(S["sc_b"], 1)
                eng.activation(m[g], yT[:, first:first + 2, :], ACT.Square).then_inc(S["sq_made"], 1)
            for g in range(3):
                ps = taken(eng, f"N{g}")
                copied(eng.activation(m[4 + g // 2][:, g % 2, 0:SEQ], ps[:, :], ACT.Sqrt, scale=1.0 / GW, bias=eps_col), f"N{g}")
            ps = taken(eng, "Ns")
            eng.activation(m[4][:, :, SEQ:T], ps[:, 0:16].rearrange("p (j t) -> p j t", j=2), ACT.Sqrt, scale=1.0 / GW, bias=eps_col)
            copied(eng.activation(m[5][:, 0, SEQ:T], ps[:, 16:24], ACT.Sqrt, scale=1.0 / GW, bias=eps_col), "Ns")
            ps = taken(eng, "TLa")
            copied(copy(tail_rows[0:24, 0:512], ps[0:24, :]), "TLa")
            ps = taken(eng, "TLb")
            copied(copy(tail_rows[0:24, 512:1024], ps[0:24, :]), "TLb")
            for i in TILES:
                r = ROWS[i]
                ps = taken(eng, f"NT{i}")
                for j in range(2):
                    ins = eng.activation(yT[:, 4 + j, COL[i]:COL[i] + r], ps[:, j * r:(j + 1) * r], ACT.Copy, scale=params[:, P_OUT_G + 4 + j:P_OUT_G + 5 + j])
                copied(ins, f"NT{i}")
            drained(eng, "TLb")
            for name_p, name_s, keep, col in (("pool_p", "pool_s", POOL_KEEP, 0), ("rgc_p", "rgc_s", RG_KEEP, 256), ("scc_p", "scc_s", SC_KEEP, 512)):
                eng.dma_start(o[name_p].rearrange("l b k c -> (l b k) c"), tail_rows[16 - keep:16, col:col + 256]).then_inc(S["tails_stored"], 16)
                eng.dma_start(o[name_s].rearrange("l b k c -> (l b) k c")[:, keep - 1, :], tail_rows[16:24, col:col + 256]).then_inc(S["tails_stored"], 16)
            eng.dma_start(o["rgh_p"].rearrange("l b c -> (l b) c"), tail_rows[15:16, 768:1024]).then_inc(S["tails_stored"], 16)
            eng.dma_start(o["rgh_s"].rearrange("l b c -> (l b) c"), tail_rows[16:24, 768:1024]).then_inc(S["tails_stored"], 16)

            def sums(n):
                i = TILES[n]
                r = ROWS[i]
                drained(eng, f"Y{i}.1")
                eng.activation(h2[0:r, i, :], x1[0:r, i, :], ACT.Square, accum_out=sumsq[0:r, i:i + 1]).then_inc(S["x1_ss"], 1)

            def h2_turned(n):
                i = TILES[n]
                r = ROWS[i]
                if n:
                    eng.wait_ge(S["routed"], n)
                for k, name in enumerate(("hTa", "hTb")):
                    ps = taken(eng, f"{name}{i}")
                    copied(copy(h2T[:, 4 * k:4 * k + 4, 0:r], ps[:, 0:4 * r].rearrange("p (c t) -> p c t", c=4)), f"{name}{i}")

            eng.wait_ge(S["rows_stored"], 16 * 4)
            eng.wait_ge(bank_full[bank_of["NT3"]], turn_of["NT3"] + 1)
            eng.wait_ge(S["h2_zeroed"], 1)
            for n in range(NTILE):
                sums(n)
                if n:
                    h2_turned(n - 1)
            h2_turned(4)
            eng.wait_ge(S["rt_d"], 1)
            eng.activation(lex, lex, ACT.Exp).then_inc(S["rt_exp"], 1)
            eng.wait_ge(S["rt_d"], 2)
            eng.activation(tdx, tdx, ACT.Exp).then_inc(S["rt_exp"], 1)

            eng.wait_ge(S["rounds_made"], 1)
            rounds = eng.value_load(n_rounds[0:1, 0:1], min_val=1, max_val=ROUNDS)
            eng.sem_inc(y_stored[0], 16)
            eng.sem_inc(y_stored[1], 16)
            eng.sem_inc(S["y_copied"], 2)
            eng.wait_ge(S["gathered"], 1)
            copy(xe[0], bank[0][:, :].rearrange("p (c s) -> p c s", c=8)).then_inc(S["xe_made"], 1)
            with eng.Fori(0, rounds) as r:
                eng.wait_ge(S["round_combined"], r + 1)
                with eng.Fori(0, N_EXP // 2) as i:
                    for b in range(2):
                        e = 2 * i + b
                        n = N_EXP * r + e
                        eng.wait_ge(S["gu_done"], n + 1)
                        eng.activation(silu[b], bank[2 + b][:, 0:256], ACT.Silu).then_inc(S["silu_done"], 1)
                        eng.wait_ge(S["gathered"], n + 2)
                        copy(xe[1 - b], bank[1 - b][:, :].rearrange("p (c s) -> p c s", c=8)).then_inc(S["xe_made"], 1)
                        eng.wait_ge(S["down_done"], n + 1)
                        eng.wait_ge(y_stored[b], (N_EXP // 2) * 16 * r + 16 * i + 16)
                        copy(y_out[b], bank[6 + b][:, :]).then_inc(S["y_copied"], 1)
                        eng.wait_ge(S["y_copied"], n + 3)
                        eng.dma_start(y_dram[bass.ds(e * CAP, CAP)].rearrange("t (s n) -> s t n", s=2), y_out[b]).then_inc(y_stored[b], 16)
                for b in range(2):
                    eng.wait_ge(y_stored[b], (N_EXP // 2) * 16 * r + (N_EXP // 2) * 16 + 16)
                eng.sem_inc(S["moe_stored"], 1)

        @block.tensor
        def _(eng):
            def mm(out, lhsT, rhs, start, stop):
                return eng.matmul(out, lhsT, rhs, start=start, stop=stop, skip_group_check=True)

            def turn(out, in_):
                return eng.transpose(out, in_, ident[0:in_.shape[0], 0:in_.shape[0]])

            eng.wait_ge(S["consts_made"], 1)
            eng.wait_ge(S["par_loaded"], 16 * PAR_DMAS)
            filled(turn(claim(eng, "params")[:, 0:P_ROWS], par_rows), "params")
            eng.wait_ge(S["xn_made"], 1)
            ps = claim(eng, "xT4")
            for c in range(KC):
                ins = turn(ps[:, 8 * c:8 * c + 8], xn[0:NS, 4, 128 * c:128 * c + 128])
            filled(ins, "xT4")
            for i in range(4):
                eng.wait_ge(S["xn_made"], i + 2)
                for k, name in enumerate(("xTa", "xTb")):
                    ps = claim(eng, f"{name}{i}")
                    for c in range(4):
                        ins = turn(ps[:, 128 * c:128 * c + 128], xn[:, i, 512 * k + 128 * c:512 * k + 128 * c + 128])
                    filled(ins, f"{name}{i}")
            eng.wait_ge(S["states_loaded"], 16 * 4)
            ps = claim(eng, "states")
            for j in range(2):
                turn(ps[:, 48 * j:48 * j + 48], st_rows[:, 128 * j:128 * j + 128])
                ins = turn(ps[:, 96 + 120 * j:216 + 120 * j], st_pool[:, 128 * j:128 * j + 128])
            filled(ins, "states")

            def project(n, i):
                r = ROWS[i]
                for half, name in enumerate("AB"):
                    ps = claim(eng, f"{name}{i}")
                    for k in range(2):
                        w = 2 * half + k
                        if n == 0:
                            eng.wait_ge(w_loaded[w], 32 if w == 3 else 16)
                        for c in range(KC):
                            ins = mm(ps[0:r, 256 * k:256 * k + 256], xnT[:, c, COL[i]:COL[i] + r], w_slot[w][:, c, :], c == 0, c == KC - 1)
                    filled(ins, f"{name}{i}")

            def turn_qk(n):
                i = TILES[n]
                r = ROWS[i]
                eng.wait_ge(S["qk_normed"], n + 1)
                ps = claim(eng, f"K{i}")
                q = qn_buf[n % 2]
                for g in range(2):
                    turn(ps[:, g * r:(g + 1) * r], q[0:r, 256 + 128 * g:384 + 128 * g])
                turn(ps[:, 2 * r:3 * r], rows[0:r, i, 256:384])
                filled(turn(ps[:, 3 * r:4 * r], win[0:r, i, 0:128]), f"K{i}")
                if i < 4:
                    ps = claim(eng, f"R{i}")
                    turn(ps[:, 0:128], rows[:, i, 0:128])
                    filled(turn(ps[:, 128:256], rows[:, i, 128:256]), f"R{i}")

            for n, i in enumerate(TILES):
                if i == 4:
                    drained(eng, "xT4")
                else:
                    drained(eng, f"xTa{i}")
                    drained(eng, f"xTb{i}")
                project(n, i)
                if n:
                    turn_qk(n - 1)
            turn_qk(4)
            ps = claim(eng, "G")
            for i in range(NTILE):
                r = ROWS[i]
                for c in range(KC):
                    ins = mm(ps[0:r, 12 * i:12 * i + 12], xnT[:, c, COL[i]:COL[i] + r], w_gate[:, c, :], c == 0, c == KC - 1)
            filled(ins, "G")

            eng.wait_ge(S["q_masked_made"], 1)
            claim(eng, "SS")
            claim(eng, "SW")

            def sample_scores(b):
                drained(eng, f"sK{b}")
                for r, name in enumerate(("SS", "SW")):
                    ins = mm(bank[bank_of[name]][0:32, 0:257], q_masked[:, 32 * b:32 * b + 32], smp_kT[b % 2][:, r, :], b == 0, b == NS - 1)
                    if b == NS - 1 and name == "SS":
                        filled(ins, name)
                if b == NS - 1:
                    filled(ins, "SW")
                else:
                    ins.then_inc(S["sample_scores"], 1)

            for b in range(NS):
                eng.wait_ge(smp_loaded[b % 2], 48 * (b // 2 + 1))
                ps = claim(eng, f"sR{b}")
                for c in range(2):
                    for g in range(2):
                        ins = turn(ps[:, 256 * c + 128 * g:256 * c + 128 * g + 128], page_k[b % 2][:, g, 128 * c:128 * c + 128])
                filled(ins, f"sR{b}")
                ps = claim(eng, f"sK{b}")
                for g in range(2):
                    turn(ps[:, 128 * g:128 * g + 128], page_k[b % 2][:, g, 256:384])
                for g in range(2):
                    ins = turn(ps[:, 256 + 128 * g:384 + 128 * g], win_k[b % 2][:, g, :])
                filled(ins, f"sK{b}")
                if b:
                    sample_scores(b - 1)
            sample_scores(NS - 1)
            eng.wait_ge(S["phi_loaded"], 16 * 4)
            drained(eng, f"sR{NS - 1}")
            for comp, name in enumerate(("CK", "CV")):
                ps2 = [claim(eng, f"{name}{kv}") for kv in range(2)]
                for half in range(2):
                    for j in range(16):
                        for kv in range(2):
                            lo = 64 * kv
                            src = raw[lo:lo + 64, comp, :].rearrange("p (n s) -> p n s", s=16)[:, :, j]
                            ins = mm(ps2[kv][lo:lo + 64, N_CHUNK * half:N_CHUNK * (half + 1)], phi[lo:lo + 64, comp, 16 * half + j, :], src, j == 0, j == 15)
                            if half == 1 and j == 15:
                                filled(ins, f"{name}{kv}")
            eng.wait_ge(S["kc_squared"], 1)
            filled(mm(claim(eng, "CN")[:, 0:N_CHUNK], block_ones, kc_sq, True, True), "CN")
            eng.wait_ge(S["kc_made"], 1)
            ps = claim(eng, "VT")
            turn(ps[:, 0:128], kc_a[:, 0:128])
            filled(turn(ps[:, 128:256], vcT[:, 32:160]), "VT")
            ps = claim(eng, "cs")
            for b in range(NS):
                ins = mm(ps[0:32, 0:15], q_masked[:, 32 * b:32 * b + 32], kcT[:, 32 + 16 * b:47 + 16 * b], b == 0, b == NS - 1)
            filled(ins, "cs")
            ps2 = [claim(eng, f"cp{kv}") for kv in range(2)]
            for i in range(4):
                for g in range(2):
                    for kv in range(2):
                        lo, u = 64 * kv, 2 * i + g
                        ins = mm(ps2[kv][:, 32 * u:32 * u + 31], qT[lo:lo + 64, g, COL[i]:COL[i] + 128], kcT[lo:lo + 64, 0:31], True, True)
                        if u == 7:
                            filled(ins, f"cp{kv}")
            eng.wait_ge(S["gates_raw"], 1)
            filled(mm(claim(eng, "g32")[0:32, 0:12], sample_of_row[0:8, :], gates[0:NS, 4, :], True, True), "g32")

            def features(g):
                n = 4 + "UXRZCB".index(g)
                eng.wait_ge(w_loaded[n % W_SLOTS], 16 * (n // W_SLOTS + 1) + (16 if n % W_SLOTS == 3 else 0))
                pss = claim(eng, f"F{g}s")
                for j in range(2):
                    ps = claim(eng, f"F{g}{j}")
                    for c in range(KC):
                        w = w_slot[n % W_SLOTS][:, c, 128 * j:128 * j + 128]
                        if c < KC - 1 or j == 0:
                            mm(pss[:, 8 * j:8 * j + 8], w, xnT[:, c, SEQ:T], c == 0, c == KC - 1)
                            ins = mm(ps[:, :], w, xnT[:, c, 0:SEQ], c == 0, c == KC - 1)
                        else:
                            filled(mm(pss[:, 8 * j:8 * j + 8], w, xnT[:, c, SEQ:T], False, True), f"F{g}s")
                            ins = mm(ps[:, :], w, xnT[:, c, 0:SEQ], False, True)
                    filled(ins, f"F{g}{j}")

            features("U")
            features("X")
            eng.wait_ge(S["sp_scaled"], 1)
            ps = claim(eng, "PT")
            for r in range(2):
                for g in range(2):
                    turn(ps[:, 64 * r + 32 * g:64 * r + 32 * g + 32], smp_p[0:32, r, 128 * g:128 * g + 128])
            filled(turn(ps[:, 128:160], smp_pc3[0:32].rearrange("p b c -> p (b c)")), "PT")
            filled(mm(claim(eng, "pn")[0:NS, 0:64], row_of_sample[0:32, :], smp_diag[0:32].rearrange("p r t -> p (r t)"), True, True), "pn")
            drained(eng, "PT")
            drained(eng, "pn")
            eng.wait_ge(S["vcache_loaded"], 16 * (2 * NS + 2))
            ps = claim(eng, "SO")
            for r, v in enumerate((vs_cache, vw_cache)):
                for g in range(2):
                    for b in range(NS):
                        at = 32 * NS * (2 * r + g) + 32 * b
                        mm(ps[0:32, 0:128], p_masked[:, at:at + 32], v[:, b, g, :], r == 0 and g == 0 and b == 0, False)
            mm(ps[0:32, 0:128], smp_new[0:NS, 0, :], rows[0:NS, 4, 384:512], False, False)
            mm(ps[0:32, 0:128], smp_new[0:NS, 1, :], win[0:NS, 4, 128:256], False, False)
            filled(mm(ps[0:32, 0:128], smp_pcT, vc_smp, False, True), "SO")
            features("R")
            eng.wait_ge(S["blocks_loaded"], 16 * 12)
            eng.wait_ge(S["pool_d"], 1)
            ps = claim(eng, "PBs")
            for j in range(2):
                ins = mm(ps[:, 8 * j:8 * j + 8], pool_w[:, j, :], m[3][:, j, SEQ:T], True, True)
            filled(ins, "PBs")
            for j in range(2):
                filled(mm(claim(eng, f"PB{j}")[:, :], pool_w[:, j, :], m[3][:, j, 0:SEQ], True, True), f"PB{j}")
            features("Z")
            eng.wait_ge(S["conv_made"], 1)
            xc = m[1]
            ps = claim(eng, "RGs")
            for k in range(4):
                ins = mm(ps[:, 8 * k:8 * k + 8], rg_w[:, k, :], xc[:, k % 2, SEQ:T], True, True)
            filled(ins, "RGs")
            for j in range(2):
                for k, name in enumerate(("RA", "RX")):
                    filled(mm(claim(eng, f"{name}{j}")[:, :], rg_w[:, 2 * k + j, :], xc[:, j, 0:SEQ], True, True), f"{name}{j}")
            features("C")
            features("B")

            def head(u):
                return u // 4, (u // 2) % 2, u % 2

            def scores(i, pair):
                width = 128 * (i + 1)
                outs = [claim(eng, f"S{i}.{2 * pair + kv}") for kv in range(2)]
                for kv in range(2):
                    br, g, _ = head(2 * pair)
                    lo = 64 * kv
                    mm(outs[kv][:, 0:width], qT[lo:lo + 64, g, COL[i]:COL[i] + 128], kT[lo:lo + 64, br, 0:width], True, False)
                for kv in range(2):
                    filled(mm(outs[kv][:, 128 * i:width], ident_bf[:, :], causal_bf[:, :], False, True), f"S{i}.{2 * pair + kv}")

            def turn_p(i, u):
                n = 8 * i + u
                drained(eng, f"S{i}.{u}")
                ps = claim(eng, f"T{i}.{u}")
                for c in range(i + 1):
                    ins = turn(ps[:, 128 * c:128 * c + 128], p_buf[n % 4][:, 128 * c:128 * c + 128])
                filled(ins, f"T{i}.{u}")

            def values(i, u):
                n = 8 * i + u
                br, g, kv = head(u)
                drained(eng, f"T{i}.{u}")
                ps = bank[bank_of[f"O{i}"]]
                at = 256 * br + 64 * (2 * kv + g)
                src = (rows, 384) if br == 0 else (win, 128)
                for c in range(i + 1):
                    ins = mm(ps[:, at:at + 64], pT_buf[n % 4][:, 128 * c:128 * c + 128], src[0][:, c, src[1] + 64 * kv:src[1] + 64 * kv + 64], c == 0, c == i)
                if u == 7:
                    filled(ins, f"O{i}")
                else:
                    ins.then_inc(S["att_pv"], 1)

            for i in range(4):
                claim(eng, f"O{i}")
                for pair in range(5):
                    if pair < 4:
                        scores(i, pair)
                    if pair > 0:
                        turn_p(i, 2 * pair - 2)
                        turn_p(i, 2 * pair - 1)
                        values(i, 2 * pair - 2)
                        values(i, 2 * pair - 1)
            eng.wait_ge(S["cmp_scaled"], 1)
            ps = claim(eng, "cT")
            for i in range(4):
                ins = turn(ps[:, 128 * i:128 * i + 128], cmp_s[:, 4 * i:4 * i + 4, :].rearrange("p u c -> p (u c)"))
            filled(ins, "cT")
            drained(eng, "cT")
            for i in range(4):
                filled(mm(claim(eng, f"Oc{i}")[:, 0:256], pT_buf[0][:, 128 * i:128 * i + 128], vc_blk, True, True), f"Oc{i}")
            for g in range(3):
                eng.wait_ge(S["sq_made"], g + 1)
                ps = claim(eng, f"N{g}")
                for j in range(2):
                    ins = mm(ps[:, :], ones, m[g][:, j, 0:SEQ], j == 0, j == 1)
                filled(ins, f"N{g}")
            ps = claim(eng, "Ns")
            for g in range(3):
                for j in range(2):
                    ins = mm(ps[:, 8 * g:8 * g + 8], ones, m[g][:, j, SEQ:T], j == 0, j == 1)
            filled(ins, "Ns")
            eng.wait_ge(S["tails_made"], 1)
            for k, name in enumerate(("TLa", "TLb")):
                ps = claim(eng, name)
                for c in range(4):
                    ins = turn(ps[0:24, 128 * c:128 * c + 128], tails[:, 4 * k + c, :])
                filled(ins, name)
            eng.wait_ge(S["yn_scaled"], 1)
            for i in TILES:
                r = ROWS[i]
                ps = claim(eng, f"NT{i}")
                for j in range(2):
                    ins = turn(ps[:, j * r:(j + 1) * r], ynsa[0:r, i, 128 * j:128 * j + 128])
                filled(ins, f"NT{i}")
            eng.wait_ge(S["wout_loaded"], 16)
            eng.wait_ge(S["yT_ready"], 1)
            claim(eng, "L")

            def project_out(n):
                i = TILES[n]
                r = ROWS[i]
                drained(eng, f"NT{i}")
                for half in range(2):
                    if half == 1 and n >= 2:
                        route(n - 2)
                    ps = claim(eng, f"Y{i}.{half}")
                    for c in range(KC):
                        ins = mm(ps[0:r, :], yT[:, c, COL[i]:COL[i] + r], w_out[:, c, 512 * half:512 * half + 512], c == 0, c == KC - 1)
                    filled(ins, f"Y{i}.{half}")

            def turn_h2(n):
                i = TILES[n]
                r = ROWS[i]
                eng.wait_ge(S["h2_made"], n + 1)
                for k, name in enumerate(("hTa", "hTb")):
                    ps = claim(eng, f"{name}{i}")
                    for c in range(4):
                        ins = turn(ps[:, c * r:(c + 1) * r], h2[0:r, i, 512 * k + 128 * c:512 * k + 128 * c + 128])
                    filled(ins, f"{name}{i}")

            def route(n):
                i = TILES[n]
                r = ROWS[i]
                drained(eng, f"hTb{i}")
                if n == 0:
                    eng.wait_ge(S["rtw_loaded"], 16 * 4)
                ps = bank[bank_of["L"]]
                for c in range(KC):
                    ins = mm(ps[0:r, 36 * i:36 * i + 36], h2T[:, c, 0:r], rt_w[:, c, :], c == 0, c == KC - 1)
                if n < 4:
                    ins.then_inc(S["routed"], 1)
                else:
                    filled(ins, "L")

            for n in range(NTILE):
                project_out(n)
                if n:
                    turn_h2(n - 1)
            route(3)
            turn_h2(4)
            route(4)
            eng.wait_ge(S["mask_made"], 1)
            ps = claim(eng, "pos")
            for i in range(NTILE):
                for k in range(i + 1):
                    ins = mm(ps[:, 32 * i:32 * i + 32], before_bf[:, :] if k == i else ones_bf[:, :], mask_bf[:, k, :], k == 0, k == i)
            filled(ins, "pos")
            ps = claim(eng, "cnt")
            for k in range(NTILE):
                ins = mm(ps[:, 0:32], ones_bf[:, :], mask_bf[:, k, :], k == 0, k == NTILE - 1)
            filled(ins, "cnt")

            def gather(b, chunks):
                for c in chunks:
                    for t in range(NTILE):
                        ins = mm(bank[b][:, 64 * c:64 * c + 64], h2[:, t, c:D:8], onehot[b][:, t, :], t == 0, t == NTILE - 1)
                return ins

            eng.wait_ge(S["rounds_made"], 1)
            rounds = eng.value_load(n_rounds[0:1, 0:1], min_val=1, max_val=ROUNDS)
            for b in range(8):
                eng.wait_ge(bank_read[b], uses[b])
            eng.wait_ge(S["onehot_made"], 1)
            gather(0, range(8)).then_inc(S["gathered"], 1)
            with eng.Fori(0, rounds) as r:
                with eng.Fori(0, N_EXP // 2) as i:
                    for b in range(2):
                        n = N_EXP * r + 2 * i + b
                        eng.wait_ge(gu_loaded[b], (N_EXP // 2) * 16 * r + 16 * i + 16)
                        eng.wait_ge(S["xe_made"], n + 1)
                        for c in range(KC):
                            for s in range(2):
                                w = gu_w[b][:, c, :].rearrange("p (h f) -> p h f", h=2)[:, :, 256 * s:256 * s + 256]
                                ins = mm(bank[2 + b][64 * s:64 * s + 64, :].rearrange("p (h f) -> p h f", h=2), xe[b][:, c, :], w, c == 0, c == KC - 1)
                        ins.then_inc(S["gu_done"], 1)
                        eng.wait_ge(S["onehot_made"], n + 2)
                        gather(1 - b, range(4))
                        eng.wait_ge(S["hid_made"], n + 1)
                        for k in range(2):
                            ins = turn(bank[4 + b][:, 128 * k:128 * k + 128], hid[b].rearrange("p (f k) -> p f k", k=2)[:, :, k])
                        ins.then_inc(S["xt_turned"], 1)
                        gather(1 - b, range(4, 8)).then_inc(S["gathered"], 1)
                        eng.wait_ge(down_loaded[b], (N_EXP // 2) * 16 * r + 16 * i + 16)
                        eng.wait_ge(S["hT_made"], n + 1)
                        eng.wait_ge(S["y_copied"], n + 1)
                        for s_in in range(2):
                            for k in range(2):
                                for s in range(2):
                                    ins = mm(bank[6 + b][64 * s:64 * s + 64, :], hT[b][:, k, 64 * s_in:64 * s_in + 64], down_w[b][:, s_in, k, 512 * s:512 * s + 512], s_in == 0 and k == 0, s_in == 1 and k == 1)
                        ins.then_inc(S["down_done"], 1)

        @block.vector
        def _(eng):
            link = chain_of(eng, "vector_chain")
            tt, ts, stt = eng.tensor_tensor, eng.tensor_scalar, eng.scalar_tensor_tensor
            ps = taken(eng, "params")
            copied(eng.tensor_copy(params, ps[:, 0:P_ROWS]), "params")
            drained(eng, "params")
            eng.wait_ge(S["consts_made"], 1)
            ts(half_b, params[:, P_BA:P_BA + 4], 0.5, None, ALU.mult)
            lam = params[:, P_LAM:P_LAM + 2]
            ts(sp[:, 1, :], lam, -1.0, None, ALU.mult)
            link(ts(qg_scaled, params[:, P_QG:P_QG + 1], HD ** -0.5, None, ALU.mult))
            tt(sp[:, 0, :], lam, sp[:, 1, :], ALU.max).then_inc(S["sp_exp_asked"], 1)
            for k, win_len in enumerate((2, 4, 8, 16)):
                lo, j = 64 * (k % 2), k // 2
                ts(inv_cnt[lo:lo + 64, j, :], inv_cnt[lo:lo + 64, j, :], float(win_len), None, ALU.min)
                ins = eng.memset(inv_win[lo:lo + 64, j:j + 1], 1.0 / win_len)
            link(ins)
            link(eng.reciprocal(inv_cnt, inv_cnt))
            link(eng.tensor_reduce(head_of_row[0:32, :], hr3[0:32].rearrange("p b h -> p h b"), X_AXIS, ALU.add))
            link(eng.tensor_reduce(kv_of_row[0:32, :], head_of_row[0:32, :].rearrange("p (k g) -> p k g", k=2), X_AXIS, ALU.add))

            eng.wait_ge(S["gain_loaded"], 16)
            for n, i in enumerate(TILES):
                r = ROWS[i]
                eng.wait_ge(S["xsq_done"], n + 1)
                ts(sumsq[0:r, i:i + 1], sumsq[0:r, i:i + 1], 1.0 / D, EPS, ALU.mult, ALU.add).then_inc(S["rstd_asked"], 1)
            for n, i in enumerate(TILES):
                r = ROWS[i]
                eng.wait_ge(S["rstd_made"], n + 1)
                stt(xn[0:r, i, :], x_in[0:r, i, :], rstd[0:r, i:i + 1], gain_mix[0:r, :], ALU.mult, ALU.mult).then_inc(S["xn_made"], 1)
            eng.wait_ge(S["sp_exp"], 1)
            link(ts(sp[:, 2, :], sp[:, 1, :], 2.0, None, ALU.add))
            link(eng.reciprocal(sp[:, 2, :], sp[:, 2, :]))
            link(tt(sp[:, 1, :], sp[:, 1, :], sp[:, 2, :], ALU.mult))
            link(tt(sp[:, 2, :], sp[:, 1, :], sp[:, 1, :], ALU.mult))
            link(ts(sp[:, 3, :], sp[:, 2, :], 1.0 / 19, None, ALU.mult))
            for k in range(8, 0, -1):
                link(stt(sp[:, 3, :], sp[:, 3, :], 1.0 / (2 * k + 1), sp[:, 2, :], ALU.add, ALU.mult))
            link(stt(sp[:, 3, :], sp[:, 3, :], 1.0, sp[:, 1, :], ALU.add, ALU.mult))
            link(ts(sp[:, 4, :], lam, -1.0, 0.0, ALU.mult, ALU.max))
            link(ts(sp[:, 4, :], sp[:, 4, :], 2.0, None, ALU.mult))
            link(stt(sp[:, 4, :], sp[:, 3, :], 4.0, sp[:, 4, :], ALU.mult, ALU.add))
            eng.sem_inc(S["params_made"], 1)
            for i in range(4):
                ps = taken(eng, f"xTb{i}")
                copied(eng.tensor_copy(xnT[:, 4:8, COL[i]:COL[i] + 128], ps[:, :].rearrange("p (c t) -> p c t", c=4)), f"xTb{i}")

            eng.wait_ge(S["kg_loaded"], 16)
            for n, i in enumerate(TILES):
                r = ROWS[i]
                q, sq = qn_buf[n % 2], sq_buf[n % 2]
                ksel, kwin = rows[0:r, i, 256:384], win[0:r, i, 0:128]
                drained(eng, f"B{i}")
                drained(eng, f"A{i}")
                tt(sq[0:r, 0:256], q[0:r, 0:256], q[0:r, 0:256], ALU.mult)
                tt(sq[0:r, 256:384], ksel, ksel, ALU.mult)
                link(tt(sq[0:r, 384:512], kwin, kwin, ALU.mult))
                link(eng.tensor_reduce(hss[0:r, i, :], sq[0:r, :].rearrange("p (h d) -> p h d", h=8), X_AXIS, ALU.add))
                ts(hss[0:r, i, :], hss[0:r, i, :], 1.0 / HD, EPS, ALU.mult, ALU.add).then_inc(S["hss_made"], 1)
                eng.wait_ge(S["hrs_made"], n + 1)
                tt(q[0:r, 256:512].rearrange("p (g k d) -> p k g d", g=2, k=2), q[0:r, 0:256].rearrange("p (k g d) -> p k g d", g=2, k=2),
                   hrs[0:r, i, 0:4].rearrange("p (k g) -> p k g", k=2).unsqueeze(3).to_broadcast([r, 2, 2, HD]), ALU.mult)
                for br, k in enumerate((ksel, kwin)):
                    v = k.rearrange("p (k d) -> p k d", k=2)
                    link(tt(v, v, hrs[0:r, i, 4 + 2 * br:6 + 2 * br].unsqueeze(2).to_broadcast([r, 2, HD]), ALU.mult))
                    ins = tt(v, v, kg[0:r, br:br + 1, :].to_broadcast([r, 2, HD]), ALU.mult)
                ins.then_inc(S["qk_normed"], 1)
            drained(eng, "G")
            ts(gates[0:NS, 4, :], gates[0:NS, 4, :], 0.5, 0.5, ALU.mult, ALU.add)
            ts(gates[:, 0:4, :], gates[:, 0:4, :], 0.5, 0.5, ALU.mult, ALU.add).then_inc(S["gates_raw"], 1)
            drained(eng, "K4")
            for kv in range(2):
                lo = 64 * kv
                for g in range(2):
                    first = 2 * kv + g
                    dst = q_masked[lo:lo + 64, first:first + 36 * (NS - 1) + 1:36]
                    ins = eng.tensor_copy(dst, qT[lo:lo + 64, g, SEQ:T])
            ins.then_inc(S["q_masked_made"], 1)
            eng.memset(kcT[:, N_CHUNK - 1:N_CHUNK], 0.0)
            for comp, (name, first, out) in enumerate((("CK", kc_a, kcT), ("CV", vcT, vcT))):
                for kv in range(2):
                    lo = 64 * kv
                    eng.wait_ge(S["kc_copied"], 2 * comp + kv + 1)
                    ps = taken(eng, f"{name}{kv}")
                    copied(tt(out[lo:lo + 64, 0:N_CHUNK - 1], first[lo:lo + 64, 0:N_CHUNK - 1], ps[lo:lo + 64, N_CHUNK + 1:2 * N_CHUNK], ALU.add), f"{name}{kv}")
                    drained(eng, f"{name}{kv}")
                if comp == 0:
                    eng.sem_inc(S["kc_sum"], 1)
            ps = taken(eng, "CN")
            copied(ts(kc_a, ps[:, 0:N_CHUNK], 1.0 / HD, EPS, ALU.mult, ALU.add), "CN")
            drained(eng, "CN")
            eng.sem_inc(S["kc_ms"], 1)
            eng.wait_ge(S["kc_rstd"], 1)
            link(stt(kcT, kcT, params[:, P_KCG:P_KCG + 1], kc_sq, ALU.mult, ALU.mult))
            eng.tensor_copy(kc_a[:, 0:128].rearrange("p (h c) -> p h c", h=4), vcT[:, 0:32].unsqueeze(1).to_broadcast([128, 4, 32])).then_inc(S["kc_made"], 1)
            ps = taken(eng, "VT")
            eng.tensor_copy(vc_smp, ps[:, 128:256])
            for kv in range(2):
                for g in range(2):
                    h = 2 * kv + g
                    ins = eng.tensor_copy(vc_blk[32 * h:32 * h + 32, 64 * h:64 * h + 64], ps[32 * h:32 * h + 32, 64 * kv:64 * kv + 64])
            copied(ins, "VT")
            for r, name in enumerate(("SS", "SW", "cs")):
                ps = taken(eng, name)
                width = 257 if r < 2 else 15
                eng.tensor_reduce(smx[0:32, r:r + 1], ps[0:32, 0:width], X_AXIS, ALU.max, negate=True).then_inc(S["smax_made"], 1)
            eng.memset(cmp_s[:, :, 31:32], NEG)
            for kv in range(2):
                ps = taken(eng, f"cp{kv}")
                for i in range(4):
                    ins = tt(cmp_s[:, 4 * i + 2 * kv:4 * i + 2 * kv + 2, 0:31], ps[:, 64 * i:64 * i + 64].rearrange("p (u c) -> p u c", u=2)[:, :, 0:31],
                             cmp_mask[:, i:i + 1, 0:31].to_broadcast([128, 2, 31]), ALU.add)
                copied(ins, f"cp{kv}")
                drained(eng, f"cp{kv}")
            link(eng.tensor_reduce(cmp_mx, cmp_s, X_AXIS, ALU.max))
            link(ts(cmp_mx, cmp_mx, NEG / 10, None, ALU.max))
            tt(cmp_s, cmp_s, cmp_mx.unsqueeze(2).to_broadcast([128, 16, 32]), ALU.subtract).then_inc(S["cmp_max"], 1)
            ps = taken(eng, "g32")
            copied(tt(g32m[0:32, :].rearrange("p (h x) -> p h x", h=4), ps[0:32, 0:12].rearrange("p (h x) -> p h x", h=4),
                      head_of_row[0:32, :].unsqueeze(2).to_broadcast([32, 4, 3]), ALU.mult), "g32")
            drained(eng, "g32")
            link(eng.tensor_reduce(g3[0:32, :], g32m[0:32, :].rearrange("p (h x) -> p x h", h=4), X_AXIS, ALU.add))
            drained(eng, "SS")
            drained(eng, "SW")
            drained(eng, "cs")
            link(eng.reciprocal(ssum[0:32, :], ssum[0:32, :]))
            tt(smx[0:32, 0:2], g3[0:32, 1:3], ssum[0:32, 0:2], ALU.mult)
            link(tt(smx[0:32, 2:3], g3[0:32, 0:1], ssum[0:32, 2:3], ALU.mult))
            for r in range(2):
                ts(smp_p[0:32, r, :], smp_p[0:32, r, :], smx[0:32, r:r + 1], None, ALU.mult)
            eng.memset(smp_pc[0:32, 15:16], 0.0)
            link(ts(smp_pc[0:32, 0:15], smp_pc[0:32, 0:15], smx[0:32, 2:3], None, ALU.mult))
            tt(smp_pc3[0:32], smp_pc[0:32, :].unsqueeze(1).to_broadcast([32, NS, 16]), row_of_sample[0:32, :].unsqueeze(2).to_broadcast([32, NS, 16]), ALU.mult)
            for r in range(2):
                ins = ts(smp_diag[0:32, r, :], ident[0:32, 0:32], smp_p[0:32, r, 256:257], None, ALU.mult)
            ins.then_inc(S["sp_scaled"], 1)
            eng.wait_ge(S["cmp_exp"], 1)
            link(eng.tensor_reduce(cmp_sum, cmp_s, X_AXIS, ALU.add))
            link(ts(cmp_sum, cmp_sum, 1e-30, None, ALU.max))
            link(eng.reciprocal(cmp_sum, cmp_sum))
            link(tt(cmp_w.rearrange("p (t h) -> p t h", t=4), cmp_sum.rearrange("p (t h) -> p t h", t=4),
                    gates[:, 0:4, :].rearrange("p t (h x) -> p t h x", h=4)[:, :, :, 0], ALU.mult))
            tt(cmp_s, cmp_s, cmp_w.unsqueeze(2).to_broadcast([128, 16, 32]), ALU.mult).then_inc(S["cmp_scaled"], 1)
            eng.memset(u_ext[:, :, 0:POOL_KEEP], 0.0)
            eng.memset(r_ext[:, :, 0:RG_KEEP], 0.0)
            link(eng.memset(c_ext[:, :, 0:SC_KEEP], 0.0))
            eng.sem_inc(S["u_copied"], 1)
            ps = taken(eng, "PT")
            for k in range(4):
                dst = p_masked[:, 256 * k:256 * k + 256]
                for h in range(4):
                    eng.tensor_copy(dst[:, h:h + 36 * (NS - 1) + 1:36], ps[:, 32 * k + h:32 * k + 32:4])
            copied(eng.tensor_copy(smp_pcT, ps[:, 128:160]), "PT")
            ps = taken(eng, "SO")
            link(ts(smp_o[0:32, :], ps[0:32, 0:64], kv_of_row[0:32, 0:1], None, ALU.mult))
            copied(stt(smp_o2[0:32, :], ps[0:32, 64:128], kv_of_row[0:32, 1:2], smp_o[0:32, :], ALU.mult, ALU.add), "SO")
            drained(eng, "SO")
            eng.sem_inc(S["smp_o_made"], 1)
            d = m[3]
            eng.wait_ge(S["u_copied"], 2)
            drained(eng, "states")
            for k, win_len in enumerate((2, 4, 8, 16)):
                lo, j = 64 * (k % 2), k // 2
                link(eng.tensor_reduce(d[lo:lo + 64, j, SEQ:T], st_poolT[j][lo:lo + 64, :, POOL_KEEP - win_len + 1:POOL_KEEP], X_AXIS, ALU.add))
                link(tt(d[lo:lo + 64, j, SEQ:T], d[lo:lo + 64, j, SEQ:T], u_smp[lo:lo + 64, j, :], ALU.add))
                link(ts(d[lo:lo + 64, j, SEQ:T], d[lo:lo + 64, j, SEQ:T], inv_win[lo:lo + 64, j:j + 1], None, ALU.mult))
            eng.sem_inc(S["pool_pad"], 1)
            eng.wait_ge(S["f_copied"], 1)
            xc, u, a_, mm_, sq = m[1], m[4], m[2], m[5], m[0]
            eng.wait_ge(S["pool_d"], 1)

            def conv(out, ext, new, keep, w_at, b_at, old_at):
                taps = keep + 1
                for j in range(2):
                    w = [params[:, w_at + 2 * k + j:w_at + 2 * k + j + 1] for k in range(taps)]
                    bias = params[:, b_at + j:b_at + j + 1]
                    old = st_misc[j][:, old_at:old_at + NS * keep].rearrange("p (b k) -> p b k", k=keep)
                    ts(out[:, j, 0:SEQ], ext[:, j, 0:SEQ], w[0], bias, ALU.mult, ALU.add)
                    link(ts(out[:, j, SEQ:T], old[:, :, 0], w[0], bias, ALU.mult, ALU.add))
                    for k in range(1, taps):
                        stt(out[:, j, 0:SEQ], ext[:, j, k:k + SEQ], w[k], out[:, j, 0:SEQ], ALU.mult, ALU.add)
                        src = old[:, :, k] if k < keep else new[:, j, :]
                        link(stt(out[:, j, SEQ:T], src, w[k], out[:, j, SEQ:T], ALU.mult, ALU.add))

            conv(xc, r_ext, r_smp, RG_KEEP, P_CONV_W, P_CONV_B, 0)
            eng.sem_inc(S["conv_made"], 1)
            eng.wait_ge(S["f_copied"], 2)
            for j in range(2):
                ps = taken(eng, f"FC{j}")
                copied(tt(c_ext[:, j, SC_KEEP:SC_KEEP + SEQ], z_buf[:, j, 0:SEQ], ps[:, :], ALU.mult), f"FC{j}")
            ps = taken(eng, "FCs")
            copied(tt(c_smp[:, :, :], z_buf[:, :, SEQ:T], ps[:, 0:16].rearrange("p (j t) -> p j t", j=2), ALU.mult), "FCs")
            drained(eng, "FCs")
            eng.sem_inc(S["sc_z"], 1)
            conv(z_buf, c_ext, c_smp, SC_KEEP, P_SC_W, P_SC_B, 24)
            for j in range(2):
                ps = taken(eng, f"FB{j}")
                copied(tt(yT[:, 6 + j, 0:SEQ], z_buf[:, j, 0:SEQ], ps[:, :], ALU.mult), f"FB{j}")
            ps = taken(eng, "FBs")
            copied(tt(yT[:, 6:8, SEQ:T], z_buf[:, :, SEQ:T], ps[:, 0:16].rearrange("p (j t) -> p j t", j=2), ALU.mult), "FBs")
            drained(eng, "FBs")
            eng.sem_inc(S["sc_b"], 1)
            ti, t2 = m[5], m[6]
            eng.wait_ge(S["rg_t2"], 1)
            link(ts(u, t2, 1.0, None, ALU.add))
            link(eng.reciprocal(u, u))
            ts(a_, u, 2.0, -1.0, ALU.mult, ALU.add)
            link(stt(ti, ti, 1.0, xc, ALU.add, ALU.mult))
            link(tt(ti, ti, u, ALU.mult))
            eng.wait_ge(S["rg_sqrt"], 1)
            link(tt(ti, ti, sq, ALU.mult))
            h = m[3]
            eng.wait_ge(bank_full[bank_of["PB1"]], turn_of["PB1"] + 1)
            for j in range(2):
                eng.tensor_tensor_scan(h[:, j, 0:SEQ], a_[:, j, 0:SEQ], ti[:, j, 0:SEQ], 0.0, ALU.mult, ALU.add)
                link(tt(h[:, j, SEQ:T], a_[:, j, SEQ:T], st_misc[j][:, 40:48], ALU.mult))
                link(tt(h[:, j, SEQ:T], h[:, j, SEQ:T], ti[:, j, SEQ:T], ALU.add))
            eng.sem_inc(S["h_made"], 1)
            drained(eng, "FRs")
            link(tt(yT[:, 2:4, :], h, g_buf, ALU.mult))
            eng.sem_inc(S["h_made"], 1)

            def row_max(i, u):
                col = 8 * i + 4 * (u // 4) + 2 * (u % 2) + (u // 2) % 2
                width = 128 * (i + 1)
                ps = taken(eng, f"S{i}.{u}")
                eng.tensor_reduce(att_mx[:, col:col + 1], ps[:, 0:width], X_AXIS, ALU.max, negate=True).then_inc(S["att_max"], 1)

            def turned(i, u):
                n = 8 * i + u
                if n >= 4:
                    pv_done(eng, n - 4)
                ps = taken(eng, f"T{i}.{u}")
                width = 128 * (i + 1)
                copied(eng.tensor_copy(pT_buf[n % 4][:, 0:width], ps[:, 0:width]), f"T{i}.{u}")

            for i in range(4):
                for pair in range(5):
                    if pair < 4:
                        row_max(i, 2 * pair)
                        row_max(i, 2 * pair + 1)
                    if pair > 0:
                        turned(i, 2 * pair - 1)
                drained(eng, f"S{i}.7")
                w8 = att_w[:, 8 * i:8 * i + 8]
                link(eng.reciprocal(w8, att_sum[:, 8 * i:8 * i + 8]))
                link(tt(w8.rearrange("p (x h) -> p x h", x=2), w8.rearrange("p (x h) -> p x h", x=2),
                        gates[:, i, :].rearrange("p (h x) -> p x h", h=4)[:, 1:3, :], ALU.mult))
                ps = taken(eng, f"O{i}")
                copied(tt(o_tmp.rearrange("p (u d) -> p u d", d=HD), ps[:, :].rearrange("p (u d) -> p u d", d=HD),
                          w8.unsqueeze(2).to_broadcast([128, 8, HD]), ALU.mult), f"O{i}")
                drained(eng, f"O{i}")
                link(tt(ynsa[:, i, :], o_tmp[:, 0:256], o_tmp[:, 256:512], ALU.add))
            for i in range(4):
                ps = taken(eng, f"Oc{i}")
                copied(tt(ynsa[:, i, :], ynsa[:, i, :], ps[:, 0:256], ALU.add), f"Oc{i}")
            drained(eng, "Oc3")
            eng.wait_ge(S["smp_o_moved"], 16)
            eng.sem_inc(S["yn_made"], 1)
            eng.wait_ge(S["yn_sq"], NTILE)
            ts(yss[0:NS, 4:5], yss[0:NS, 4:5], 1.0 / GW, EPS, ALU.mult, ALU.add)
            ts(yss[:, 0:4], yss[:, 0:4], 1.0 / GW, EPS, ALU.mult, ALU.add).then_inc(S["yn_ss"], 1)
            eng.wait_ge(S["yn_rs"], 2)
            for i in TILES:
                r = ROWS[i]
                ins = ts(ynsa[0:r, i, :], ynsa[0:r, i, :], yrs[0:r, i:i + 1], None, ALU.mult)
            ins.then_inc(S["yn_scaled"], 1)
            drained(eng, "N2")
            drained(eng, "Ns")
            link(eng.reciprocal(m[4], m[4]))
            link(eng.reciprocal(m[5][:, 0, :], m[5][:, 0, :]))
            for g, first in ((0, 0), (1, 2), (2, 6)):
                rs = m[4 + g // 2][:, g % 2, :]
                for j in range(2):
                    gain = params[:, P_OUT_G + first + j:P_OUT_G + first + j + 1]
                    ins = stt(yT[:, first + j, :], yT[:, first + j, :], gain, rs, ALU.mult, ALU.mult)
            link(ins)
            eng.sem_inc(S["yT_ready"], 1)
            eng.wait_ge(bank_full[bank_of["NT3"]], turn_of["NT3"] + 1)
            eng.memset(h2[:, 4, :], 0.0).then_inc(S["h2_zeroed"], 1)

            eng.wait_ge(S["x_reloaded"], 32)
            eng.wait_ge(S["gainf_loaded"], 16)

            def second_norm(n):
                i = TILES[n]
                r = ROWS[i]
                eng.wait_ge(S["x1_rs"], n + 1)
                stt(h2[0:r, i, :], x1[0:r, i, :], rstd[0:r, i:i + 1], gain_ffn[0:r, :], ALU.mult, ALU.mult).then_inc(S["h2_made"], 1)

            for n, i in enumerate(TILES):
                r = ROWS[i]
                for half in range(2):
                    ps = taken(eng, f"Y{i}.{half}")
                    copied(tt(x1[0:r, i, 512 * half:512 * half + 512], x1[0:r, i, 512 * half:512 * half + 512], ps[0:r, :], ALU.add), f"Y{i}.{half}")
                eng.wait_ge(S["x1_ss"], n + 1)
                ts(sumsq[0:r, i:i + 1], sumsq[0:r, i:i + 1], 1.0 / D, EPS, ALU.mult, ALU.add).then_inc(S["x1_asked"], 1)
                second_norm(n)

            eng.wait_ge(bank_full[bank_of["L"]], turn_of["L"] + 1)
            eng.memset(logits, 0.0)
            eng.memset(lg8, NEG)
            ps = taken(eng, "L")
            link(eng.memset(cnt, 0.0))
            eng.wait_ge(S["rtw_loaded"], 16 * 4)
            tt(logits[:, 0:4, :], ps[:, 0:144].rearrange("p (t e) -> p t e", t=4), rt_b.unsqueeze(1).to_broadcast([128, 4, 36]), ALU.add)
            copied(tt(logits[0:NS, 4, :], ps[0:NS, 144:180], rt_b[0:NS, :], ALU.add), "L")
            drained(eng, "L")
            link(eng.tensor_copy(lg8[:, :, 0:4], logits[:, :, 0:4]))
            for t in range(NTILE):
                ins = eng.max(mx8[:, t, :], lg8[:, t, :])
            link(ins)
            for t in range(NTILE):
                ins = eng.max_index(mi8[:, t, :].bitcast(U32), mx8[:, t, :], lg8[:, t, :])
            link(ins)
            tt(lex, logits[:, :, 0:4], mx8[:, :, 0:1].to_broadcast([128, 5, 4]), ALU.subtract).then_inc(S["rt_d"], 1)
            link(eng.tensor_copy(gsel, mi8[:, :, 0].bitcast(U32)))
            link(tt(eqg, grp_iota.unsqueeze(1).to_broadcast([128, 5, N_EXP]), gsel.unsqueeze(2).to_broadcast([128, 5, N_EXP]), ALU.is_equal))
            ts(eqt, eqg, -NEG, NEG, ALU.mult, ALU.add)
            link(tt(eqg, eqg, logits[:, :, 4:36], ALU.mult))
            link(tt(eqg, eqg, eqt, ALU.add))
            for t in range(NTILE):
                ins = eng.max(tv8[:, t, :], eqg[:, t, :])
            link(ins)
            for t in range(NTILE):
                ins = eng.max_index(ti8[:, t, :].bitcast(U32), tv8[:, t, :], eqg[:, t, :])
            link(ins)
            tt(tdx, tv8[:, :, 1], tv8[:, :, 0], ALU.subtract).then_inc(S["rt_d"], 1)
            link(eng.tensor_copy(tif, ti8[:, :, 0:2].bitcast(U32).rearrange("p t k -> p k t")))
            eng.memset(pass_no, 0.0)
            for k in range(2):
                ins = tt(oh[:, k], exp_iota.unsqueeze(1).to_broadcast([128, 5, N_EXP]), tif[:, k, :].unsqueeze(2).to_broadcast([128, 5, N_EXP]), ALU.is_equal)
            link(ins)
            for k in range(2):
                ins = tt(oh[:, k], oh[:, k], valid.unsqueeze(2).to_broadcast([128, 5, N_EXP]), ALU.mult)
            link(ins)
            link(tt(mask, oh[:, 0], oh[:, 1], ALU.add))
            eng.tensor_copy(mask_bf[:, :, :], mask).then_inc(S["mask_made"], 1)
            eng.wait_ge(S["rt_exp"], 2)
            link(eng.tensor_reduce(psel, lex, X_AXIS, ALU.add))
            link(ts(gate[:, 0, :], tdx, 1.0, None, ALU.add))
            link(tt(gate[:, 0, :], gate[:, 0, :], psel, ALU.mult))
            link(eng.reciprocal(gate[:, 0, :], gate[:, 0, :]))
            link(tt(gate[:, 1, :], gate[:, 0, :], tdx, ALU.mult))
            ps = taken(eng, "pos")
            copied(eng.tensor_copy(pos, ps[:, 0:160].rearrange("p (t e) -> p t e", t=5)), "pos")
            drained(eng, "pos")
            link(stt(posm[:, :, 0:N_EXP], pos, 1.0, mask, ALU.add, ALU.mult))
            link(ts(posm[:, :, 0:N_EXP], posm[:, :, 0:N_EXP], -1.0, None, ALU.add))
            for r in range(1, ROUNDS):
                ts(posm[:, :, N_EXP * r:N_EXP * r + N_EXP], posm[:, :, 0:N_EXP], float(-CAP * r), None, ALU.add)
            link(eng.memset(posm[:, :, ROUNDS * N_EXP:n_cols], -1.0))

            def make_onehot(n, b):
                tt(onehot[b], cap_iota.unsqueeze(1).to_broadcast([128, 5, CAP]), posm[:, :, bass.ds(n, 1)].to_broadcast([128, 5, CAP]), ALU.is_equal).then_inc(S["onehot_made"], 1)

            make_onehot(0, 0)
            make_onehot(1, 1)
            ps = taken(eng, "cnt")
            copied(eng.tensor_reduce(cnt[:, 0:1], ps[:, 0:32], X_AXIS, ALU.max), "cnt")
            drained(eng, "cnt")
            link(ts(flr[:, 0, :], thr, cnt[:, 0:1], None, ALU.is_lt))
            link(eng.tensor_reduce(cnt[:, 1:2], flr[:, 0, :], X_AXIS, ALU.add))
            link(ts(cnt[:, 1:2], cnt[:, 1:2], 1.0, None, ALU.add))
            eng.tensor_copy(n_rounds[:, :], cnt[:, 1:2]).then_inc(S["rounds_made"], 1)
            eng.wait_ge(S["rounds_made"], 1)
            link(tt(ohp, oh, pos.unsqueeze(1).to_broadcast([128, 2, 5, N_EXP]), ALU.mult))
            link(eng.tensor_reduce(pk, ohp, X_AXIS, ALU.add))
            pk10 = pk.rearrange("p k t -> p (k t)")
            link(tt(flr, pk10.unsqueeze(2).to_broadcast([128, 10, 8]), thr.unsqueeze(1).to_broadcast([128, 10, 8]), ALU.is_ge))
            link(eng.tensor_reduce(flk, flr, X_AXIS, ALU.add))
            link(stt(slot_f.rearrange("p k t -> p (k t)"), flk, float(-CAP), pk10, ALU.mult, ALU.add))
            link(stt(slot_f, tif, float(CAP), slot_f, ALU.mult, ALU.add))
            eng.tensor_copy(slot_u[:, :], slot_f.rearrange("p k t -> p (k t)")).then_inc(S["slots_made"], 1)

            rounds = eng.value_load(n_rounds[0:1, 0:1], min_val=1, max_val=ROUNDS)
            eng.sem_inc(S["y_tile_done"], NTILE)
            eng.sem_inc(S["round_combined"], 1)
            with eng.Fori(0, rounds) as r:
                with eng.Fori(0, N_EXP // 2) as i:
                    for b in range(2):
                        n = N_EXP * r + 2 * i + b
                        eng.wait_ge(S["silu_done"], n + 1)
                        tt(hid[b], silu[b], bank[2 + b][:, 256:512], ALU.mult).then_inc(S["hid_made"], 1)
                        eng.wait_ge(S["gathered"], n + 1)
                        make_onehot(n + 2, b)
                        eng.wait_ge(S["xt_turned"], n + 1)
                        eng.tensor_copy(hT[b], bank[4 + b][:, 0:256].rearrange("p (k s) -> p k s", k=2)).then_inc(S["hT_made"], 1)
                ts(gate_r.rearrange("p k t -> p (k t)"), flk, pass_no, None, ALU.is_equal)
                eng.tensor_copy(pass_next, pass_no).then_inc(S["pass_counted"], 1)
                eng.wait_ge(S["pass_counted"], 3 * r + 1)
                tt(gate_r, gate_r, gate, ALU.mult)
                ts(pass_no, pass_next, 1.0, None, ALU.add).then_inc(S["pass_counted"], 1)
                eng.wait_ge(S["pass_counted"], 3 * r + 2)
                for n, t in enumerate(TILES):
                    q = ROWS[t]
                    eng.wait_ge(rows_gathered[t], 32 * r + 32)
                    for k in range(2):
                        stt(x1[0:q, t, :], reg_a.t[0:q, (2 * t + k) * D:(2 * t + k + 1) * D], gate_r[0:q, k, t:t + 1], x1[0:q, t, :], ALU.mult, ALU.add).then_inc(S["half_added" if k == 0 else "y_tile_done"], 1)
                        if k == 0:
                            eng.wait_ge(S["half_added"], NTILE * r + n + 1)
                eng.wait_ge(S["y_tile_done"], NTILE * r + 2 * NTILE)
                eng.sem_inc(S["pass_counted"], 1)
                eng.sem_inc(S["round_combined"], 1)


_INS = ['x_prompt', 'x_sample', 'cache_nsa', 'state_win_kv', 'state_pool', 'state_rg_conv', 'state_rg_h', 'state_sc_conv',
        'page_table', 'norm_mix_g', 'w_in', 'pool_w', 'pool_scale', 'rg_conv_w', 'rg_conv_b', 'rg_w_a', 'rg_b_a', 'rg_w_x',
        'rg_b_x', 'rg_lambda', 'nsa_phi', 'nsa_phi_b', 'nsa_qk_g', 'sc_conv_w', 'sc_conv_b', 'mix_out_g', 'w_out',
        'norm_ffn_g', 'router_group_w', 'router_group_b', 'router_expert_w', 'router_expert_b', 'exp_w_gu', 'exp_w_down']
_OUTS = [('y_p', (1, SEQ, D)), ('y_s', (NS, 1, D)), ('rows_p', (1, 1, SEQ, 4, 2, HD)), ('rows_s', (1, NS, 1, 4, 2, HD)),
         ('win_p', (1, 1, SEQ, 2, 2, HD)), ('win_s', (1, NS, PAST, 2, 2, HD)), ('pool_p', (1, 1, POOL_KEEP, GW)),
         ('pool_s', (1, NS, POOL_KEEP, GW)), ('rgc_p', (1, 1, RG_KEEP, GW)), ('rgc_s', (1, NS, RG_KEEP, GW)),
         ('rgh_p', (1, 1, GW)), ('rgh_s', (1, NS, GW)), ('scc_p', (1, 1, SC_KEEP, GW)), ('scc_s', (1, NS, SC_KEEP, GW))]


def kernel(**inputs):
    import numpy as _np
    import concourse.bacc as _bacc
    from concourse.bass_utils import run_bass_kernel_spmd as _run

    nc = _bacc.Bacc("TRN2", target_bir_lowering=False, num_devices=1)
    arrays, ins, outs = {}, {}, {}
    for name in _INS:
        arr = _np.ascontiguousarray(inputs[name])
        arrays[f"in_{name}"] = arr
        ins[name] = nc.dram_tensor(f"in_{name}", arr.shape, mybir.dt.from_np(arr.dtype), kind="ExternalInput").ap()
    for name, shape in _OUTS:
        outs[name] = nc.dram_tensor(f"out_{name}", shape, F32, kind="ExternalOutput").ap()
    layer_kernel(nc, ins, outs)
    r = _run(nc, [arrays], core_ids=[0])
    return tuple(r.results[0][f"out_{name}"] for name, _ in _OUTS)
```

```python
import concourse.bass as bass
from concourse import mybir
from contextlib import ExitStack

F32 = mybir.dt.float32
BF16 = mybir.dt.bfloat16
I32 = mybir.dt.int32
U32 = mybir.dt.uint32
ALU = mybir.AluOpType
ACT = mybir.ActivationFunctionType
X_AXIS = mybir.AxisListType.X

D = 1024
SEQ = 512
NS = 8
T = SEQ + NS
HALF = T // 2
PAST = 256
PAGE = 128
GW = 256
HD = 64
NTILE = 5
KC = D // 128
POOL_KEEP = 15
RG_KEEP = 3
SC_KEEP = 2
N_CMP_P = SEQ // 16
N_CMP_S = PAST // 16
N_CHUNK = N_CMP_P + NS * N_CMP_S
N_GROUPS = 4
N_EXP = 32
DE = 512
CAP = 64
GU_PARTS = 4
ROUNDS = -(-T // CAP)
EPS = 1e-6
NEG = -1e30
OFF_U, OFF_X, OFF_R, OFF_Q = 0, 256, 512, 768
OFF_GATE, OFF_Z, OFF_BG, OFF_CG = 1792, 1804, 2060, 2316
W_CHUNKS = [OFF_Q, OFF_Q + 256, OFF_Q + 512, OFF_Q + 768, OFF_U, OFF_X, OFF_R, OFF_Z, OFF_CG, OFF_BG]
W_SLOTS = 4
W_LAST = 256 + 12
NORM_STEP = 8
N_PAIR = 16
TILES = [4, 0, 1, 2, 3]
PROJ_TILES = [0, 4, 1, 2, 3]
COMBINE_TILES = [0, 4, 1, 2, 3]
SAMPLES_AT = {1: (0,), 2: (1, 2), 3: (3, 4, 5), "end": (6, 7)}
ROWS = [128] * 4 + [NS]
COL = [0, 128, 256, 384, SEQ]

P_POOL_SCALE, P_CONV_W, P_CONV_B, P_BA, P_BX, P_LAM = 0, 2, 10, 12, 14, 16
P_SC_W, P_SC_B, P_OUT_G, P_PHI_B, P_QG, P_KCG, P_ROWS = 18, 24, 26, 34, 36, 37, 38


def psum_jobs():
    jobs, turn = [], [0]

    def take(name, bank=None):
        if bank is None:
            bank = turn[0] % 6
            turn[0] += 1
        jobs.append((name, bank))

    def feature(g):
        for part in ("00", "01", "10", "11"):
            take(f"F{g}{part}")

    take("xT4")
    for i in range(4):
        take(f"xTa{i}")
        take(f"xTb{i}")
    last = None
    for i in PROJ_TILES:
        take(f"A{i}")
        if i < 4:
            take(f"B{i}")
            take(f"C{i}")
        if i == 0:
            take("params")
            take("states")
        if last is not None:
            take(f"K{last}")
            if last < 4:
                take(f"R{last}")
        for b in SAMPLES_AT.get(i, ()):
            take(f"sR{b}")
            take(f"sK{b}")
        last = i
    take("K3")
    take("R3")
    for b in SAMPLES_AT["end"]:
        take(f"sR{b}")
        take(f"sK{b}")
    take("SS", 6)
    take("SW", 7)
    for n in ("CK0", "CK1", "CV0", "CV1"):
        take(n)
    feature("U")
    take("CN")
    feature("X")
    take("VT")
    take("cs")
    take("cp0")
    take("cp1")
    take("g32")
    feature("R")
    take("PT")
    take("pn")
    take("SO")
    feature("Z")
    take("RGs")
    for n in ("RA0", "RX0", "RA1", "RX1"):
        take(n)
    take("PBs")
    take("PB0")
    take("PB1")
    feature("C")
    feature("B")
    take("cT")
    for i in range(4):
        take(f"Oc{i}")
    for step in range(N_PAIR + 1):
        if step == NORM_STEP:
            for g in range(3):
                take(f"N{g}")
            take("Ns")
        for kv in range(2):
            if step < N_PAIR:
                take(f"S{2 * step + kv}")
        for kv in range(2):
            if step > 0:
                take(f"T{2 * step - 2 + kv}")
    for i in range(4):
        take(f"O{i}", 6 + i % 2)
    take("TLa")
    take("TLb")
    for i in TILES:
        take(f"NT{i}")
    last = None
    take("L", 7)
    for i in TILES:
        take(f"Y{i}.0")
        if i < 4:
            take(f"Y{i}.1")
        if last is not None:
            take(f"hTa{last}")
            take(f"hTb{last}")
        last = i
    take("hTa3")
    take("hTb3")
    take("pos")
    take("cnt", 6)
    return jobs


def layer_kernel(nc, a, o):
    jobs = psum_jobs()
    bank_of, turn_of, uses = {}, {}, [0] * 8
    for name, bank in jobs:
        bank_of[name], turn_of[name] = bank, uses[bank]
        uses[bank] += 1

    ctx = ExitStack()
    with ctx:
        def sb(name, shape, dt=F32):
            return ctx.enter_context(nc.sbuf_tensor(name, shape, dt))

        def sem(name):
            return ctx.enter_context(nc.semaphore(name))

        class Region:

            def __init__(self, name, floats):
                self.t, self.n, self.at = sb(name, [128, floats]), floats, 0

            def cut(self, floats, pattern=None, **dims):
                assert self.at + floats <= self.n, (self.at, floats, self.n)
                v = self.t[:, self.at:self.at + floats]
                self.at += floats
                return v.rearrange(pattern, **dims) if pattern else v

            def rewind(self, at=0):
                self.at = at

        reg_a = Region("reg_a", 12288)
        reg_b = Region("reg_b", 12288)
        reg_x = Region("reg_x", 5120)
        reg_h = Region("reg_h", 5120)
        reg_y = Region("reg_y", 4352)
        reg_w = Region("reg_w", 8288)
        reg_q = Region("reg_q", 2080)
        small = Region("small", 2240)

        gu_w = [r.t[:, 0:8192].rearrange("p (c n) -> p c n", c=8) for r in (reg_a, reg_b, reg_w)]
        down_w = [r.t[:, 8192:12288].rearrange("p (s c n) -> p s c n", s=2, c=2) for r in (reg_a, reg_b)]

        x_in = reg_x.cut(5120, "p (t d) -> p t d", t=5)
        xn = reg_h.cut(5120, "p (t d) -> p t d", t=5)
        xnT = reg_b.cut(8 * T, "p (c t) -> p c t", c=8)
        w_slot = [reg_w.cut(2048, "p (c n) -> p c n", c=8) for _ in range(W_SLOTS)]
        w_last = reg_w.t[:, 6144:6144 + 8 * W_LAST].rearrange("p (c n) -> p c n", c=8)
        reg_h.rewind()
        rows = reg_h.cut(2560, "p (t f) -> p t f", t=5)
        win = reg_h.cut(1280, "p (t f) -> p t f", t=5)
        ynsa = reg_h.cut(1280, "p (t f) -> p t f", t=5)
        qT = reg_q.cut(2 * T, "p (g t) -> p g t", g=2)
        kT = reg_q.cut(2 * T, "p (r t) -> p r t", r=2)
        raw = reg_x.t[:, :].rearrange("p (c t) -> p c t", c=2)
        gain_mix = reg_y.cut(D)
        par_rows = reg_y.cut(128)[0:P_ROWS]
        st_rows = reg_y.cut(GW)[0:48]
        st_pool = reg_y.cut(GW)[0:120]
        qn_buf = [reg_b.t[:, 4160 + 512 * k:4672 + 512 * k] for k in range(2)]
        sq_buf = [reg_b.t[:, 5184 + 512 * k:5696 + 512 * k] for k in range(2)]
        phi = reg_a.cut(4096, "p (c j h n) -> p c j h n", c=2, j=16, h=2)
        page_k = [reg_a.cut(768, "p (g f) -> p g f", g=2) for _ in range(2)]
        win_k = [reg_a.cut(256, "p (g f) -> p g f", g=2) for _ in range(2)]
        vs_cache = reg_a.cut(2048, "p (b g f) -> p b g f", b=NS, g=2)
        vw_cache = reg_a.cut(2048, "p (b g f) -> p b g f", b=NS, g=2)
        smp_kT = [reg_a.cut(514, "p (r t) -> p r t", r=2) for _ in range(2)]
        reg_b.at = 6208
        q_masked = reg_b.cut(NS * 32)
        p_masked = reg_b.cut(4 * NS * 32)
        smp_p = reg_b.cut(2 * 257, "p (r t) -> p r t", r=2)
        smp_pc = reg_b.cut(16)
        smp_pc3 = reg_b.cut(128, "p (b c) -> p b c", b=NS)
        smp_pcT = reg_b.cut(32)
        smp_diag = reg_b.cut(64, "p (r t) -> p r t", r=2)
        smp_new = reg_b.cut(64, "p (r t) -> p r t", r=2)
        smp_o = reg_b.cut(64)
        smp_o2 = reg_b.cut(64)
        kc_a = reg_b.cut(N_CHUNK)
        kcT = reg_b.cut(N_CHUNK)
        kc_sq = reg_b.cut(N_CHUNK)
        vcT = reg_b.cut(N_CHUNK)
        vc_smp = reg_b.cut(128)
        vc_blk = reg_b.cut(256)
        cmp_s = reg_b.cut(512, "p (u c) -> p u c", u=16)
        reg_x.rewind()
        u_ext = reg_x.cut(2 * (POOL_KEEP + SEQ), "p (j t) -> p j t", j=2)
        r_ext = reg_x.cut(2 * (RG_KEEP + SEQ), "p (j t) -> p j t", j=2)
        c_ext = reg_x.cut(2 * (SC_KEEP + SEQ), "p (j t) -> p j t", j=2)
        u_smp = reg_x.cut(16, "p (j t) -> p j t", j=2)
        r_smp = reg_x.cut(16, "p (j t) -> p j t", j=2)
        c_smp = reg_x.cut(16, "p (j t) -> p j t", j=2)
        z_buf = reg_x.cut(2 * T, "p (j t) -> p j t", j=2)
        pool_w = reg_a.t[:, 11904:12160].rearrange("p (j n) -> p j n", j=2)
        m = [reg_a.t[:, 1040 * k:1040 * (k + 1)].rearrange("p (j t) -> p j t", j=2) for k in (1, 2, 3, 4, 5, 6, 7, 0)]
        g_buf = m[7]
        reg_y.rewind()
        yT = reg_y.cut(8 * T, "p (c t) -> p c t", c=8)
        tails = reg_y.cut(8 * 24, "p (c t) -> p c t", c=8)
        p_buf = [reg_b.t[:, 4160 + 512 * k:4672 + 512 * k] for k in range(4)]
        pT_buf = [reg_a.t[:, 8320 + 512 * k:8832 + 512 * k] for k in range(4)]
        o_tmp = reg_a.t[:, 10368:10880]
        tail_rows = reg_a.t[:, 10880:11904]
        w_out = reg_w.t[:, 0:8192].rearrange("p (c n) -> p c n", c=8)
        x1 = x_in
        y_smp = xn[0:NS, 4, :]
        h2 = xn
        sq_at = [7280, 7536, 7792, 8048, 0]
        h2T = reg_q.t[:, 0:1024].rearrange("p (c t) -> p c t", c=8)
        gain_ffn = reg_q.t[:, 1024:2048]
        reg_y.rewind()
        xe = [reg_y.cut(512, "p (j s n) -> p j s n", j=4, s=2) for _ in range(2)]
        hT = [reg_y.cut(256, "p (c s) -> p c s", c=2) for _ in range(2)]
        silu = [reg_y.cut(256) for _ in range(2)]
        hid = [reg_y.cut(256) for _ in range(2)]
        scratch_end = reg_y.at
        x_tok = reg_y.cut(512)
        onehot = [reg_y.cut(320, "p (t s) -> p t s", t=5) for _ in range(2)]
        reg_q.rewind()
        y_out = [reg_y.cut(512), reg_q.cut(512)]
        n_cols = ROUNDS * N_EXP + 2
        posm = reg_q.cut(5 * n_cols, "p (t n) -> p t n", t=5)
        flk = reg_q.cut(10)
        gate = reg_q.cut(10, "p (k t) -> p k t", k=2)
        gate_r = reg_q.cut(10, "p (k t) -> p k t", k=2)
        pass_no = reg_q.cut(1)
        pass_next = reg_q.cut(1)
        reg_y.rewind()

        def rt(floats, pattern=None, **dims):
            v = reg_y.cut(floats, pattern, **dims)
            assert reg_y.at <= scratch_end
            return v

        logits = rt(5 * 36, "p (t e) -> p t e", t=5)
        lg8 = rt(40, "p (t e) -> p t e", t=5)
        mx8 = rt(40, "p (t e) -> p t e", t=5)
        tv8 = rt(40, "p (t e) -> p t e", t=5)
        mi8 = rt(40, "p (t e) -> p t e", t=5)
        ti8 = rt(40, "p (t e) -> p t e", t=5)
        gsel = rt(5)
        lex = rt(20, "p (t e) -> p t e", t=5)
        psel = rt(5)
        eqg = rt(160, "p (t e) -> p t e", t=5)
        eqt = rt(160, "p (t e) -> p t e", t=5)
        tif = rt(10, "p (k t) -> p k t", k=2)
        tdx = rt(5)
        oh = rt(320, "p (k t e) -> p k t e", k=2, t=5)
        mask = rt(160, "p (t e) -> p t e", t=5)
        pos = rt(160, "p (t e) -> p t e", t=5)
        ohp = rt(320, "p (k t e) -> p k t e", k=2, t=5)
        pk = rt(10, "p (k t) -> p k t", k=2)
        flr = rt(80, "p (k e) -> p k e", k=10)
        slot_f = rt(10, "p (k t) -> p k t", k=2)
        cnt = rt(8)
        mask_bf = sb("mask_bf", [128, 5, N_EXP], BF16)

        ident = small.cut(128)
        ones = small.cut(128)
        block_ones = small.cut(128)
        cmp_mask = small.cut(128, "p (t c) -> p t c", t=4)
        cap_iota = small.cut(CAP)
        exp_iota = small.cut(N_EXP)
        grp_iota = small.cut(N_EXP)
        thr = small.cut(8)
        valid = small.cut(5)
        minus_half = small.cut(160)
        params = small.cut(P_ROWS)
        half_b = small.cut(4)
        qg_scaled = small.cut(1)
        sp = small.cut(12, "p (k j) -> p k j", j=2)
        row_of_sample = small.cut(NS)
        sample_of_row = small.cut(32)
        head_of_row = small.cut(4)
        hr3 = small.cut(32, "p (b h) -> p b h", b=NS)
        kv_of_row = small.cut(2)
        inv_cnt = small.cut(32, "p (j t) -> p j t", j=2)
        inv_win = small.cut(2)
        eps_col = small.cut(1)
        rt_w = small.cut(KC * 36, "p (c e) -> p c e", c=KC)
        rt_b = small.cut(36)
        kg = small.cut(128, "p (r d) -> p r d", r=2)
        sumsq = small.cut(8)
        rstd = small.cut(8)
        hss = small.cut(40, "p (t h) -> p t h", t=5)
        hrs = small.cut(40, "p (t h) -> p t h", t=5)
        gates = small.cut(60, "p (t h) -> p t h", t=5)
        g32 = small.cut(12)
        g32m = small.cut(12)
        g3 = small.cut(3)
        smx = small.cut(3)
        ssum = small.cut(3)
        att_mx = small.cut(32)
        att_sum = small.cut(32)
        att_w = small.cut(32)
        cmp_mx = small.cut(16)
        cmp_sum = small.cut(16)
        cmp_w = small.cut(16)
        yss = small.cut(8)
        yrs = small.cut(8)
        n_rounds = sb("n_rounds", [128, 1], I32)
        slot_u = sb("slot_u", [128, 10], U32)
        pages = sb("pages", [1, 2 * NS], I32)
        ident_bf = sb("ident_bf", [128, 128], BF16)
        causal_bf = sb("causal_bf", [128, 128], BF16)
        before_bf = sb("before_bf", [128, 128], BF16)
        ones_bf = sb("ones_bf", [128, 128], BF16)
        rg_w = sb("rg_w", [128, 4, 128])
        states = sb("states", [128, 336])
        st_misc = [states[:, 48 * j:48 * j + 48] for j in range(2)]
        st_poolT = [states[:, 96 + 120 * j:216 + 120 * j].rearrange("p (b k) -> p b k", k=POOL_KEEP) for j in range(2)]
        bank = [ctx.enter_context(nc.psum_tensor(f"bank{i}", [128, 512], F32)) for i in range(8)]
        y_dram = nc.dram_tensor("expert_rows", [N_EXP * CAP, D], F32, kind="Internal").ap()

        bank_full = [sem(f"bank_full{i}") for i in range(8)]
        bank_read = [sem(f"bank_read{i}") for i in range(8)]
        names = """par_loaded gain_loaded gainf_loaded states_loaded blocks_loaded phi_loaded pages_loaded
            kg_loaded wout_loaded rtw_loaded
            vcache_loaded consts_made vector_chain pool_chain
            xsq_done rstd_asked rstd_made xn_made hss_made hrs_made qk_normed gates_tanh gates_raw
            rows_stored states_stored params_made sp_exp_asked sp_exp sample_scores q_masked_made
            kc_copied kc_sum kc_made smax_made sp_scaled smp_o_made smp_o_moved
            u_copied pool_pad pool_d f_copied conv_made rg_t2 rg_sqrt h_made sc_z sc_b
            att_max att_pv cmp_max cmp_exp cmp_scaled yn_made yn_ss yn_rs yn_scaled sq_made nrm_made tails_made
            tails_stored x1_ss x1_asked x1_rs h2_made x_reloaded yT_ready routed h2_zeroed kc_squared yn_sq
            rt_d rt_exp mask_made rounds_made slots_made
            gathered x_tok_made xe_turned xe_made gu_done silu_done hid_made xt_turned hT_made down_done y_copied
            onehot_made moe_stored round_combined pass_counted half_added y_tile_done y_stored_out gather_begun ident_made blocks_zeroed x1_smp""".split()
        S = {n: sem(n) for n in names}
        x_loaded = [sem(f"x_loaded{i}") for i in range(NTILE)]
        w_loaded = [sem(f"w_loaded{i}") for i in range(W_SLOTS)]
        smp_loaded = [sem(f"smp_loaded{i}") for i in range(2)]
        gu_loaded = [[sem(f"gu_loaded{i}_{part}") for part in range(GU_PARTS)] for i in range(3)]
        gu_part_done = [sem(f"gu_part_done{part}") for part in range(GU_PARTS - 1)] + [S["gu_done"]]
        down_loaded = [sem(f"down_loaded{i}") for i in range(2)]
        y_stored = [sem(f"y_stored{i}") for i in range(2)]
        rows_gathered = [[sem(f"rows_gathered{k}_{i}") for i in range(NTILE)] for k in range(2)]

        def claim(eng, job):
            if turn_of[job]:
                eng.wait_ge(bank_read[bank_of[job]], turn_of[job])
            return bank[bank_of[job]]

        def filled(ins, job):
            ins.then_inc(bank_full[bank_of[job]], 1)

        def taken(eng, job):
            eng.wait_ge(bank_full[bank_of[job]], turn_of[job] + 1)
            return bank[bank_of[job]]

        def copied(ins, job):
            ins.then_inc(bank_read[bank_of[job]], 1)

        def drained(eng, job):
            eng.wait_ge(bank_read[bank_of[job]], turn_of[job] + 1)

        def pv_done(eng, n):
            if n % 8 == 7:
                eng.wait_ge(bank_full[bank_of[f"O{n // 8}"]], turn_of[f"O{n // 8}"] + 1)
            else:
                eng.wait_ge(S["att_pv"], 7 * (n // 8) + n % 8 + 1)

        def chain_of(eng, s):
            count = [0]

            def link(ins):
                count[0] += 1
                ins.then_inc(S[s], 1)
                eng.wait_ge(S[s], count[0])
            return link

        cache = a["cache_nsa"].rearrange("l n p c k d -> (l n p) (c k d)")
        win_state = a["state_win_kv"].rearrange("l b t c k d -> (l b) t (c k d)")
        w_in = a["w_in"].rearrange("l (c p) n -> p (l c) n", p=128)
        gu_dram = a["exp_w_gu"].rearrange("l e (p c) n -> (l e p) c n", c=8)
        down_dram = a["exp_w_down"].rearrange("l e (s p c) n -> (l e) p s c n", s=2, c=2)
        x_dram = a["x_prompt"].rearrange("b (t p) d -> p (b t) d", p=128)
        xs_dram = a["x_sample"].rearrange("b t d -> (b t) d")
        PAR_DMAS = 13

        block = ctx.enter_context(nc.Block())

        @block.sync
        def _(sp_eng):
            eng = sp_eng
            eng.dma_start(x_in[0:NS, 4, :], xs_dram).then_inc(x_loaded[4], 16)
            eng.dma_start(gain_mix, a["norm_mix_g"].rearrange("l d -> (l d)").partition_broadcast(128)).then_inc(S["gain_loaded"], 16)
            for i in range(4):
                eng.dma_start(x_in[:, i, :], x_dram[:, i, :]).then_inc(x_loaded[i], 16)
            for n, off in enumerate(W_CHUNKS[:W_SLOTS]):
                width = W_LAST if n == W_SLOTS - 1 else 256
                eng.dma_start(w_last if n == W_SLOTS - 1 else w_slot[n], w_in[:, :, off:off + width]).then_inc(w_loaded[n], 16)
            eng.dma_start(par_rows[P_POOL_SCALE:P_POOL_SCALE + 2, :], a["pool_scale"].rearrange("l (j p) -> (l j) p", p=128)).then_inc(S["par_loaded"], 16)
            eng.dma_start(par_rows[P_CONV_W:P_CONV_W + 8, :], a["rg_conv_w"].rearrange("l k (j p) -> (l k j) p", p=128)).then_inc(S["par_loaded"], 16)
            for name, at in (("rg_conv_b", P_CONV_B), ("rg_b_a", P_BA), ("rg_b_x", P_BX), ("rg_lambda", P_LAM), ("sc_conv_b", P_SC_B)):
                eng.dma_start(par_rows[at:at + 2, :], a[name].rearrange("l (j p) -> (l j) p", p=128)).then_inc(S["par_loaded"], 16)
            eng.dma_start(par_rows[P_SC_W:P_SC_W + 6, :], a["sc_conv_w"].rearrange("l k (j p) -> (l k j) p", p=128)).then_inc(S["par_loaded"], 16)
            eng.dma_start(par_rows[P_OUT_G:P_OUT_G + 8, :], a["mix_out_g"].rearrange("l (j p) -> (l j) p", p=128)).then_inc(S["par_loaded"], 16)
            for half in range(2):
                lo = 64 * half
                eng.dma_start(par_rows[P_PHI_B:P_PHI_B + 2, lo:lo + 64], a["nsa_phi_b"].rearrange("l c d -> (l c) d")).then_inc(S["par_loaded"], 16)
                eng.dma_start(par_rows[P_QG:P_QG + 2, lo:lo + 64], a["nsa_qk_g"].rearrange("l c d -> (l c) d")[0:2]).then_inc(S["par_loaded"], 16)
            eng.dma_start(st_rows[0:24, :], a["state_rg_conv"].rearrange("l b k c -> (l b k) c")).then_inc(S["states_loaded"], 16)
            eng.dma_start(st_rows[24:40, :], a["state_sc_conv"].rearrange("l b k c -> (l b k) c")).then_inc(S["states_loaded"], 16)
            eng.dma_start(st_rows[40:48, :], a["state_rg_h"].rearrange("l b c -> (l b) c")).then_inc(S["states_loaded"], 16)
            eng.dma_start(st_pool[:, :], a["state_pool"].rearrange("l b k c -> (l b k) c")).then_inc(S["states_loaded"], 16)
            eng.dma_start(kg[:, :, :], a["nsa_qk_g"].rearrange("l r d -> (l r) d")[2:4].partition_broadcast(128)).then_inc(S["kg_loaded"], 16)
            eng.dma_start(pages[:, :], a["page_table"].rearrange("b n -> (b n)").unsqueeze(0)).then_inc(S["pages_loaded"], 16)
            for c in range(2):
                for kv in range(2):
                    for half in range(2):
                        src = a["nsa_phi"].rearrange("l c (h j d) n -> d (l c h) j n", h=2, d=HD)[:, 2 * c + half]
                        eng.dma_start(phi[64 * kv:64 * kv + 64, c, :, kv ^ half, :], src).then_inc(S["phi_loaded"], 16)
            eng.wait_ge(S["blocks_zeroed"], 1)
            for k in range(4):
                lo, j = 64 * (k % 2), k // 2
                eng.dma_start(pool_w[lo:lo + 64, j, lo:lo + 64], a["pool_w"][0, k]).then_inc(S["blocks_loaded"], 16)
                eng.dma_start(rg_w[lo:lo + 64, j, lo:lo + 64], a["rg_w_a"][0, k]).then_inc(S["blocks_loaded"], 16)
                eng.dma_start(rg_w[lo:lo + 64, 2 + j, lo:lo + 64], a["rg_w_x"][0, k]).then_inc(S["blocks_loaded"], 16)
            eng.wait_ge(S["pages_loaded"], 16)
            for b in range(NS):
                if b >= 2:
                    eng.wait_ge(bank_full[bank_of[f"sK{b - 2}"]], turn_of[f"sK{b - 2}"] + 1)
                for g in range(2):
                    page = eng.value_load(pages[0:1, 2 * b + g:2 * b + g + 1], min_val=0, max_val=cache.shape[0] // PAGE - 1)
                    rows_of_page = cache[bass.ds(page * PAGE, PAGE)]
                    eng.dma_start(page_k[b % 2][:, g, :], rows_of_page[:, 0:384]).then_inc(smp_loaded[b % 2], 16)
                    eng.dma_start(vs_cache[:, b, g, :], rows_of_page[:, 384:512]).then_inc(S["vcache_loaded"], 16)
                eng.dma_start(win_k[b % 2][:, :, :], win_state[b].rearrange("(g p) f -> p g f", p=128)[:, :, 0:128]).then_inc(smp_loaded[b % 2], 16)
            eng.dma_start(vw_cache[:, :, 0, :], win_state[:, 0:128, 128:256].rearrange("b p f -> p b f")).then_inc(S["vcache_loaded"], 16)
            eng.dma_start(vw_cache[:, :, 1, :], win_state[:, 128:256, 128:256].rearrange("b p f -> p b f")).then_inc(S["vcache_loaded"], 16)
            readers = ["A3", "A3", "B3", "C3", "FU11", "FX11"]
            for n in range(W_SLOTS, len(W_CHUNKS)):
                reader = readers[n - W_SLOTS]
                eng.wait_ge(bank_full[bank_of[reader]], turn_of[reader] + 1)
                off = W_CHUNKS[n]
                eng.dma_start(w_slot[n % W_SLOTS], w_in[:, :, off:off + 256]).then_inc(w_loaded[n % W_SLOTS], 16)
            eng.dma_start(rt_w[:, :, 0:4], a["router_group_w"].rearrange("l (p c) n -> p (l c) n", p=128)).then_inc(S["rtw_loaded"], 16)
            eng.dma_start(rt_w[:, :, 4:36], a["router_expert_w"].rearrange("l (p c) n -> p (l c) n", p=128)).then_inc(S["rtw_loaded"], 16)
            eng.dma_start(rt_b[:, 0:4], a["router_group_b"].rearrange("l d -> (l d)").partition_broadcast(128)).then_inc(S["rtw_loaded"], 16)
            eng.dma_start(rt_b[:, 4:36], a["router_expert_b"].rearrange("l d -> (l d)").partition_broadcast(128)).then_inc(S["rtw_loaded"], 16)
            eng.wait_ge(S["smp_o_made"], 1)
            for h in range(4):
                eng.dma_start(ynsa[0:NS, 4, HD * h:HD * h + HD], smp_o2[h:32:4, :]).then_inc(S["smp_o_moved"], 16)
            eng.wait_ge(S["qk_normed"], NTILE)
            eng.dma_start(o["rows_p"].rearrange("l b (t p) c k d -> p (l b t) (c k d)", p=128), rows[:, 0:4, :]).then_inc(S["rows_stored"], 16)
            eng.dma_start(o["rows_s"].rearrange("l b t c k d -> (l b t) (c k d)"), rows[0:NS, 4, :]).then_inc(S["rows_stored"], 16)
            eng.dma_start(o["win_p"].rearrange("l b (t p) c k d -> p (l b t) (c k d)", p=128), win[:, 0:4, :]).then_inc(S["rows_stored"], 16)
            eng.dma_start(o["win_s"].rearrange("l b t c k d -> (l b) t (c k d)")[:, PAST - 1, :], win[0:NS, 4, :]).then_inc(S["rows_stored"], 16)
            eng.wait_ge(bank_full[bank_of["FB11"]], turn_of["FB11"] + 1)
            eng.dma_start(w_out, a["w_out"].rearrange("l (c p) n -> p (l c) n", p=128)).then_inc(S["wout_loaded"], 16)
            eng.wait_ge(S["sc_b"], 1)
            eng.wait_ge(S["tails_made"], 1)
            eng.dma_start(x1[0:NS, 4, :], xs_dram).then_inc(S["x_reloaded"], 16)
            eng.dma_start(x1[:, 0:4, :], x_dram).then_inc(S["x_reloaded"], 16)

            def load_gu(e, g, free=None):
                width = KC // GU_PARTS
                for part in range(GU_PARTS):
                    lo = part * width
                    if free is not None:
                        eng.wait_ge(gu_part_done[part], free)
                    eng.dma_start(gu_w[g][:, lo:lo + width, :], gu_dram[bass.ds(e * 128, 128), lo:lo + width, :]).then_inc(gu_loaded[g][part], 16)

            def load_down(e, b, free=None):
                if free is not None:
                    eng.wait_ge(S["down_done"], free)
                eng.dma_start(down_w[b], down_dram[bass.ds(e, 1)].rearrange("e p s c n -> (e p) s c n")).then_inc(down_loaded[b], 16)

            def load_experts(first):
                for e, g in ((3, 0), (4, 1), (5, 2), (6, 0), (7, 1)):
                    load_gu(e, g, first + e - 2)
                    load_down(e - 1, (e - 1) % 2, first + e - 2)
                with eng.Fori(0, (N_EXP - 8) // 2) as i:
                    for k in range(2):
                        e = 2 * i + 7 + k
                        load_down(e, 1 - k, first + e - 1)
                        load_gu(e + 1, k, first + e)
                load_down(N_EXP - 1, 1, first + N_EXP - 2)

            eng.wait_ge(S["yn_sq"], NTILE)
            eng.wait_ge(S["tails_stored"], 16 * 8)
            eng.wait_ge(S["yT_ready"], 1)
            eng.dma_start(gain_ffn, a["norm_ffn_g"].rearrange("l d -> (l d)").partition_broadcast(128)).then_inc(S["gainf_loaded"], 16)
            for e in range(2):
                load_gu(e, e)
                load_down(e, e)
            eng.wait_ge(bank_full[bank_of["Y3.1"]], turn_of["Y3.1"] + 1)
            load_gu(2, 2)
            load_experts(0)
            eng.wait_ge(S["rounds_made"], 1)
            rounds = eng.value_load(n_rounds[0:1, 0:1], min_val=1, max_val=ROUNDS)
            with eng.If(rounds > 1):
                with eng.Fori(1, rounds) as r:
                    eng.wait_ge(S["round_combined"], r + 1)
                    for e in range(2):
                        load_gu(e, e)
                        load_down(e, e)
                    load_gu(2, 2)
                    load_experts(N_EXP * r)
            for n in range(NTILE):
                i = COMBINE_TILES[n]
                eng.wait_ge(S["y_tile_done"], rounds * NTILE + n + 1)
                if i == 4:
                    eng.dma_start(o["y_s"].rearrange("b t d -> (b t) d"), x1[0:NS, 4, :]).then_inc(S["y_stored_out"], 16)
                else:
                    eng.dma_start(o["y_p"].rearrange("b (t p) d -> p (b t) d", p=128)[:, i, :], x1[:, i, :]).then_inc(S["y_stored_out"], 16)
            eng.wait_ge(S["y_stored_out"], 16 * NTILE)
            eng.wait_ge(S["rows_stored"], 16 * 4)
            eng.wait_ge(S["states_stored"], 16 * 4)
            eng.wait_ge(S["tails_stored"], 16 * 8)

        @block.gpsimd
        def _(eng):
            link = chain_of(eng, "pool_chain")
            link(eng.memset(ident, 0.0))
            eng.affine_select(out=ident, in_=ident, compare_op=ALU.not_equal, fill=1.0, base=0, pattern=[[-1, 128]], channel_multiplier=1).then_inc(S["ident_made"], 1)
            eng.memset(ones, 1.0)
            eng.memset(ones_bf[:, :], 1.0)
            eng.memset(ident_bf[:, :], 0.0)
            eng.memset(causal_bf[:, :], 0.0)
            eng.memset(before_bf[:, :], 1.0)
            eng.memset(minus_half, -0.5)
            eng.memset(eps_col, EPS)
            link(eng.memset(pool_w[:, :, :], 0.0))
            eng.affine_select(out=ident_bf[:, :], in_=ident_bf[:, :], compare_op=ALU.not_equal, fill=1.0, base=0, pattern=[[-1, 128]], channel_multiplier=1)
            link(eng.memset(rg_w[:, :, :], 0.0))
            eng.sem_inc(S["blocks_zeroed"], 1)
            eng.affine_select(out=causal_bf[:, :], in_=causal_bf[:, :], compare_op=ALU.is_ge, fill=NEG, base=0, pattern=[[-1, 128]], channel_multiplier=1)
            eng.affine_select(out=before_bf[:, :], in_=before_bf[:, :], compare_op=ALU.is_gt, fill=0.0, base=0, pattern=[[1, 128]], channel_multiplier=-1)
            link(eng.memset(block_ones, 1.0))
            eng.affine_select(out=block_ones[:, 0:64], in_=block_ones[:, 0:64], compare_op=ALU.is_ge, fill=0.0, base=63, pattern=[[0, 64]], channel_multiplier=-1)
            eng.affine_select(out=block_ones[:, 64:128], in_=block_ones[:, 64:128], compare_op=ALU.is_ge, fill=0.0, base=-64, pattern=[[0, 64]], channel_multiplier=1)
            eng.memset(cmp_mask, 0.0)
            eng.memset(valid, 1.0)
            eng.memset(row_of_sample[0:32, :], 1.0)
            eng.memset(sample_of_row[0:8, :], 1.0)
            eng.memset(q_masked, 0.0)
            eng.memset(p_masked, 0.0)
            eng.memset(vc_blk, 0.0)
            eng.memset(hr3[0:32], 0.0)
            eng.iota(cap_iota, pattern=[[1, CAP]], base=0, channel_multiplier=0, allow_small_or_imprecise_dtypes=True)
            eng.iota(exp_iota, pattern=[[1, N_EXP]], base=0, channel_multiplier=0, allow_small_or_imprecise_dtypes=True)
            eng.iota(grp_iota, pattern=[[1, N_GROUPS], [0, N_EXP // N_GROUPS]], base=0, channel_multiplier=0, allow_small_or_imprecise_dtypes=True)
            eng.iota(thr, pattern=[[CAP, 8]], base=CAP, channel_multiplier=0, allow_small_or_imprecise_dtypes=True)
            link(eng.iota(inv_cnt, pattern=[[0, 2], [1, 16]], base=1, channel_multiplier=0, allow_small_or_imprecise_dtypes=True))
            eng.affine_select(out=cmp_mask, in_=cmp_mask, compare_op=ALU.is_ge, fill=NEG, base=-31, pattern=[[128, 4], [-16, 32]], channel_multiplier=1)
            eng.affine_select(out=valid, in_=valid, compare_op=ALU.is_ge, fill=0.0, base=SEQ + NS - 1, pattern=[[-128, 5]], channel_multiplier=-1)
            link(eng.affine_select(out=hr3[0:32], in_=hr3[0:32], compare_op=ALU.not_equal, fill=1.0, base=0, pattern=[[-4, NS], [-1, 4]], channel_multiplier=1))
            link(eng.affine_select(out=row_of_sample[0:32, :], in_=row_of_sample[0:32, :], compare_op=ALU.is_ge, fill=0.0, base=0, pattern=[[-4, NS]], channel_multiplier=1))
            link(eng.affine_select(out=row_of_sample[0:32, :], in_=row_of_sample[0:32, :], compare_op=ALU.is_ge, fill=0.0, base=3, pattern=[[4, NS]], channel_multiplier=-1))
            link(eng.affine_select(out=sample_of_row[0:8, :], in_=sample_of_row[0:8, :], compare_op=ALU.is_ge, fill=0.0, base=0, pattern=[[1, 32]], channel_multiplier=-4))
            link(eng.affine_select(out=sample_of_row[0:8, :], in_=sample_of_row[0:8, :], compare_op=ALU.is_ge, fill=0.0, base=3, pattern=[[-1, 32]], channel_multiplier=4))
            eng.sem_inc(S["consts_made"], 1)

            def power(out, in_, s_ask, asked, s_done):
                eng.wait_ge(S[s_ask], asked)
                eng.tensor_tensor(out, in_, minus_half[0:out.shape[0], 0:out.shape[-1]], ALU.pow).then_inc(S[s_done], 1)

            for n, i in enumerate(TILES):
                power(rstd[0:ROWS[i], i:i + 1], sumsq[0:ROWS[i], i:i + 1], "rstd_asked", n + 1, "rstd_made")
            for n, i in enumerate(PROJ_TILES):
                power(hrs[0:ROWS[i], i, :], hss[0:ROWS[i], i, :], "hss_made", n + 1, "hrs_made")
            eng.wait_ge(S["u_copied"], 2)
            eng.wait_ge(S["smp_o_made"], 1)
            E = POOL_KEEP + SEQ
            s2, s4, s8, d = m[0], m[6], m[2], m[3]
            link(eng.tensor_tensor(s2[:, 0, 0:SEQ], u_ext[:, 0, 15:E], u_ext[:, 0, 14:E - 1], ALU.add))
            link(eng.tensor_copy(s4[64:128, 0, 0:SEQ], s2[64:128, 0, 0:SEQ]))
            link(eng.tensor_tensor(s4[64:128, 0, 2:SEQ], s2[64:128, 0, 2:SEQ], s2[64:128, 0, 0:SEQ - 2], ALU.add))
            sums = [(0, 0, s2), (64, 0, s4), (0, 1, s8), (64, 1, d)]
            for lo, j, s in sums:
                hi = lo + 64
                if (lo, j) == (0, 1):
                    eng.wait_ge(S["pool_pad"], 1)
                link(eng.tensor_tensor(m[2][lo:hi, 0, 16 * j:16 * j + 16], s[lo:hi, j, 0:16], inv_cnt[lo:hi, j, :], ALU.mult))
                link(eng.tensor_scalar(d[lo:hi, j, 16:SEQ], s[lo:hi, j, 16:SEQ], inv_win[lo:hi, j:j + 1], None, ALU.mult))
                link(eng.tensor_copy(d[lo:hi, j, 0:16], m[2][lo:hi, 0, 16 * j:16 * j + 16]))
            link(eng.tensor_tensor(d[:, :, 0:SEQ], d[:, :, 0:SEQ], u_ext[:, :, 15:E], ALU.subtract))
            eng.tensor_tensor(d[:, :, SEQ:T], d[:, :, SEQ:T], u_smp[:, :, :], ALU.subtract).then_inc(S["pool_d"], 1)
            eng.tensor_copy(tails[:, 0:2, 0:16], u_ext[:, :, E - 16:E])
            eng.tensor_copy(tails[:, 0:2, 16:24], u_smp[:, :, :])
            eng.wait_ge(S["f_copied"], 1)
            eng.tensor_copy(tails[:, 2:4, 0:16], r_ext[:, :, RG_KEEP + SEQ - 16:RG_KEEP + SEQ])
            eng.tensor_copy(tails[:, 2:4, 16:24], r_smp[:, :, :])
            eng.wait_ge(S["sc_z"], 1)
            eng.tensor_copy(tails[:, 4:6, 0:16], c_ext[:, :, SC_KEEP + SEQ - 16:SC_KEEP + SEQ])
            eng.tensor_copy(tails[:, 4:6, 16:24], c_smp[:, :, :])
            eng.wait_ge(S["h_made"], 1)
            eng.tensor_copy(tails[:, 6:8, :], m[3][:, :, T - 24:T]).then_inc(S["tails_made"], 1)
            for g, first in ((0, 0), (1, 2), (2, 6)):
                if g == 0:
                    drained(eng, "PBs")
                    eng.wait_ge(S["h_made"], 2)
                if g == 2:
                    eng.wait_ge(S["sc_b"], 1)
                y = yT[:, first:first + 2, :]
                eng.tensor_tensor(m[g], y, y, ALU.mult).then_inc(S["sq_made"], 1)
            power(yrs[:, 0:3], yss[:, 0:3], "yn_ss", 1, "yn_rs")
            power(yrs[0:NS, 4:5], yss[0:NS, 4:5], "yn_ss", 1, "yn_rs")
            power(yrs[:, 3:4], yss[:, 3:4], "yn_ss", 2, "yn_rs")
            for n, i in enumerate(TILES):
                power(rstd[0:ROWS[i], i:i + 1], sumsq[0:ROWS[i], i:i + 1], "x1_asked", n + 1, "x1_rs")
            eng.wait_ge(S["slots_made"], 1)
            rounds = eng.value_load(n_rounds[0:1, 0:1], min_val=1, max_val=ROUNDS)
            with eng.Fori(0, rounds) as r:
                eng.wait_ge(S["moe_stored"], r + 1)
                eng.sem_inc(S["gather_begun"], 1)
                for i in COMBINE_TILES:
                    for k in range(2):
                        dst = reg_a.t[0:ROWS[i], (2 * i + k) * D:(2 * i + k + 1) * D]
                        eng.indirect_dma_start(dst, None, y_dram[:, :], bass.IndirectOffsetOnAxis(ap=slot_u[0:ROWS[i], 5 * k + i:5 * k + i + 1], axis=0)).then_inc(rows_gathered[k][i], 16)

        @block.scalar
        def _(eng):

            def copy(out, in_):
                return eng.activation(out, in_, ACT.Copy)

            for i in TILES:
                eng.wait_ge(x_loaded[i], 16)
                eng.activation(xn[0:ROWS[i], i, :], x_in[0:ROWS[i], i, :], ACT.Square, accum_out=sumsq[0:ROWS[i], i:i + 1]).then_inc(S["xsq_done"], 1)
            ps = taken(eng, "xT4")
            copied(copy(xnT[:, :, SEQ:T], ps[:, 0:64].rearrange("p (c t) -> p c t", c=8)), "xT4")
            for i in range(4):
                ps = taken(eng, f"xTa{i}")
                copied(copy(xnT[:, 0:4, COL[i]:COL[i] + 128], ps[:, :].rearrange("p (c t) -> p c t", c=4)), f"xTa{i}")

            def kv_rows(n, i):
                r = ROWS[i]
                if n == 0:
                    eng.wait_ge(bank_full[bank_of["xTb3"]], turn_of["xTb3"] + 1)
                if n >= 2:
                    eng.wait_ge(bank_full[bank_of[f"K{PROJ_TILES[n - 2]}"]], turn_of[f"K{PROJ_TILES[n - 2]}"] + 1)
                ps = taken(eng, f"A{i}")
                if i == 4:
                    copy(qn_buf[n % 2][0:NS, 0:256], ps[0:NS, 0:256])
                    copy(rows[0:NS, 4, 0:256], ps[32:32 + NS, 0:256])
                    copy(rows[0:NS, 4, 256:512], ps[64:64 + NS, 0:256])
                    copy(gates[0:NS, 4, :], ps[96:96 + NS, 256:W_LAST])
                    copied(copy(win[0:NS, 4, :], ps[96:96 + NS, 0:256]), "A4")
                    return
                copy(qn_buf[n % 2][0:r, 0:256], ps[0:r, 0:256])
                copied(copy(rows[0:r, i, 0:256], ps[0:r, 256:512]), f"A{i}")
                ps = taken(eng, f"B{i}")
                copied(copy(rows[0:r, i, 256:512], ps[0:r, 0:256]), f"B{i}")
                ps = taken(eng, f"C{i}")
                copy(gates[0:r, i, :], ps[0:r, 256:W_LAST])
                copied(copy(win[0:r, i, :], ps[0:r, 0:256]), f"C{i}")

            def feature_qk(i):
                r, c = ROWS[i], COL[i]
                ps = taken(eng, f"K{i}")
                if i == 4:
                    eng.wait_ge(S["params_made"], 1)
                v = ps[:, 0:4 * r].rearrange("p (g t) -> p g t", g=4)
                eng.activation(qT[:, :, c:c + r], v[:, 0:2, :], ACT.Copy, scale=qg_scaled)
                copied(copy(kT[:, :, c:c + r], v[:, 2:4, :]), f"K{i}")
                if i < 4:
                    ps = taken(eng, f"R{i}")
                    copied(copy(raw[:, :, c:c + r], ps[:, 0:256].rearrange("p (g t) -> p g t", g=2)), f"R{i}")

            def sample_keys(b):
                ps = taken(eng, f"sR{b}")
                copied(copy(raw[:, :, SEQ + PAST * b:SEQ + PAST * (b + 1)], ps[:, :].rearrange("p (c t) -> p c t", c=2)), f"sR{b}")
                if b >= 2:
                    eng.wait_ge(S["sample_scores"], b - 1)
                if b == 0:
                    drained(eng, "K4")
                copy(smp_kT[b % 2][:, :, 256:257], kT[:, :, SEQ + b:SEQ + b + 1])
                ps = taken(eng, f"sK{b}")
                copied(copy(smp_kT[b % 2][:, :, 0:256], ps[:, :].rearrange("p (r t) -> p r t", r=2)), f"sK{b}")

            for n, i in enumerate(PROJ_TILES):
                kv_rows(n, i)
                if i == 0:
                    ps = taken(eng, "states")
                    copied(copy(states[:, :], ps[:, 0:336]), "states")
                    eng.wait_ge(S["sp_exp_asked"], 1)
                    eng.activation(sp[:, 1, :], sp[:, 0, :], ACT.Exp, scale=-1.0).then_inc(S["sp_exp"], 1)
                if n:
                    feature_qk(PROJ_TILES[n - 1])
                for b in SAMPLES_AT.get(i, ()):
                    sample_keys(b)
            feature_qk(3)
            drained(eng, "C3")
            eng.activation(gates[:, 0:4, :], gates[:, 0:4, :], ACT.Tanh, scale=0.5)
            eng.activation(gates[0:NS, 4, :], gates[0:NS, 4, :], ACT.Tanh, scale=0.5).then_inc(S["gates_tanh"], 1)

            for b in SAMPLES_AT["end"]:
                sample_keys(b)
            for comp, (name, out) in enumerate((("CK", kc_a), ("CV", vcT))):
                for kv in range(2):
                    lo = 64 * kv
                    other = 64 - lo
                    ps = taken(eng, f"{name}{kv}")
                    eng.activation(out[lo:lo + 64, 0:N_CHUNK - 1], ps[other:other + 64, 1:N_CHUNK], ACT.Identity, bias=params[lo:lo + 64, P_PHI_B + comp:P_PHI_B + comp + 1]).then_inc(S["kc_copied"], 1)
            eng.wait_ge(S["kc_sum"], 1)
            eng.activation(kc_sq, kcT, ACT.Square).then_inc(S["kc_squared"], 1)
            def features(g, out_p, out_s, pad, func=ACT.Copy):
                for j in range(2):
                    ps = taken(eng, f"F{g}{j}0")
                    copied(eng.activation(out_p[:, j, pad:pad + HALF], ps[:, 0:HALF], func), f"F{g}{j}0")
                    ps = taken(eng, f"F{g}{j}1")
                    if out_s is None:
                        copied(eng.activation(out_p[:, j, HALF:T], ps[:, 0:HALF], func), f"F{g}{j}1")
                    else:
                        eng.activation(out_p[:, j, pad + HALF:pad + SEQ], ps[:, 0:SEQ - HALF], func)
                        copied(eng.activation(out_s[:, j, :], ps[:, SEQ - HALF:HALF], func), f"F{g}{j}1")

            eng.dma_start(o["pool_s"].rearrange("l b k c -> (l b) k c")[:, 0:POOL_KEEP - 1, :], a["state_pool"].rearrange("l b k c -> (l b) k c")[:, 1:POOL_KEEP, :]).then_inc(S["states_stored"], 16)
            eng.dma_start(o["rgc_s"].rearrange("l b k c -> (l b) k c")[:, 0:RG_KEEP - 1, :], a["state_rg_conv"].rearrange("l b k c -> (l b) k c")[:, 1:RG_KEEP, :]).then_inc(S["states_stored"], 16)
            eng.dma_start(o["scc_s"].rearrange("l b k c -> (l b) k c")[:, 0:SC_KEEP - 1, :], a["state_sc_conv"].rearrange("l b k c -> (l b) k c")[:, 1:SC_KEEP, :]).then_inc(S["states_stored"], 16)
            eng.dma_start(o["win_s"].rearrange("l b t c k d -> (l b) t (c k d)")[:, 0:PAST - 1, :], win_state[:, 1:PAST, :]).then_inc(S["states_stored"], 16)

            features("U", u_ext, u_smp[:, :, :], POOL_KEEP)
            drained(eng, "FU11")
            eng.sem_inc(S["u_copied"], 1)
            ps = taken(eng, "CN")
            copied(eng.activation(kc_sq, ps[:, 0:N_CHUNK], ACT.Sqrt, scale=1.0 / HD, bias=eps_col), "CN")
            features("X", r_ext, r_smp[:, :, :], RG_KEEP)
            drained(eng, "FX11")
            eng.sem_inc(S["f_copied"], 1)
            for r in range(3):
                eng.wait_ge(S["smax_made"], r + 1)
                if r < 2:
                    ps = taken(eng, "SSSW"[2 * r:2 * r + 2])
                    copied(eng.activation(smp_p[0:32, r, :], ps[0:32, 0:257], ACT.Exp, bias=smx[0:32, r:r + 1], accum_out=ssum[0:32, r:r + 1]), "SSSW"[2 * r:2 * r + 2])
                else:
                    ps = taken(eng, "cs")
                    copied(eng.activation(smp_pc[0:32, 0:15], ps[0:32, 0:15], ACT.Exp, bias=smx[0:32, 2:3], accum_out=ssum[0:32, 2:3]), "cs")
            eng.wait_ge(S["cmp_max"], 1)
            eng.activation(cmp_s, cmp_s, ACT.Exp).then_inc(S["cmp_exp"], 1)

            features("R", g_buf, None, 0, ACT.Gelu_apprx_tanh)
            ps = taken(eng, "pn")
            copied(copy(smp_new[0:NS, :, :], ps[0:NS, 0:64].rearrange("p (r t) -> p r t", r=2)), "pn")
            drained(eng, "SO")
            features("Z", z_buf, None, 0)
            drained(eng, "FZ11")
            eng.sem_inc(S["f_copied"], 1)
            tr, ti, t2, sq = m[4], m[5], m[6], m[0]
            for j in range(2):
                ps = taken(eng, f"RA{j}")
                copied(eng.activation(tr[:, j, 0:SEQ], ps[:, :], ACT.Tanh, scale=0.5, bias=half_b[:, j:j + 1]), f"RA{j}")
                ps = taken(eng, f"RX{j}")
                copied(eng.activation(ti[:, j, 0:SEQ], ps[:, :], ACT.Tanh, scale=0.5, bias=half_b[:, 2 + j:3 + j]), f"RX{j}")
            ps = taken(eng, "RGs")
            for j in range(2):
                eng.activation(tr[:, j, SEQ:T], ps[:, 8 * j:8 * j + 8], ACT.Tanh, scale=0.5, bias=half_b[:, j:j + 1])
                ins = eng.activation(ti[:, j, SEQ:T], ps[:, 16 + 8 * j:24 + 8 * j], ACT.Tanh, scale=0.5, bias=half_b[:, 2 + j:3 + j])
            copied(ins, "RGs")
            drained(eng, "RGs")
            for j in range(2):
                ps = taken(eng, f"PB{j}")
                copied(eng.activation(yT[:, j, 0:SEQ], ps[:, :], ACT.Copy, scale=params[:, P_POOL_SCALE + j:P_POOL_SCALE + j + 1]), f"PB{j}")
            ps = taken(eng, "PBs")
            for j in range(2):
                ins = eng.activation(yT[:, j, SEQ:T], ps[:, 8 * j:8 * j + 8], ACT.Copy, scale=params[:, P_POOL_SCALE + j:P_POOL_SCALE + j + 1])
            copied(ins, "PBs")
            for j in range(2):
                ins = eng.activation(t2[:, j, :], tr[:, j, :], ACT.Tanh, scale=sp[:, 4, j:j + 1], bias=sp[:, 4, j:j + 1])
            ins.then_inc(S["rg_t2"], 1)
            eng.wait_ge(S["rg_t2"], 1)
            drained(eng, "PB1")
            eng.activation(sq, t2, ACT.Sqrt).then_inc(S["rg_sqrt"], 1)

            def exps(n):
                i, u = n // 8, n % 8
                eng.wait_ge(S["att_max"], n + 1)
                if n >= 4:
                    job = f"T{n - 4}"
                    eng.wait_ge(bank_full[bank_of[job]], turn_of[job] + 1)
                ps = taken(eng, f"S{n}")
                col = 8 * i + 4 * (u // 4) + 2 * (u % 2) + (u // 2) % 2
                width = 128 * (i + 1)
                copied(eng.activation(p_buf[n % 4][:, 0:width], ps[:, 0:width], ACT.Exp, bias=att_mx[:, col:col + 1], accum_out=att_sum[:, col:col + 1]), f"S{n}")

            def turned(n):
                if n >= 4:
                    pv_done(eng, n - 4)
                ps = taken(eng, f"T{n}")
                width = 128 * (n // 8 + 1)
                copied(copy(pT_buf[n % 4][:, 0:width], ps[:, 0:width]), f"T{n}")

            def square_outputs(made, tiles):
                eng.wait_ge(S["yn_made"], made)
                for i in tiles:
                    r = ROWS[i]
                    eng.activation(reg_a.t[0:r, sq_at[i]:sq_at[i] + GW], ynsa[0:r, i, :], ACT.Square, accum_out=yss[0:r, i:i + 1]).then_inc(S["yn_sq"], 1)

            ps = taken(eng, "cT")
            copied(copy(pT_buf[0], ps[:, :]), "cT")
            eng.wait_ge(bank_full[bank_of["Oc3"]], turn_of["Oc3"] + 1)
            for step in range(N_PAIR + 1):
                if step == NORM_STEP:
                    for g in range(3):
                        ps = taken(eng, f"N{g}")
                        copied(eng.activation(m[4 + g // 2][:, g % 2, 0:SEQ], ps[:, :], ACT.Sqrt, scale=1.0 / GW, bias=eps_col), f"N{g}")
                    ps = taken(eng, "Ns")
                    eng.activation(m[4][:, :, SEQ:T], ps[:, 0:16].rearrange("p (j t) -> p j t", j=2), ACT.Sqrt, scale=1.0 / GW, bias=eps_col)
                    copied(eng.activation(m[5][:, 0, SEQ:T], ps[:, 16:24], ACT.Sqrt, scale=1.0 / GW, bias=eps_col), "Ns")
                if step < N_PAIR:
                    exps(2 * step)
                    exps(2 * step + 1)
                if step > 0:
                    turned(2 * step - 2)
                if step == N_PAIR - 1:
                    square_outputs(2, [4, 0, 1, 2])
            square_outputs(3, [3])
            ps = taken(eng, "TLa")
            copied(copy(tail_rows[0:24, 0:512], ps[0:24, :]), "TLa")
            ps = taken(eng, "TLb")
            copied(copy(tail_rows[0:24, 512:1024], ps[0:24, :]), "TLb")
            for i in TILES:
                r = ROWS[i]
                ps = taken(eng, f"NT{i}")
                for j in range(2):
                    ins = eng.activation(yT[:, 4 + j, COL[i]:COL[i] + r], ps[:, j * r:(j + 1) * r], ACT.Copy, scale=params[:, P_OUT_G + 4 + j:P_OUT_G + 5 + j])
                copied(ins, f"NT{i}")
            drained(eng, "TLb")
            for name_p, name_s, keep, col in (("pool_p", "pool_s", POOL_KEEP, 0), ("rgc_p", "rgc_s", RG_KEEP, 256), ("scc_p", "scc_s", SC_KEEP, 512)):
                eng.dma_start(o[name_p].rearrange("l b k c -> (l b k) c"), tail_rows[16 - keep:16, col:col + 256]).then_inc(S["tails_stored"], 16)
                eng.dma_start(o[name_s].rearrange("l b k c -> (l b) k c")[:, keep - 1, :], tail_rows[16:24, col:col + 256]).then_inc(S["tails_stored"], 16)
            eng.dma_start(o["rgh_p"].rearrange("l b c -> (l b) c"), tail_rows[15:16, 768:1024]).then_inc(S["tails_stored"], 16)
            eng.dma_start(o["rgh_s"].rearrange("l b c -> (l b) c"), tail_rows[16:24, 768:1024]).then_inc(S["tails_stored"], 16)

            def sums(n):
                i = TILES[n]
                r = ROWS[i]
                if i < 4:
                    drained(eng, f"Y{i}.1")
                else:
                    ps = taken(eng, "Y4.0")
                    for w in range(4):
                        ins = copy(y_smp[:, 256 * w:256 * w + 256], ps[32 * w:32 * w + NS, 0:256])
                    copied(ins, "Y4.0")
                    eng.wait_ge(S["x1_smp"], 1)
                eng.activation(h2[0:r, i, :], x1[0:r, i, :], ACT.Square, accum_out=sumsq[0:r, i:i + 1]).then_inc(S["x1_ss"], 1)

            def h2_turned(n):
                i = TILES[n]
                r = ROWS[i]
                if n:
                    eng.wait_ge(S["routed"], n)
                for k, name in enumerate(("hTa", "hTb")):
                    ps = taken(eng, f"{name}{i}")
                    copied(copy(h2T[:, 4 * k:4 * k + 4, 0:r], ps[:, 0:4 * r].rearrange("p (c t) -> p c t", c=4)), f"{name}{i}")

            eng.wait_ge(S["rows_stored"], 16 * 4)
            eng.wait_ge(bank_full[bank_of["NT3"]], turn_of["NT3"] + 1)
            eng.wait_ge(S["h2_zeroed"], 1)
            for n in range(NTILE):
                sums(n)
                if n:
                    h2_turned(n - 1)
            h2_turned(4)
            eng.wait_ge(S["rt_d"], 1)
            eng.activation(lex, lex, ACT.Exp).then_inc(S["rt_exp"], 1)
            eng.wait_ge(S["rt_d"], 2)
            eng.activation(tdx, tdx, ACT.Exp).then_inc(S["rt_exp"], 1)

            eng.wait_ge(S["rounds_made"], 1)
            rounds = eng.value_load(n_rounds[0:1, 0:1], min_val=1, max_val=ROUNDS)
            eng.sem_inc(y_stored[0], 16)
            eng.sem_inc(y_stored[1], 16)
            eng.sem_inc(S["y_copied"], 2)
            eng.wait_ge(S["gathered"], 1)
            copy(x_tok, bank[0][:, :]).then_inc(S["x_tok_made"], 1)
            with eng.Fori(0, rounds) as r:
                eng.wait_ge(S["round_combined"], r + 1)
                with eng.Fori(0, N_EXP // 2) as i:
                    for b in range(2):
                        e = 2 * i + b
                        n = N_EXP * r + e
                        eng.wait_ge(S["gu_done"], n + 1)
                        eng.activation(silu[b], bank[2 + b][:, 0:256], ACT.Silu).then_inc(S["silu_done"], 1)
                        eng.wait_ge(S["gathered"], n + 2)
                        copy(x_tok, bank[0][:, :]).then_inc(S["x_tok_made"], 1)
                        eng.wait_ge(S["down_done"], n + 1)
                        eng.wait_ge(y_stored[b], (N_EXP // 2) * 16 * r + 16 * i + 16)
                        copy(y_out[b], bank[6 + b][:, :]).then_inc(S["y_copied"], 1)
                        eng.wait_ge(S["y_copied"], n + 3)
                        eng.dma_start(y_dram[bass.ds(e * CAP, CAP)].rearrange("t (s n) -> s t n", s=2), y_out[b]).then_inc(y_stored[b], 16)
                for b in range(2):
                    eng.wait_ge(y_stored[b], (N_EXP // 2) * 16 * r + (N_EXP // 2) * 16 + 16)
                eng.sem_inc(S["moe_stored"], 1)

        @block.tensor
        def _(eng):
            def mm(out, lhsT, rhs, start, stop):
                return eng.matmul(out, lhsT, rhs, start=start, stop=stop, skip_group_check=True)

            def turn(out, in_):
                return eng.transpose(out, in_, ident[0:in_.shape[0], 0:in_.shape[0]])

            eng.wait_ge(S["ident_made"], 1)
            eng.wait_ge(S["xn_made"], 1)
            ps = claim(eng, "xT4")
            for c in range(KC):
                ins = turn(ps[:, 8 * c:8 * c + 8], xn[0:NS, 4, 128 * c:128 * c + 128])
            filled(ins, "xT4")
            for i in range(4):
                eng.wait_ge(S["xn_made"], i + 2)
                for k, name in enumerate(("xTa", "xTb")):
                    ps = claim(eng, f"{name}{i}")
                    for c in range(4):
                        ins = turn(ps[:, 128 * c:128 * c + 128], xn[:, i, 512 * k + 128 * c:512 * k + 128 * c + 128])
                    filled(ins, f"{name}{i}")

            def project_samples():
                ps = claim(eng, "A4")
                for c in range(KC):
                    for w in range(4):
                        weights = w_last if w == 3 else w_slot[w]
                        ins = mm(ps[32 * w:32 * w + NS, 0:weights.shape[2]], xnT[:, c, SEQ:T], weights[:, c, :], c == 0, c == KC - 1)
                filled(ins, "A4")

            def project(i):
                for name, slots in (("A", (0, 1)), ("B", (2,)), ("C", (3,))):
                    ps = claim(eng, f"{name}{i}")
                    for k, w in enumerate(slots):
                        if i == 0:
                            eng.wait_ge(w_loaded[w], 16)
                        weights = w_last if w == 3 else w_slot[w]
                        width = weights.shape[2]
                        for c in range(KC):
                            ins = mm(ps[:, 256 * k:256 * k + width], xnT[:, c, COL[i]:COL[i] + 128], weights[:, c, :], c == 0, c == KC - 1)
                    filled(ins, f"{name}{i}")

            def turn_qk(n):
                i = PROJ_TILES[n]
                r = ROWS[i]
                eng.wait_ge(S["qk_normed"], n + 1)
                ps = claim(eng, f"K{i}")
                q = qn_buf[n % 2]
                for g in range(2):
                    turn(ps[:, g * r:(g + 1) * r], q[0:r, 256 + 128 * g:384 + 128 * g])
                turn(ps[:, 2 * r:3 * r], rows[0:r, i, 256:384])
                filled(turn(ps[:, 3 * r:4 * r], win[0:r, i, 0:128]), f"K{i}")
                if i < 4:
                    ps = claim(eng, f"R{i}")
                    turn(ps[:, 0:128], rows[:, i, 0:128])
                    filled(turn(ps[:, 128:256], rows[:, i, 128:256]), f"R{i}")

            def sample_scores(b):
                drained(eng, f"sK{b}")
                for r, name in enumerate(("SS", "SW")):
                    ps = claim(eng, name) if b == 0 else bank[bank_of[name]]
                    ins = mm(ps[0:32, 0:257], q_masked[:, 32 * b:32 * b + 32], smp_kT[b % 2][:, r, :], b == 0, b == NS - 1)
                    if b == NS - 1 and name == "SS":
                        filled(ins, name)
                if b == NS - 1:
                    filled(ins, "SW")
                else:
                    ins.then_inc(S["sample_scores"], 1)

            def sample_keys(b):
                eng.wait_ge(smp_loaded[b % 2], 48 * (b // 2 + 1))
                ps = claim(eng, f"sR{b}")
                for c in range(2):
                    for g in range(2):
                        ins = turn(ps[:, 256 * c + 128 * g:256 * c + 128 * g + 128], page_k[b % 2][:, g, 128 * c:128 * c + 128])
                filled(ins, f"sR{b}")
                ps = claim(eng, f"sK{b}")
                for g in range(2):
                    turn(ps[:, 128 * g:128 * g + 128], page_k[b % 2][:, g, 256:384])
                for g in range(2):
                    ins = turn(ps[:, 256 + 128 * g:384 + 128 * g], win_k[b % 2][:, g, :])
                filled(ins, f"sK{b}")
                if b == 1:
                    eng.wait_ge(S["q_masked_made"], 1)
                if b:
                    sample_scores(b - 1)

            for n, i in enumerate(PROJ_TILES):
                if i == 4:
                    drained(eng, "xT4")
                    project_samples()
                else:
                    drained(eng, f"xTa{i}")
                    drained(eng, f"xTb{i}")
                    project(i)
                if i == 0:
                    eng.wait_ge(S["par_loaded"], 16 * PAR_DMAS)
                    filled(turn(claim(eng, "params")[:, 0:P_ROWS], par_rows), "params")
                    eng.wait_ge(S["states_loaded"], 16 * 4)
                    ps = claim(eng, "states")
                    for j in range(2):
                        turn(ps[:, 48 * j:48 * j + 48], st_rows[:, 128 * j:128 * j + 128])
                        ins = turn(ps[:, 96 + 120 * j:216 + 120 * j], st_pool[:, 128 * j:128 * j + 128])
                    filled(ins, "states")
                if n:
                    turn_qk(n - 1)
                for b in SAMPLES_AT.get(i, ()):
                    sample_keys(b)
            turn_qk(4)
            for b in SAMPLES_AT["end"]:
                sample_keys(b)
            sample_scores(NS - 1)
            eng.wait_ge(S["phi_loaded"], 16 * 8)
            drained(eng, f"sR{NS - 1}")
            for comp, name in enumerate(("CK", "CV")):
                ps2 = [claim(eng, f"{name}{kv}") for kv in range(2)]
                for j in range(16):
                    for kv in range(2):
                        lo = 64 * kv
                        src = raw[lo:lo + 64, comp, :].rearrange("p (n s) -> p n s", s=16)[:, :, j]
                        ins = mm(ps2[kv][:, 0:N_CHUNK], phi[lo:lo + 64, comp, j].rearrange("p h n -> p (h n)"), src, j == 0, j == 15)
                        if j == 15:
                            filled(ins, f"{name}{kv}")
            def features(g):
                n = 4 + "UXRZCB".index(g)
                eng.wait_ge(w_loaded[n % W_SLOTS], 16 * (n // W_SLOTS + 1))
                for j in range(2):
                    halves = [claim(eng, f"F{g}{j}{h}") for h in range(2)]
                    for c in range(KC):
                        w = w_slot[n % W_SLOTS][:, c, 128 * j:128 * j + 128]
                        for h in range(2):
                            ins = mm(halves[h][:, 0:HALF], w, xnT[:, c, HALF * h:HALF * (h + 1)], c == 0, c == KC - 1)
                            if c == KC - 1:
                                filled(ins, f"F{g}{j}{h}")

            features("U")
            eng.wait_ge(S["kc_squared"], 1)
            filled(mm(claim(eng, "CN")[:, 0:N_CHUNK], block_ones, kc_sq, True, True), "CN")
            features("X")
            eng.wait_ge(S["kc_made"], 1)
            ps = claim(eng, "VT")
            turn(ps[:, 0:128], kc_a[:, 0:128])
            filled(turn(ps[:, 128:256], vcT[:, 32:160]), "VT")
            ps = claim(eng, "cs")
            for b in range(NS):
                ins = mm(ps[0:32, 0:15], q_masked[:, 32 * b:32 * b + 32], kcT[:, 32 + 16 * b:47 + 16 * b], b == 0, b == NS - 1)
            filled(ins, "cs")
            ps2 = [claim(eng, f"cp{kv}") for kv in range(2)]
            for i in range(4):
                for g in range(2):
                    for kv in range(2):
                        lo, u = 64 * kv, 2 * i + g
                        ins = mm(ps2[kv][:, 32 * u:32 * u + 31], qT[lo:lo + 64, g, COL[i]:COL[i] + 128], kcT[lo:lo + 64, 0:31], True, True)
                        if u == 7:
                            filled(ins, f"cp{kv}")
            eng.wait_ge(S["gates_raw"], 1)
            filled(mm(claim(eng, "g32")[0:32, 0:12], sample_of_row[0:8, :], gates[0:NS, 4, :], True, True), "g32")

            features("R")
            eng.wait_ge(S["sp_scaled"], 1)
            ps = claim(eng, "PT")
            for r in range(2):
                for g in range(2):
                    turn(ps[:, 64 * r + 32 * g:64 * r + 32 * g + 32], smp_p[0:32, r, 128 * g:128 * g + 128])
            filled(turn(ps[:, 128:160], smp_pc3[0:32].rearrange("p b c -> p (b c)")), "PT")
            filled(mm(claim(eng, "pn")[0:NS, 0:64], row_of_sample[0:32, :], smp_diag[0:32].rearrange("p r t -> p (r t)"), True, True), "pn")
            drained(eng, "PT")
            drained(eng, "pn")
            eng.wait_ge(S["vcache_loaded"], 16 * (2 * NS + 2))
            ps = claim(eng, "SO")
            for r, v in enumerate((vs_cache, vw_cache)):
                for g in range(2):
                    for b in range(NS):
                        at = 32 * NS * (2 * r + g) + 32 * b
                        mm(ps[0:32, 0:128], p_masked[:, at:at + 32], v[:, b, g, :], r == 0 and g == 0 and b == 0, False)
            mm(ps[0:32, 0:128], smp_new[0:NS, 0, :], rows[0:NS, 4, 384:512], False, False)
            mm(ps[0:32, 0:128], smp_new[0:NS, 1, :], win[0:NS, 4, 128:256], False, False)
            filled(mm(ps[0:32, 0:128], smp_pcT, vc_smp, False, True), "SO")
            features("Z")
            eng.wait_ge(S["conv_made"], 1)
            xc = m[1]
            ps = claim(eng, "RGs")
            for k in range(4):
                ins = mm(ps[:, 8 * k:8 * k + 8], rg_w[:, k, :], xc[:, k % 2, SEQ:T], True, True)
            filled(ins, "RGs")
            for j in range(2):
                for k, name in enumerate(("RA", "RX")):
                    filled(mm(claim(eng, f"{name}{j}")[:, :], rg_w[:, 2 * k + j, :], xc[:, j, 0:SEQ], True, True), f"{name}{j}")
            eng.wait_ge(S["blocks_loaded"], 16 * 12)
            eng.wait_ge(S["pool_d"], 1)
            ps = claim(eng, "PBs")
            for j in range(2):
                ins = mm(ps[:, 8 * j:8 * j + 8], pool_w[:, j, :], m[3][:, j, SEQ:T], True, True)
            filled(ins, "PBs")
            for j in range(2):
                filled(mm(claim(eng, f"PB{j}")[:, :], pool_w[:, j, :], m[3][:, j, 0:SEQ], True, True), f"PB{j}")
            features("C")
            features("B")

            eng.wait_ge(S["cmp_scaled"], 1)
            ps = claim(eng, "cT")
            for i in range(4):
                ins = turn(ps[:, 128 * i:128 * i + 128], cmp_s[:, 4 * i:4 * i + 4, :].rearrange("p u c -> p (u c)"))
            filled(ins, "cT")
            drained(eng, "cT")
            for i in range(4):
                filled(mm(claim(eng, f"Oc{i}")[:, 0:256], pT_buf[0][:, 128 * i:128 * i + 128], vc_blk, True, True), f"Oc{i}")

            def head(u):
                return u // 4, (u // 2) % 2, u % 2

            def scores(step):
                i = step // 4
                br, g, _ = head(2 * step % 8)
                width = 128 * (i + 1)
                outs = [claim(eng, f"S{2 * step + kv}") for kv in range(2)]
                for kv in range(2):
                    lo = 64 * kv
                    mm(outs[kv][:, 0:width], qT[lo:lo + 64, g, COL[i]:COL[i] + 128], kT[lo:lo + 64, br, 0:width], True, False)
                for kv in range(2):
                    filled(mm(outs[kv][:, 128 * i:width], ident_bf[:, :], causal_bf[:, :], False, True), f"S{2 * step + kv}")

            def turn_p(n):
                drained(eng, f"S{n}")
                ps = claim(eng, f"T{n}")
                for c in range(n // 8 + 1):
                    ins = turn(ps[:, 128 * c:128 * c + 128], p_buf[n % 4][:, 128 * c:128 * c + 128])
                filled(ins, f"T{n}")

            def values(n):
                i, u = n // 8, n % 8
                br, g, kv = head(u)
                if u == 0:
                    claim(eng, f"O{i}")
                drained(eng, f"T{n}")
                ps = bank[bank_of[f"O{i}"]]
                at = 256 * br + 64 * (2 * kv + g)
                src = (rows, 384) if br == 0 else (win, 128)
                for c in range(i + 1):
                    ins = mm(ps[:, at:at + 64], pT_buf[n % 4][:, 128 * c:128 * c + 128], src[0][:, c, src[1] + 64 * kv:src[1] + 64 * kv + 64], c == 0, c == i)
                if u == 7:
                    filled(ins, f"O{i}")
                else:
                    ins.then_inc(S["att_pv"], 1)

            for step in range(N_PAIR + 2):
                if step == NORM_STEP:
                    for g in range(3):
                        eng.wait_ge(S["sq_made"], g + 1)
                        ps = claim(eng, f"N{g}")
                        for j in range(2):
                            ins = mm(ps[:, :], ones, m[g][:, j, 0:SEQ], j == 0, j == 1)
                        filled(ins, f"N{g}")
                    ps = claim(eng, "Ns")
                    for g in range(3):
                        for j in range(2):
                            ins = mm(ps[:, 8 * g:8 * g + 8], ones, m[g][:, j, SEQ:T], j == 0, j == 1)
                    filled(ins, "Ns")
                if step < N_PAIR:
                    scores(step)
                for kv in range(2):
                    if 0 < step <= N_PAIR:
                        turn_p(2 * step - 2 + kv)
                for kv in range(2):
                    if step > 1:
                        values(2 * step - 4 + kv)
            eng.wait_ge(S["tails_made"], 1)
            for k, name in enumerate(("TLa", "TLb")):
                ps = claim(eng, name)
                for c in range(4):
                    ins = turn(ps[0:24, 128 * c:128 * c + 128], tails[:, 4 * k + c, :])
                filled(ins, name)
            for n, i in enumerate(TILES):
                r = ROWS[i]
                if n == 0:
                    eng.wait_ge(S["yn_scaled"], 1)
                if n == 4:
                    eng.wait_ge(S["yn_scaled"], 2)
                ps = claim(eng, f"NT{i}")
                for j in range(2):
                    ins = turn(ps[:, j * r:(j + 1) * r], ynsa[0:r, i, 128 * j:128 * j + 128])
                filled(ins, f"NT{i}")
            eng.wait_ge(S["wout_loaded"], 16)
            eng.wait_ge(S["yT_ready"], 1)
            claim(eng, "L")

            def project_out(n):
                i = TILES[n]
                r = ROWS[i]
                drained(eng, f"NT{i}")
                if i == 4:
                    ps = claim(eng, "Y4.0")
                    for c in range(KC):
                        for w in range(4):
                            ins = mm(ps[32 * w:32 * w + NS, 0:256], yT[:, c, SEQ:T], w_out[:, c, 256 * w:256 * w + 256], c == 0, c == KC - 1)
                    filled(ins, "Y4.0")
                    return
                for half in range(2):
                    if half == 1 and n >= 2:
                        route(n - 2)
                    ps = claim(eng, f"Y{i}.{half}")
                    for c in range(KC):
                        ins = mm(ps[0:r, :], yT[:, c, COL[i]:COL[i] + r], w_out[:, c, 512 * half:512 * half + 512], c == 0, c == KC - 1)
                    filled(ins, f"Y{i}.{half}")

            def turn_h2(n):
                i = TILES[n]
                r = ROWS[i]
                eng.wait_ge(S["h2_made"], n + 1)
                for k, name in enumerate(("hTa", "hTb")):
                    ps = claim(eng, f"{name}{i}")
                    for c in range(4):
                        ins = turn(ps[:, c * r:(c + 1) * r], h2[0:r, i, 512 * k + 128 * c:512 * k + 128 * c + 128])
                    filled(ins, f"{name}{i}")

            def route(n):
                i = TILES[n]
                r = ROWS[i]
                drained(eng, f"hTb{i}")
                if n == 0:
                    eng.wait_ge(S["rtw_loaded"], 16 * 4)
                ps = bank[bank_of["L"]]
                for c in range(KC):
                    ins = mm(ps[0:r, 36 * i:36 * i + 36], h2T[:, c, 0:r], rt_w[:, c, :], c == 0, c == KC - 1)
                if n < 4:
                    ins.then_inc(S["routed"], 1)
                else:
                    filled(ins, "L")

            for n in range(NTILE):
                project_out(n)
                if n:
                    turn_h2(n - 1)
            route(3)
            turn_h2(4)
            route(4)
            eng.wait_ge(S["mask_made"], 1)
            ps = claim(eng, "pos")
            for i in range(NTILE):
                for k in range(i + 1):
                    ins = mm(ps[:, 32 * i:32 * i + 32], before_bf[:, :] if k == i else ones_bf[:, :], mask_bf[:, k, :], k == 0, k == i)
            filled(ins, "pos")
            ps = claim(eng, "cnt")
            for k in range(NTILE):
                ins = mm(ps[:, 0:32], ones_bf[:, :], mask_bf[:, k, :], k == 0, k == NTILE - 1)
            filled(ins, "cnt")

            def gather(b, tiles):
                for t in tiles:
                    for s in range(2):
                        ins = mm(bank[0][64 * s:64 * s + 64, :], onehot[b][:, t, :], h2[:, t, 512 * s:512 * s + 512], t == 0, t == NTILE - 1)
                if t == NTILE - 1:
                    ins.then_inc(S["gathered"], 1)

            def turn_tokens():
                for j in range(4):
                    ins = turn(bank[1][:, 128 * j:128 * j + 128], x_tok[:, 128 * j:128 * j + 128])
                ins.then_inc(S["xe_turned"], 1)

            drained(eng, "pos")
            for b in range(8):
                eng.wait_ge(bank_read[b], uses[b] - (1 if b == bank_of["cnt"] else 0))
            eng.wait_ge(S["onehot_made"], 1)
            gather(0, range(NTILE))
            eng.wait_ge(S["x_tok_made"], 1)
            turn_tokens()
            drained(eng, "cnt")
            eng.wait_ge(S["rounds_made"], 1)
            rounds = eng.value_load(n_rounds[0:1, 0:1], min_val=1, max_val=ROUNDS)
            def expert(n, b, g, gu_loads, down_loads):
                eng.wait_ge(S["xe_made"], n + 1)
                for c in range(KC):
                    part, within = divmod(c, KC // GU_PARTS)
                    if within == 0:
                        eng.wait_ge(gu_loaded[g][part], gu_loads)
                    for s in range(2):
                        w = gu_w[g][:, c, :].rearrange("p (h f) -> p h f", h=2)[:, :, 256 * s:256 * s + 256]
                        ins = mm(bank[2 + b][64 * s:64 * s + 64, :].rearrange("p (h f) -> p h f", h=2), xe[b][:, c % 4, c // 4, :], w, c == 0, c == KC - 1)
                    if within == KC // GU_PARTS - 1:
                        ins.then_inc(gu_part_done[part], 1)
                eng.wait_ge(S["onehot_made"], n + 2)
                gather(1 - b, range(4))
                eng.wait_ge(S["hid_made"], n + 1)
                for k in range(2):
                    ins = turn(bank[4 + b][:, 128 * k:128 * k + 128], hid[b].rearrange("p (f k) -> p f k", k=2)[:, :, k])
                ins.then_inc(S["xt_turned"], 1)
                gather(1 - b, [4])
                eng.wait_ge(down_loaded[b], down_loads)
                eng.wait_ge(S["hT_made"], n + 1)
                eng.wait_ge(S["y_copied"], n + 1)
                for s_in in range(2):
                    if s_in == 1:
                        eng.wait_ge(S["x_tok_made"], n + 2)
                        turn_tokens()
                    for k in range(2):
                        for s in range(2):
                            ins = mm(bank[6 + b][64 * s:64 * s + 64, :], hT[b][:, k, 64 * s_in:64 * s_in + 64], down_w[b][:, s_in, k, 512 * s:512 * s + 512], s_in == 0 and k == 0, s_in == 1 and k == 1)
                ins.then_inc(S["down_done"], 1)

            with eng.Fori(0, rounds) as r:
                n = N_EXP * r
                for e in range(6):
                    gu_before = 32 * r if e % 3 == 2 else 240 * r
                    expert(n + e, e % 2, e % 3, gu_before + 16 * (e // 3) + 16, 256 * r + 16 * (e // 2) + 16)
                with eng.Fori(0, (N_EXP - 6) // 2) as i:
                    for b in range(2):
                        expert(n + 6 + 2 * i + b, b, b, 240 * r + 16 * i + 48, 256 * r + 16 * i + 64)

        @block.vector
        def _(eng):
            link = chain_of(eng, "vector_chain")
            tt, ts, stt = eng.tensor_tensor, eng.tensor_scalar, eng.scalar_tensor_tensor
            eng.wait_ge(S["gain_loaded"], 16)
            for n, i in enumerate(TILES):
                r = ROWS[i]
                eng.wait_ge(S["xsq_done"], n + 1)
                ts(sumsq[0:r, i:i + 1], sumsq[0:r, i:i + 1], 1.0 / D, EPS, ALU.mult, ALU.add).then_inc(S["rstd_asked"], 1)
            for n, i in enumerate(TILES):
                r = ROWS[i]
                eng.wait_ge(S["rstd_made"], n + 1)
                stt(xn[0:r, i, :], x_in[0:r, i, :], rstd[0:r, i:i + 1], gain_mix[0:r, :], ALU.mult, ALU.mult).then_inc(S["xn_made"], 1)
            for i in range(4):
                ps = taken(eng, f"xTb{i}")
                copied(eng.tensor_copy(xnT[:, 4:8, COL[i]:COL[i] + 128], ps[:, :].rearrange("p (c t) -> p c t", c=4)), f"xTb{i}")
            def parameters():
                ps = taken(eng, "params")
                copied(eng.tensor_copy(params, ps[:, 0:P_ROWS]), "params")
                drained(eng, "params")
                eng.wait_ge(S["consts_made"], 1)
                ts(half_b, params[:, P_BA:P_BA + 4], 0.5, None, ALU.mult)
                lam = params[:, P_LAM:P_LAM + 2]
                ts(sp[:, 1, :], lam, -1.0, None, ALU.mult)
                link(ts(qg_scaled, params[:, P_QG:P_QG + 1], HD ** -0.5, None, ALU.mult))
                tt(sp[:, 0, :], lam, sp[:, 1, :], ALU.max).then_inc(S["sp_exp_asked"], 1)
                for k, win_len in enumerate((2, 4, 8, 16)):
                    lo, j = 64 * (k % 2), k // 2
                    ts(inv_cnt[lo:lo + 64, j, :], inv_cnt[lo:lo + 64, j, :], float(win_len), None, ALU.min)
                    ins = eng.memset(inv_win[lo:lo + 64, j:j + 1], 1.0 / win_len)
                link(ins)
                link(eng.reciprocal(inv_cnt, inv_cnt))
                link(eng.tensor_reduce(head_of_row[0:32, :], hr3[0:32].rearrange("p b h -> p h b"), X_AXIS, ALU.add))
                link(eng.tensor_reduce(kv_of_row[0:32, :], head_of_row[0:32, :].rearrange("p (k g) -> p k g", k=2), X_AXIS, ALU.add))

                eng.wait_ge(S["sp_exp"], 1)
                link(ts(sp[:, 2, :], sp[:, 1, :], 2.0, None, ALU.add))
                link(eng.reciprocal(sp[:, 2, :], sp[:, 2, :]))
                link(tt(sp[:, 1, :], sp[:, 1, :], sp[:, 2, :], ALU.mult))
                link(tt(sp[:, 2, :], sp[:, 1, :], sp[:, 1, :], ALU.mult))
                link(ts(sp[:, 3, :], sp[:, 2, :], 1.0 / 19, None, ALU.mult))
                for k in range(8, 0, -1):
                    link(stt(sp[:, 3, :], sp[:, 3, :], 1.0 / (2 * k + 1), sp[:, 2, :], ALU.add, ALU.mult))
                link(stt(sp[:, 3, :], sp[:, 3, :], 1.0, sp[:, 1, :], ALU.add, ALU.mult))
                link(ts(sp[:, 4, :], lam, -1.0, 0.0, ALU.mult, ALU.max))
                link(ts(sp[:, 4, :], sp[:, 4, :], 2.0, None, ALU.mult))
                link(stt(sp[:, 4, :], sp[:, 3, :], 4.0, sp[:, 4, :], ALU.mult, ALU.add))
                eng.sem_inc(S["params_made"], 1)

            eng.wait_ge(S["kg_loaded"], 16)
            for n, i in enumerate(PROJ_TILES):
                r = ROWS[i]
                q, sq = qn_buf[n % 2], sq_buf[n % 2]
                ksel, kwin = rows[0:r, i, 256:384], win[0:r, i, 0:128]
                if i < 4:
                    drained(eng, f"C{i}")
                drained(eng, f"A{i}")
                tt(sq[0:r, 0:256], q[0:r, 0:256], q[0:r, 0:256], ALU.mult)
                tt(sq[0:r, 256:384], ksel, ksel, ALU.mult)
                link(tt(sq[0:r, 384:512], kwin, kwin, ALU.mult))
                link(eng.tensor_reduce(hss[0:r, i, :], sq[0:r, :].rearrange("p (h d) -> p h d", h=8), X_AXIS, ALU.add))
                ts(hss[0:r, i, :], hss[0:r, i, :], 1.0 / HD, EPS, ALU.mult, ALU.add).then_inc(S["hss_made"], 1)
                eng.wait_ge(S["hrs_made"], n + 1)
                tt(q[0:r, 256:512].rearrange("p (g k d) -> p k g d", g=2, k=2), q[0:r, 0:256].rearrange("p (k g d) -> p k g d", g=2, k=2),
                   hrs[0:r, i, 0:4].rearrange("p (k g) -> p k g", k=2).unsqueeze(3).to_broadcast([r, 2, 2, HD]), ALU.mult)
                for br, k in enumerate((ksel, kwin)):
                    v = k.rearrange("p (k d) -> p k d", k=2)
                    link(tt(v, v, hrs[0:r, i, 4 + 2 * br:6 + 2 * br].unsqueeze(2).to_broadcast([r, 2, HD]), ALU.mult))
                    ins = tt(v, v, kg[0:r, br:br + 1, :].to_broadcast([r, 2, HD]), ALU.mult)
                ins.then_inc(S["qk_normed"], 1)
                if n == 0:
                    parameters()
                if n == 2:
                    drained(eng, "K4")
                    for kv in range(2):
                        lo = 64 * kv
                        for g in range(2):
                            first = 2 * kv + g
                            dst = q_masked[lo:lo + 64, first:first + 36 * (NS - 1) + 1:36]
                            ins = eng.tensor_copy(dst, qT[lo:lo + 64, g, SEQ:T])
                    ins.then_inc(S["q_masked_made"], 1)
            eng.wait_ge(S["gates_tanh"], 1)
            ts(gates[0:NS, 4, :], gates[0:NS, 4, :], 0.5, 0.5, ALU.mult, ALU.add)
            ts(gates[:, 0:4, :], gates[:, 0:4, :], 0.5, 0.5, ALU.mult, ALU.add).then_inc(S["gates_raw"], 1)
            eng.memset(kcT[:, N_CHUNK - 1:N_CHUNK], 0.0)
            eng.memset(vcT[:, N_CHUNK - 1:N_CHUNK], 0.0)
            for comp, (name, first, out) in enumerate((("CK", kc_a, kcT), ("CV", vcT, vcT))):
                for kv in range(2):
                    lo = 64 * kv
                    eng.wait_ge(S["kc_copied"], 2 * comp + kv + 1)
                    ps = taken(eng, f"{name}{kv}")
                    copied(tt(out[lo:lo + 64, 0:N_CHUNK - 1], first[lo:lo + 64, 0:N_CHUNK - 1], ps[lo:lo + 64, 0:N_CHUNK - 1], ALU.add), f"{name}{kv}")
                    drained(eng, f"{name}{kv}")
                if comp == 0:
                    eng.sem_inc(S["kc_sum"], 1)
            drained(eng, "CN")
            link(eng.reciprocal(kc_sq, kc_sq))
            link(stt(kcT, kcT, params[:, P_KCG:P_KCG + 1], kc_sq, ALU.mult, ALU.mult))
            eng.tensor_copy(kc_a[:, 0:128].rearrange("p (h c) -> p h c", h=4), vcT[:, 0:32].unsqueeze(1).to_broadcast([128, 4, 32])).then_inc(S["kc_made"], 1)
            ps = taken(eng, "VT")
            eng.tensor_copy(vc_smp, ps[:, 128:256])
            for kv in range(2):
                for g in range(2):
                    h = 2 * kv + g
                    ins = eng.tensor_copy(vc_blk[32 * h:32 * h + 32, 64 * h:64 * h + 64], ps[32 * h:32 * h + 32, 64 * kv:64 * kv + 64])
            copied(ins, "VT")
            for r, name in enumerate(("SS", "SW", "cs")):
                ps = taken(eng, name)
                width = 257 if r < 2 else 15
                eng.tensor_reduce(smx[0:32, r:r + 1], ps[0:32, 0:width], X_AXIS, ALU.max, negate=True).then_inc(S["smax_made"], 1)
            eng.memset(cmp_s[:, :, 31:32], NEG)
            for kv in range(2):
                ps = taken(eng, f"cp{kv}")
                for i in range(4):
                    ins = tt(cmp_s[:, 4 * i + 2 * kv:4 * i + 2 * kv + 2, 0:31], ps[:, 64 * i:64 * i + 64].rearrange("p (u c) -> p u c", u=2)[:, :, 0:31],
                             cmp_mask[:, i:i + 1, 0:31].to_broadcast([128, 2, 31]), ALU.add)
                copied(ins, f"cp{kv}")
                drained(eng, f"cp{kv}")
            link(eng.tensor_reduce(cmp_mx, cmp_s, X_AXIS, ALU.max))
            link(ts(cmp_mx, cmp_mx, NEG / 10, None, ALU.max))
            tt(cmp_s, cmp_s, cmp_mx.unsqueeze(2).to_broadcast([128, 16, 32]), ALU.subtract).then_inc(S["cmp_max"], 1)
            ps = taken(eng, "g32")
            copied(tt(g32m[0:32, :].rearrange("p (h x) -> p h x", h=4), ps[0:32, 0:12].rearrange("p (h x) -> p h x", h=4),
                      head_of_row[0:32, :].unsqueeze(2).to_broadcast([32, 4, 3]), ALU.mult), "g32")
            drained(eng, "g32")
            link(eng.tensor_reduce(g3[0:32, :], g32m[0:32, :].rearrange("p (h x) -> p x h", h=4), X_AXIS, ALU.add))
            drained(eng, "SS")
            drained(eng, "SW")
            drained(eng, "cs")
            link(eng.reciprocal(ssum[0:32, :], ssum[0:32, :]))
            tt(smx[0:32, 0:2], g3[0:32, 1:3], ssum[0:32, 0:2], ALU.mult)
            link(tt(smx[0:32, 2:3], g3[0:32, 0:1], ssum[0:32, 2:3], ALU.mult))
            for r in range(2):
                ts(smp_p[0:32, r, :], smp_p[0:32, r, :], smx[0:32, r:r + 1], None, ALU.mult)
            eng.memset(smp_pc[0:32, 15:16], 0.0)
            link(ts(smp_pc[0:32, 0:15], smp_pc[0:32, 0:15], smx[0:32, 2:3], None, ALU.mult))
            tt(smp_pc3[0:32], smp_pc[0:32, :].unsqueeze(1).to_broadcast([32, NS, 16]), row_of_sample[0:32, :].unsqueeze(2).to_broadcast([32, NS, 16]), ALU.mult)
            for r in range(2):
                ins = ts(smp_diag[0:32, r, :], ident[0:32, 0:32], smp_p[0:32, r, 256:257], None, ALU.mult)
            ins.then_inc(S["sp_scaled"], 1)
            eng.wait_ge(S["cmp_exp"], 1)
            link(eng.tensor_reduce(cmp_sum, cmp_s, X_AXIS, ALU.add))
            link(ts(cmp_sum, cmp_sum, 1e-30, None, ALU.max))
            link(eng.reciprocal(cmp_sum, cmp_sum))
            link(tt(cmp_w.rearrange("p (t h) -> p t h", t=4), cmp_sum.rearrange("p (t h) -> p t h", t=4),
                    gates[:, 0:4, :].rearrange("p t (h x) -> p t h x", h=4)[:, :, :, 0], ALU.mult))
            tt(cmp_s, cmp_s, cmp_w.unsqueeze(2).to_broadcast([128, 16, 32]), ALU.mult).then_inc(S["cmp_scaled"], 1)
            eng.memset(u_ext[:, :, 0:POOL_KEEP], 0.0)
            eng.memset(r_ext[:, :, 0:RG_KEEP], 0.0)
            link(eng.memset(c_ext[:, :, 0:SC_KEEP], 0.0))
            eng.sem_inc(S["u_copied"], 1)
            ps = taken(eng, "PT")
            for k in range(4):
                dst = p_masked[:, 256 * k:256 * k + 256]
                for h in range(4):
                    eng.tensor_copy(dst[:, h:h + 36 * (NS - 1) + 1:36], ps[:, 32 * k + h:32 * k + 32:4])
            copied(eng.tensor_copy(smp_pcT, ps[:, 128:160]), "PT")
            ps = taken(eng, "SO")
            link(ts(smp_o[0:32, :], ps[0:32, 0:64], kv_of_row[0:32, 0:1], None, ALU.mult))
            copied(stt(smp_o2[0:32, :], ps[0:32, 64:128], kv_of_row[0:32, 1:2], smp_o[0:32, :], ALU.mult, ALU.add), "SO")
            drained(eng, "SO")
            eng.sem_inc(S["smp_o_made"], 1)
            d = m[3]
            eng.wait_ge(S["u_copied"], 2)
            drained(eng, "states")
            for k, win_len in enumerate((2, 4, 8, 16)):
                lo, j = 64 * (k % 2), k // 2
                link(eng.tensor_reduce(d[lo:lo + 64, j, SEQ:T], st_poolT[j][lo:lo + 64, :, POOL_KEEP - win_len + 1:POOL_KEEP], X_AXIS, ALU.add))
                link(tt(d[lo:lo + 64, j, SEQ:T], d[lo:lo + 64, j, SEQ:T], u_smp[lo:lo + 64, j, :], ALU.add))
                link(ts(d[lo:lo + 64, j, SEQ:T], d[lo:lo + 64, j, SEQ:T], inv_win[lo:lo + 64, j:j + 1], None, ALU.mult))
            E = POOL_KEEP + SEQ
            s2, s4, s8 = m[0], m[6], m[2]
            link(eng.tensor_tensor(s2[:, 1, 0:SEQ], u_ext[:, 1, 15:E], u_ext[:, 1, 14:E - 1], ALU.add))
            link(eng.tensor_copy(s4[:, 1, 0:2], s2[:, 1, 0:2]))
            link(eng.tensor_tensor(s4[:, 1, 2:SEQ], s2[:, 1, 2:SEQ], s2[:, 1, 0:SEQ - 2], ALU.add))
            link(eng.tensor_copy(s8[:, 1, 0:4], s4[:, 1, 0:4]))
            link(eng.tensor_tensor(s8[:, 1, 4:SEQ], s4[:, 1, 4:SEQ], s4[:, 1, 0:SEQ - 4], ALU.add))
            link(eng.tensor_copy(d[64:128, 1, 0:8], s8[64:128, 1, 0:8]))
            link(eng.tensor_tensor(d[64:128, 1, 8:SEQ], s8[64:128, 1, 8:SEQ], s8[64:128, 1, 0:SEQ - 8], ALU.add))
            eng.sem_inc(S["pool_pad"], 1)
            eng.wait_ge(S["f_copied"], 1)
            xc, u, a_, sq = m[1], m[4], m[2], m[0]

            def conv(out, ext, new, keep, w_at, b_at, old_at):
                taps = keep + 1
                for j in range(2):
                    w = [params[:, w_at + 2 * k + j:w_at + 2 * k + j + 1] for k in range(taps)]
                    bias = params[:, b_at + j:b_at + j + 1]
                    old = st_misc[j][:, old_at:old_at + NS * keep].rearrange("p (b k) -> p b k", k=keep)
                    ts(out[:, j, 0:SEQ], ext[:, j, 0:SEQ], w[0], bias, ALU.mult, ALU.add)
                    link(ts(out[:, j, SEQ:T], old[:, :, 0], w[0], bias, ALU.mult, ALU.add))
                    for k in range(1, taps):
                        stt(out[:, j, 0:SEQ], ext[:, j, k:k + SEQ], w[k], out[:, j, 0:SEQ], ALU.mult, ALU.add)
                        src = old[:, :, k] if k < keep else new[:, j, :]
                        link(stt(out[:, j, SEQ:T], src, w[k], out[:, j, SEQ:T], ALU.mult, ALU.add))

            conv(xc, r_ext, r_smp, RG_KEEP, P_CONV_W, P_CONV_B, 0)
            eng.sem_inc(S["conv_made"], 1)
            ti, t2 = m[5], m[6]
            eng.wait_ge(S["rg_t2"], 1)
            link(ts(u, t2, 1.0, None, ALU.add))
            link(eng.reciprocal(u, u))
            ts(a_, u, 2.0, -1.0, ALU.mult, ALU.add)
            link(stt(ti, ti, 1.0, xc, ALU.add, ALU.mult))
            link(tt(ti, ti, u, ALU.mult))
            eng.wait_ge(S["rg_sqrt"], 1)
            link(tt(ti, ti, sq, ALU.mult))
            h = m[3]
            eng.wait_ge(bank_full[bank_of["PB1"]], turn_of["PB1"] + 1)
            for j in range(2):
                eng.tensor_tensor_scan(h[:, j, 0:SEQ], a_[:, j, 0:SEQ], ti[:, j, 0:SEQ], 0.0, ALU.mult, ALU.add)
                link(tt(h[:, j, SEQ:T], a_[:, j, SEQ:T], st_misc[j][:, 40:48], ALU.mult))
                link(tt(h[:, j, SEQ:T], h[:, j, SEQ:T], ti[:, j, SEQ:T], ALU.add))
            eng.sem_inc(S["h_made"], 1)
            drained(eng, "FR11")
            link(tt(yT[:, 2:4, :], h, g_buf, ALU.mult))
            eng.sem_inc(S["h_made"], 1)

            eng.wait_ge(S["f_copied"], 2)
            for j in range(2):
                ps = taken(eng, f"FC{j}0")
                copied(tt(c_ext[:, j, SC_KEEP:SC_KEEP + HALF], z_buf[:, j, 0:HALF], ps[:, 0:HALF], ALU.mult), f"FC{j}0")
                ps = taken(eng, f"FC{j}1")
                tt(c_ext[:, j, SC_KEEP + HALF:SC_KEEP + SEQ], z_buf[:, j, HALF:SEQ], ps[:, 0:SEQ - HALF], ALU.mult)
                copied(tt(c_smp[:, j, :], z_buf[:, j, SEQ:T], ps[:, SEQ - HALF:HALF], ALU.mult), f"FC{j}1")
            drained(eng, "FC11")
            eng.sem_inc(S["sc_z"], 1)
            conv(z_buf, c_ext, c_smp, SC_KEEP, P_SC_W, P_SC_B, 24)
            for j in range(2):
                for h in range(2):
                    at = slice(HALF * h, HALF * (h + 1))
                    ps = taken(eng, f"FB{j}{h}")
                    copied(tt(yT[:, 6 + j, at], z_buf[:, j, at], ps[:, 0:HALF], ALU.mult), f"FB{j}{h}")
            drained(eng, "FB11")
            eng.sem_inc(S["sc_b"], 1)
            def row_max(n):
                i, u = n // 8, n % 8
                col = 8 * i + 4 * (u // 4) + 2 * (u % 2) + (u // 2) % 2
                width = 128 * (i + 1)
                ps = taken(eng, f"S{n}")
                eng.tensor_reduce(att_mx[:, col:col + 1], ps[:, 0:width], X_AXIS, ALU.max, negate=True).then_inc(S["att_max"], 1)

            def turned(n):
                if n >= 4:
                    pv_done(eng, n - 4)
                ps = taken(eng, f"T{n}")
                width = 128 * (n // 8 + 1)
                copied(eng.tensor_copy(pT_buf[n % 4][:, 0:width], ps[:, 0:width]), f"T{n}")

            def branches(i):
                drained(eng, f"S{8 * i + 7}")
                w8 = att_w[:, 8 * i:8 * i + 8]
                link(eng.reciprocal(w8, att_sum[:, 8 * i:8 * i + 8]))
                link(tt(w8.rearrange("p (x h) -> p x h", x=2), w8.rearrange("p (x h) -> p x h", x=2),
                        gates[:, i, :].rearrange("p (h x) -> p x h", h=4)[:, 1:3, :], ALU.mult))
                ps = taken(eng, f"O{i}")
                copied(tt(o_tmp.rearrange("p (u d) -> p u d", d=HD), ps[:, :].rearrange("p (u d) -> p u d", d=HD),
                          w8.unsqueeze(2).to_broadcast([128, 8, HD]), ALU.mult), f"O{i}")
                drained(eng, f"O{i}")
                link(tt(ynsa[:, i, :], ynsa[:, i, :], o_tmp[:, 0:256], ALU.add))
                link(tt(ynsa[:, i, :], ynsa[:, i, :], o_tmp[:, 256:512], ALU.add))

            for i in range(4):
                ps = taken(eng, f"Oc{i}")
                copied(eng.tensor_copy(ynsa[:, i, :], ps[:, 0:256]), f"Oc{i}")
            for step in range(N_PAIR + 3):
                if step < N_PAIR:
                    row_max(2 * step)
                    row_max(2 * step + 1)
                if 0 < step <= N_PAIR:
                    turned(2 * step - 1)
                if NORM_STEP < step < NORM_STEP + 4:
                    g = step - NORM_STEP - 1
                    if g == 0:
                        drained(eng, "N2")
                        drained(eng, "Ns")
                    rs = m[4 + g // 2][:, g % 2, :]
                    eng.reciprocal(rs, rs).then_inc(S["nrm_made"], 1)
                if step == NORM_STEP + 4:
                    eng.wait_ge(S["nrm_made"], 3)
                    for g, first in ((0, 0), (1, 2), (2, 6)):
                        rs = m[4 + g // 2][:, g % 2, :]
                        for j in range(2):
                            gain = params[:, P_OUT_G + first + j:P_OUT_G + first + j + 1]
                            ins = stt(yT[:, first + j, :], yT[:, first + j, :], gain, rs, ALU.mult, ALU.mult)
                    ins.then_inc(S["yT_ready"], 1)
                if step >= 6 and step % 4 == 2:
                    branches(step // 4 - 1)
                if step == N_PAIR - 2:
                    eng.wait_ge(S["smp_o_moved"], 16 * 4)
                    eng.sem_inc(S["yn_made"], 2)
                if step == N_PAIR:
                    eng.wait_ge(S["yn_sq"], 4)
                    ts(yss[0:NS, 4:5], yss[0:NS, 4:5], 1.0 / GW, EPS, ALU.mult, ALU.add)
                    ts(yss[:, 0:3], yss[:, 0:3], 1.0 / GW, EPS, ALU.mult, ALU.add).then_inc(S["yn_ss"], 1)
                    eng.wait_ge(S["yn_rs"], 2)
                    for i in (4, 0, 1, 2):
                        r = ROWS[i]
                        ins = ts(ynsa[0:r, i, :], ynsa[0:r, i, :], yrs[0:r, i:i + 1], None, ALU.mult)
                    ins.then_inc(S["yn_scaled"], 1)
            eng.sem_inc(S["yn_made"], 1)
            eng.wait_ge(S["yn_sq"], NTILE)
            ts(yss[:, 3:4], yss[:, 3:4], 1.0 / GW, EPS, ALU.mult, ALU.add).then_inc(S["yn_ss"], 1)
            eng.wait_ge(S["yn_rs"], 3)
            ts(ynsa[:, 3, :], ynsa[:, 3, :], yrs[:, 3:4], None, ALU.mult).then_inc(S["yn_scaled"], 1)
            eng.wait_ge(bank_full[bank_of["NT3"]], turn_of["NT3"] + 1)
            eng.memset(h2[:, 4, :], 0.0).then_inc(S["h2_zeroed"], 1)

            eng.wait_ge(S["x_reloaded"], 32)
            eng.wait_ge(S["gainf_loaded"], 16)

            def second_norm(n):
                i = TILES[n]
                r = ROWS[i]
                eng.wait_ge(S["x1_rs"], n + 1)
                by_channel = "q (p c) -> q c p"
                stt(h2[0:r, i, :].rearrange("q (c p) -> q c p", c=KC), x1[0:r, i, :].rearrange(by_channel, c=KC), rstd[0:r, i:i + 1],
                    gain_ffn[0:r, :].rearrange(by_channel, c=KC), ALU.mult, ALU.mult).then_inc(S["h2_made"], 1)

            for n, i in enumerate(TILES):
                r = ROWS[i]
                if i == 4:
                    drained(eng, "Y4.0")
                    tt(x1[0:NS, 4, :], x1[0:NS, 4, :], y_smp, ALU.add).then_inc(S["x1_smp"], 1)
                for half in range(2) if i < 4 else ():
                    ps = taken(eng, f"Y{i}.{half}")
                    copied(tt(x1[0:r, i, 512 * half:512 * half + 512], x1[0:r, i, 512 * half:512 * half + 512], ps[0:r, :], ALU.add), f"Y{i}.{half}")
                eng.wait_ge(S["x1_ss"], n + 1)
                ts(sumsq[0:r, i:i + 1], sumsq[0:r, i:i + 1], 1.0 / D, EPS, ALU.mult, ALU.add).then_inc(S["x1_asked"], 1)
                second_norm(n)

            eng.memset(logits, 0.0)
            eng.memset(lg8, NEG)
            link(eng.memset(cnt, 0.0))
            eng.wait_ge(S["rtw_loaded"], 16 * 4)
            ps = taken(eng, "L")
            tile_logits = ps[:, 0:144].rearrange("p (t e) -> p t e", t=4)
            tt(lg8[:, 0:4, 0:4], tile_logits[:, :, 0:4], rt_b[:, 0:4].unsqueeze(1).to_broadcast([128, 4, 4]), ALU.add)
            tt(lg8[0:NS, 4, 0:4], ps[0:NS, 144:148], rt_b[0:NS, 0:4], ALU.add)
            tt(logits[:, 0:4, 4:36], tile_logits[:, :, 4:36], rt_b[:, 4:36].unsqueeze(1).to_broadcast([128, 4, 32]), ALU.add)
            copied(tt(logits[0:NS, 4, 4:36], ps[0:NS, 148:180], rt_b[0:NS, 4:36], ALU.add), "L")
            drained(eng, "L")
            for t in range(NTILE):
                ins = eng.max(mx8[:, t, :], lg8[:, t, :])
            link(ins)
            for t in range(NTILE):
                ins = eng.max_index(mi8[:, t, :].bitcast(U32), mx8[:, t, :], lg8[:, t, :])
            link(ins)
            tt(lex, lg8[:, :, 0:4], mx8[:, :, 0:1].to_broadcast([128, 5, 4]), ALU.subtract).then_inc(S["rt_d"], 1)
            link(eng.tensor_copy(gsel, mi8[:, :, 0].bitcast(U32)))
            link(tt(eqg, grp_iota.unsqueeze(1).to_broadcast([128, 5, N_EXP]), gsel.unsqueeze(2).to_broadcast([128, 5, N_EXP]), ALU.is_equal))
            ts(eqt, eqg, -NEG, NEG, ALU.mult, ALU.add)
            link(tt(eqg, eqg, logits[:, :, 4:36], ALU.mult))
            link(tt(eqg, eqg, eqt, ALU.add))
            for t in range(NTILE):
                ins = eng.max(tv8[:, t, :], eqg[:, t, :])
            link(ins)
            for t in range(NTILE):
                ins = eng.max_index(ti8[:, t, :].bitcast(U32), tv8[:, t, :], eqg[:, t, :])
            link(ins)
            tt(tdx, tv8[:, :, 1], tv8[:, :, 0], ALU.subtract).then_inc(S["rt_d"], 1)
            link(eng.tensor_copy(tif, ti8[:, :, 0:2].bitcast(U32).rearrange("p t k -> p k t")))
            eng.memset(pass_no, 0.0)
            for k in range(2):
                ins = tt(oh[:, k], exp_iota.unsqueeze(1).to_broadcast([128, 5, N_EXP]), tif[:, k, :].unsqueeze(2).to_broadcast([128, 5, N_EXP]), ALU.is_equal)
            link(ins)
            for k in range(2):
                ins = tt(oh[:, k], oh[:, k], valid.unsqueeze(2).to_broadcast([128, 5, N_EXP]), ALU.mult)
            link(ins)
            link(tt(mask, oh[:, 0], oh[:, 1], ALU.add))
            eng.tensor_copy(mask_bf[:, :, :], mask).then_inc(S["mask_made"], 1)
            ps = taken(eng, "pos")
            copied(eng.tensor_copy(pos, ps[:, 0:160].rearrange("p (t e) -> p t e", t=5)), "pos")
            drained(eng, "pos")
            link(stt(posm[:, :, 0:N_EXP], pos, 1.0, mask, ALU.add, ALU.mult))
            link(ts(posm[:, :, 0:N_EXP], posm[:, :, 0:N_EXP], -1.0, None, ALU.add))

            def make_onehot(n, b):
                tt(onehot[b], cap_iota.unsqueeze(1).to_broadcast([128, 5, CAP]), posm[:, :, bass.ds(n, 1)].to_broadcast([128, 5, CAP]), ALU.is_equal).then_inc(S["onehot_made"], 1)

            make_onehot(0, 0)
            make_onehot(1, 1)
            for r in range(1, ROUNDS):
                ts(posm[:, :, N_EXP * r:N_EXP * r + N_EXP], posm[:, :, 0:N_EXP], float(-CAP * r), None, ALU.add)
            link(eng.memset(posm[:, :, ROUNDS * N_EXP:n_cols], -1.0))
            ps = taken(eng, "cnt")
            copied(eng.tensor_reduce(cnt[:, 0:1], ps[:, 0:32], X_AXIS, ALU.max), "cnt")
            drained(eng, "cnt")
            link(ts(flr[:, 0, :], thr, cnt[:, 0:1], None, ALU.is_lt))
            link(eng.tensor_reduce(cnt[:, 1:2], flr[:, 0, :], X_AXIS, ALU.add))
            link(ts(cnt[:, 1:2], cnt[:, 1:2], 1.0, None, ALU.add))
            eng.tensor_copy(n_rounds[:, :], cnt[:, 1:2]).then_inc(S["rounds_made"], 1)
            eng.wait_ge(S["rounds_made"], 1)
            eng.wait_ge(S["rt_exp"], 2)
            link(eng.tensor_reduce(psel, lex, X_AXIS, ALU.add))
            link(ts(gate[:, 0, :], tdx, 1.0, None, ALU.add))
            link(tt(gate[:, 0, :], gate[:, 0, :], psel, ALU.mult))
            link(eng.reciprocal(gate[:, 0, :], gate[:, 0, :]))
            link(tt(gate[:, 1, :], gate[:, 0, :], tdx, ALU.mult))
            link(tt(ohp, oh, pos.unsqueeze(1).to_broadcast([128, 2, 5, N_EXP]), ALU.mult))
            link(eng.tensor_reduce(pk, ohp, X_AXIS, ALU.add))
            pk10 = pk.rearrange("p k t -> p (k t)")
            link(tt(flr, pk10.unsqueeze(2).to_broadcast([128, 10, 8]), thr.unsqueeze(1).to_broadcast([128, 10, 8]), ALU.is_ge))
            link(eng.tensor_reduce(flk, flr, X_AXIS, ALU.add))
            link(stt(slot_f.rearrange("p k t -> p (k t)"), flk, float(-CAP), pk10, ALU.mult, ALU.add))
            link(stt(slot_f, tif, float(CAP), slot_f, ALU.mult, ALU.add))
            eng.tensor_copy(slot_u[:, :], slot_f.rearrange("p k t -> p (k t)")).then_inc(S["slots_made"], 1)

            rounds = eng.value_load(n_rounds[0:1, 0:1], min_val=1, max_val=ROUNDS)
            eng.sem_inc(S["y_tile_done"], NTILE)
            eng.sem_inc(S["round_combined"], 1)

            def copy_xe(b):
                eng.tensor_copy(xe[b], bank[1][:, :].rearrange("p (j s n) -> p j s n", j=4, s=2)).then_inc(S["xe_made"], 1)

            eng.wait_ge(S["xe_turned"], 1)
            copy_xe(0)
            with eng.Fori(0, rounds) as r:
                with eng.Fori(0, N_EXP // 2) as i:
                    for b in range(2):
                        n = N_EXP * r + 2 * i + b
                        eng.wait_ge(S["silu_done"], n + 1)
                        tt(hid[b], silu[b], bank[2 + b][:, 256:512], ALU.mult).then_inc(S["hid_made"], 1)
                        eng.wait_ge(S["gathered"], n + 1)
                        make_onehot(n + 2, b)
                        eng.wait_ge(S["xt_turned"], n + 1)
                        eng.tensor_copy(hT[b], bank[4 + b][:, 0:256].rearrange("p (k s) -> p k s", k=2)).then_inc(S["hT_made"], 1)
                        eng.wait_ge(S["xe_turned"], n + 2)
                        copy_xe(1 - b)
                ts(gate_r.rearrange("p k t -> p (k t)"), flk, pass_no, None, ALU.is_equal)
                eng.tensor_copy(pass_next, pass_no).then_inc(S["pass_counted"], 1)
                eng.wait_ge(S["pass_counted"], 3 * r + 1)
                tt(gate_r, gate_r, gate, ALU.mult)
                ts(pass_no, pass_next, 1.0, None, ALU.add).then_inc(S["pass_counted"], 1)
                eng.wait_ge(S["pass_counted"], 3 * r + 2)
                for n, t in enumerate(COMBINE_TILES):
                    q = ROWS[t]
                    for k in range(2):
                        eng.wait_ge(rows_gathered[k][t], 16 * r + 16)
                        stt(x1[0:q, t, :], reg_a.t[0:q, (2 * t + k) * D:(2 * t + k + 1) * D], gate_r[0:q, k, t:t + 1], x1[0:q, t, :], ALU.mult, ALU.add).then_inc(S["half_added" if k == 0 else "y_tile_done"], 1)
                        if k == 0:
                            eng.wait_ge(S["half_added"], NTILE * r + n + 1)
                eng.wait_ge(S["y_tile_done"], NTILE * r + 2 * NTILE)
                eng.sem_inc(S["pass_counted"], 1)
                eng.sem_inc(S["round_combined"], 1)


_INS = ['x_prompt', 'x_sample', 'cache_nsa', 'state_win_kv', 'state_pool', 'state_rg_conv', 'state_rg_h', 'state_sc_conv',
        'page_table', 'norm_mix_g', 'w_in', 'pool_w', 'pool_scale', 'rg_conv_w', 'rg_conv_b', 'rg_w_a', 'rg_b_a', 'rg_w_x',
        'rg_b_x', 'rg_lambda', 'nsa_phi', 'nsa_phi_b', 'nsa_qk_g', 'sc_conv_w', 'sc_conv_b', 'mix_out_g', 'w_out',
        'norm_ffn_g', 'router_group_w', 'router_group_b', 'router_expert_w', 'router_expert_b', 'exp_w_gu', 'exp_w_down']
_OUTS = [('y_p', (1, SEQ, D)), ('y_s', (NS, 1, D)), ('rows_p', (1, 1, SEQ, 4, 2, HD)), ('rows_s', (1, NS, 1, 4, 2, HD)),
         ('win_p', (1, 1, SEQ, 2, 2, HD)), ('win_s', (1, NS, PAST, 2, 2, HD)), ('pool_p', (1, 1, POOL_KEEP, GW)),
         ('pool_s', (1, NS, POOL_KEEP, GW)), ('rgc_p', (1, 1, RG_KEEP, GW)), ('rgc_s', (1, NS, RG_KEEP, GW)),
         ('rgh_p', (1, 1, GW)), ('rgh_s', (1, NS, GW)), ('scc_p', (1, 1, SC_KEEP, GW)), ('scc_s', (1, NS, SC_KEEP, GW))]


def kernel(**inputs):
    import numpy as _np
    import concourse.bacc as _bacc
    from concourse.bass_utils import run_bass_kernel_spmd as _run

    nc = _bacc.Bacc("TRN2", target_bir_lowering=False, num_devices=1)
    arrays, ins, outs = {}, {}, {}
    for name in _INS:
        arr = _np.ascontiguousarray(inputs[name])
        arrays[f"in_{name}"] = arr
        ins[name] = nc.dram_tensor(f"in_{name}", arr.shape, mybir.dt.from_np(arr.dtype), kind="ExternalInput").ap()
    for name, shape in _OUTS:
        outs[name] = nc.dram_tensor(f"out_{name}", shape, F32, kind="ExternalOutput").ap()
    layer_kernel(nc, ins, outs)
    r = _run(nc, [arrays], core_ids=[0])
    return tuple(r.results[0][f"out_{name}"] for name, _ in _OUTS)
```
